# Optimizing a Trainium2 kernel written in Bass

```python
import math
import jax
import jax.numpy as jnp
from jax import lax
import numpy as np
import jax, jax.numpy as jnp

D_MODEL = 1024
BATCH = 1
SEQ = 1024
DEPTH = 1

CHUNK = 64
Q_BLOCK = 128
EPS = 1e-6
N_BRANCHES = 4
BRANCH_WIDTH = D_MODEL // 4
HEADS = 4
HEAD_DIM = BRANCH_WIDTH // HEADS
D_FF = 4 * D_MODEL

DN_DK = HEAD_DIM
DN_DV = HEAD_DIM
CONV_K = 4
MLA_NOPE = HEAD_DIM
MLA_ROPE = HEAD_DIM // 2
MLA_V = HEAD_DIM
MLA_Q_LORA = D_MODEL // 4
MLA_KV_LORA = D_MODEL // 8
ROPE_THETA = 10000.0
GLA_DK = HEAD_DIM // 2
GLA_DV = HEAD_DIM
GLA_RANK = 16
GLA_TAU = 16.0
FOX_DH = HEAD_DIM

IN_SIZES = (
    HEADS * (2 * DN_DK + DN_DV), HEADS * DN_DV, HEADS, HEADS,
    MLA_Q_LORA, MLA_KV_LORA, MLA_ROPE,
    HEADS * GLA_DK, HEADS * GLA_DK, HEADS * GLA_DV, HEADS * GLA_DV, GLA_RANK,
    HEADS * FOX_DH, HEADS * FOX_DH, HEADS * FOX_DH, HEADS,
)
IN_WIDTH = sum(IN_SIZES)


def rms_norm(x, gain):
    xf = x.astype(jnp.float32)
    y = xf * lax.rsqrt(jnp.mean(xf * xf, axis=-1, keepdims=True) + EPS)
    return (y * gain.astype(jnp.float32)).astype(x.dtype)

def l2_normalize(x):
    xf = x.astype(jnp.float32)
    return (xf * lax.rsqrt(jnp.sum(xf * xf, axis=-1, keepdims=True) + EPS)).astype(x.dtype)

def causal_depthwise_conv(x, w):
    k = w.shape[0]
    return lax.conv_general_dilated(
        x, w[:, None, :].astype(x.dtype), window_strides=(1,), padding=((k - 1, 0),),
        dimension_numbers=('NWC', 'WIO', 'NWC'), feature_group_count=x.shape[-1])

def to_chunks(t):
    b, s, h, d = t.shape
    return t.reshape(b, s // CHUNK, CHUNK, h, d).transpose(0, 3, 1, 2, 4)

def from_chunks(t):
    b, h, n, c, d = t.shape
    return t.transpose(0, 2, 3, 1, 4).reshape(b, n * c, h, d)

def scalar_chunks(t):
    b, s, h = t.shape
    return t.reshape(b, s // CHUNK, CHUNK, h).transpose(0, 3, 1, 2)

def gated_delta_rule(q, k, v, g, beta):
    out_dtype = v.dtype
    f32 = jnp.float32
    b_sz, s_len, n_h, dk = q.shape
    dv = v.shape[-1]
    qc = to_chunks(q.astype(f32)) * (dk ** -0.5)
    kc = to_chunks(k.astype(f32))
    vc = to_chunks(v.astype(f32))
    gc = jnp.cumsum(scalar_chunks(g.astype(f32)), axis=-1)
    bc = scalar_chunks(beta.astype(f32))
    lower = jnp.tril(jnp.ones((CHUNK, CHUNK), dtype=bool))
    strict = jnp.tril(jnp.ones((CHUNK, CHUNK), dtype=bool), -1)
    diff = gc[..., :, None] - gc[..., None, :]
    decay_ts = jnp.where(lower, jnp.exp(jnp.where(lower, diff, 0.0)), 0.0)
    kk = jnp.einsum('bhncd,bhnsd->bhncs', kc, kc)
    a_strict = jnp.where(strict, bc[..., None] * kk * decay_ts, 0.0)
    eye = jnp.eye(CHUNK, dtype=f32)
    rhs = jnp.concatenate([vc * bc[..., None], kc * (bc * jnp.exp(gc))[..., None]], axis=-1)
    sol = lax.linalg.triangular_solve(a_strict + eye, rhs, left_side=True, lower=True,
                                      unit_diagonal=True)
    u = sol[..., :dv]
    w = sol[..., dv:]
    qk = jnp.einsum('bhncd,bhnsd->bhncs', qc, kc) * decay_ts
    q_decay = qc * jnp.exp(gc)[..., None]
    k_tail = kc * jnp.exp(gc[..., -1:] - gc)[..., None]
    chunk_decay = jnp.exp(gc[..., -1])

    def step(state, inp):
        u_c, w_c, qk_c, qd_c, kt_c, cd_c = inp
        v_new = u_c - jnp.einsum('bhck,bhkv->bhcv', w_c, state)
        o_c = (jnp.einsum('bhck,bhkv->bhcv', qd_c, state)
               + jnp.einsum('bhcs,bhsv->bhcv', qk_c, v_new))
        state = state * cd_c[..., None, None] + jnp.einsum('bhck,bhcv->bhkv', kt_c, v_new)
        return state, o_c

    xs = tuple(jnp.moveaxis(t, 2, 0) for t in (u, w, qk, q_decay, k_tail, chunk_decay))
    s0 = jnp.zeros((b_sz, n_h, dk, dv), f32)
    _, o = lax.scan(step, s0, xs)
    return from_chunks(jnp.moveaxis(o, 0, 2)).astype(out_dtype)

def gla_chunked(q, k, v, log_a):
    out_dtype = v.dtype
    f32 = jnp.float32
    b_sz, s_len, n_h, dk = q.shape
    dv = v.shape[-1]
    qc = to_chunks(q.astype(f32)) * (dk ** -0.5)
    kc = to_chunks(k.astype(f32))
    vc = to_chunks(v.astype(f32))
    bcum = jnp.cumsum(to_chunks(log_a.astype(f32)), axis=3)
    q_in = qc * jnp.exp(bcum)
    k_in = kc * jnp.exp(-bcum)
    lower = jnp.tril(jnp.ones((CHUNK, CHUNK), dtype=bool))
    attn = jnp.where(lower, jnp.einsum('bhncd,bhnsd->bhncs', q_in, k_in), 0.0)
    o_intra = jnp.einsum('bhncs,bhnsv->bhncv', attn, vc)
    b_last = bcum[..., -1:, :]
    k_tail = kc * jnp.exp(b_last - bcum)
    chunk_decay = jnp.exp(b_last[..., 0, :])

    def step(state, inp):
        qi_c, kt_c, v_c, cd_c = inp
        o_c = jnp.einsum('bhck,bhkv->bhcv', qi_c, state)
        state = state * cd_c[..., None] + jnp.einsum('bhck,bhcv->bhkv', kt_c, v_c)
        return state, o_c

    xs = tuple(jnp.moveaxis(t, 2, 0) for t in (q_in, k_tail, vc, chunk_decay))
    s0 = jnp.zeros((b_sz, n_h, dk, dv), f32)
    _, o_inter = lax.scan(step, s0, xs)
    o = o_intra + jnp.moveaxis(o_inter, 0, 2)
    return from_chunks(o).astype(out_dtype)

def rope_cos_sin(seq, dim):
    inv_freq = 1.0 / (ROPE_THETA ** (jnp.arange(0, dim, 2, dtype=jnp.float32) / dim))
    ang = jnp.arange(seq, dtype=jnp.float32)[:, None] * inv_freq[None, :]
    ang = jnp.concatenate([ang, ang], axis=-1)
    return jnp.cos(ang), jnp.sin(ang)

def apply_rope(x, cos, sin):
    xf = x.astype(jnp.float32)
    x1, x2 = jnp.split(xf, 2, axis=-1)
    rot = jnp.concatenate([-x2, x1], axis=-1)
    return (xf * cos[None, :, None, :] + rot * sin[None, :, None, :]).astype(x.dtype)

def block_sweep_attention(q, k, v, scale, forget_cum):
    s_len = q.shape[1]
    outs = []
    for start in range(0, s_len, Q_BLOCK):
        end = start + Q_BLOCK
        logits = jnp.einsum('bqhd,bkhd->bhqk', q[:, start:end], k[:, :end],
                            preferred_element_type=jnp.float32) * scale
        q_pos = jnp.arange(start, end)
        k_pos = jnp.arange(end)
        if forget_cum is None:
            allowed = (k_pos[None, :] // CHUNK) <= (q_pos[:, None] // CHUNK)
        else:
            allowed = k_pos[None, :] <= q_pos[:, None]
            f_q = forget_cum[:, start:end].transpose(0, 2, 1)
            f_k = forget_cum[:, :end].transpose(0, 2, 1)
            logits = logits + (f_q[..., :, None] - f_k[..., None, :])
        logits = jnp.where(allowed, logits, -jnp.inf)
        p = jax.nn.softmax(logits, axis=-1)
        outs.append(jnp.einsum('bhqk,bkhd->bqhd', p.astype(v.dtype), v[:, :end]))
    return jnp.concatenate(outs, axis=1)

def hybrid_layer(x, norm_mix_pre, norm_mix_post, norm_mlp_pre, norm_mlp_post, w_in,
                 dn_conv, dn_a_log, dn_dt_bias, dn_norm,
                 mla_q_norm, mla_w_q_up, mla_kv_norm, mla_w_kv_up,
                 gla_w_gate_up, gla_gate_bias, gla_norm, fox_f_bias,
                 w_branch_up, w_gate, b_gate, w_out, w_mlp_in, w_mlp_out):
    f32 = jnp.float32
    b_sz, s_len, _ = x.shape
    h = rms_norm(x, norm_mix_pre)
    proj = h @ w_in
    split_at = np.cumsum(IN_SIZES)[:-1].tolist()
    (dn_qkv, dn_z, dn_b, dn_a, mla_cq, mla_ckv, mla_kpe,
     gla_q, gla_k, gla_v, gla_g, gla_lr,
     fox_q, fox_k, fox_v, fox_f) = jnp.split(proj, split_at, axis=-1)

    qkv = jax.nn.silu(causal_depthwise_conv(dn_qkv, dn_conv))
    a_q, a_k, a_v = jnp.split(qkv, [HEADS * DN_DK, 2 * HEADS * DN_DK], axis=-1)
    a_q = l2_normalize(a_q.reshape(b_sz, s_len, HEADS, DN_DK))
    a_k = l2_normalize(a_k.reshape(b_sz, s_len, HEADS, DN_DK))
    a_v = a_v.reshape(b_sz, s_len, HEADS, DN_DV)
    beta = jax.nn.sigmoid(dn_b.astype(f32))
    g = -jnp.exp(dn_a_log.astype(f32)) * jax.nn.softplus(dn_a.astype(f32) + dn_dt_bias.astype(f32))
    o_a = gated_delta_rule(a_q, a_k, a_v, g, beta)
    o_a = (rms_norm(o_a, dn_norm) * jax.nn.silu(dn_z.reshape(b_sz, s_len, HEADS, DN_DV))
           ).reshape(b_sz, s_len, BRANCH_WIDTH)

    cq = rms_norm(mla_cq, mla_q_norm)
    b_q = (cq @ mla_w_q_up).reshape(b_sz, s_len, HEADS, MLA_NOPE + MLA_ROPE)
    q_nope, q_pe = jnp.split(b_q, [MLA_NOPE], axis=-1)
    ckv = rms_norm(mla_ckv, mla_kv_norm)
    b_kv = (ckv @ mla_w_kv_up).reshape(b_sz, s_len, HEADS, MLA_NOPE + MLA_V)
    k_nope, b_v = jnp.split(b_kv, [MLA_NOPE], axis=-1)
    cos, sin = rope_cos_sin(s_len, MLA_ROPE)
    q_pe = apply_rope(q_pe, cos, sin)
    k_pe = apply_rope(mla_kpe[:, :, None, :], cos, sin)
    b_qf = jnp.concatenate([q_nope, q_pe], axis=-1)
    b_kf = jnp.concatenate([k_nope, jnp.broadcast_to(k_pe, (b_sz, s_len, HEADS, MLA_ROPE))], axis=-1)
    o_b = block_sweep_attention(b_qf, b_kf, b_v, (MLA_NOPE + MLA_ROPE) ** -0.5, None)
    o_b = o_b.reshape(b_sz, s_len, BRANCH_WIDTH)

    log_a = jax.nn.log_sigmoid((gla_lr @ gla_w_gate_up + gla_gate_bias).astype(f32)) / GLA_TAU
    o_c = gla_chunked(gla_q.reshape(b_sz, s_len, HEADS, GLA_DK),
                      gla_k.reshape(b_sz, s_len, HEADS, GLA_DK),
                      gla_v.reshape(b_sz, s_len, HEADS, GLA_DV),
                      log_a.reshape(b_sz, s_len, HEADS, GLA_DK))
    o_c = (rms_norm(o_c, gla_norm) * jax.nn.silu(gla_g.reshape(b_sz, s_len, HEADS, GLA_DV))
           ).reshape(b_sz, s_len, BRANCH_WIDTH)

    log_f = jax.nn.log_sigmoid((fox_f + fox_f_bias).astype(f32))
    forget_cum = jnp.cumsum(log_f, axis=1)
    o_d = block_sweep_attention(fox_q.reshape(b_sz, s_len, HEADS, FOX_DH),
                                fox_k.reshape(b_sz, s_len, HEADS, FOX_DH),
                                fox_v.reshape(b_sz, s_len, HEADS, FOX_DH),
                                FOX_DH ** -0.5, forget_cum)
    o_d = o_d.reshape(b_sz, s_len, BRANCH_WIDTH)

    branches = (o_a, o_b, o_c, o_d)
    merged = jnp.zeros_like(x)
    for i in range(N_BRANCHES):
        gate = jax.nn.sigmoid(h @ w_gate[i] + b_gate[i])
        merged = merged + gate * (branches[i] @ w_branch_up[i])
    x = x + rms_norm(merged @ w_out, norm_mix_post)

    h2 = rms_norm(x, norm_mlp_pre)
    u = jax.nn.relu(h2 @ w_mlp_in)
    x = x + rms_norm((u * u) @ w_mlp_out, norm_mlp_post)
    return x

def first_inputs(seed: int = 0) -> dict:
    key = jax.random.key(seed)
    ks = jax.random.split(key, 24)
    L, D, f32 = DEPTH, D_MODEL, jnp.float32

    def nrm(i, shape, scale):
        return jax.random.normal(ks[i], shape, f32) * scale

    def gain(i, shape):
        return 1.0 + 0.1 * jax.random.normal(ks[i], shape, f32)

    conv_width = HEADS * (2 * DN_DK + DN_DV)
    dt = jnp.exp(jax.random.uniform(ks[7], (L, HEADS), f32, math.log(1e-3), math.log(1e-1)))
    return {
        'x': nrm(0, (BATCH, SEQ, D), 1.0),
        'norm_mix_pre': gain(1, (L, D)),
        'norm_mix_post': gain(2, (L, D)),
        'norm_mlp_pre': gain(3, (L, D)),
        'norm_mlp_post': gain(4, (L, D)),
        'w_in': nrm(5, (L, D, IN_WIDTH), D ** -0.5),
        'dn_conv': nrm(8, (L, CONV_K, conv_width), CONV_K ** -0.5),
        'dn_a_log': jnp.log(jax.random.uniform(ks[6], (L, HEADS), f32, 1.0, 16.0)),
        'dn_dt_bias': dt + jnp.log(-jnp.expm1(-dt)),
        'dn_norm': gain(9, (L, DN_DV)),
        'mla_q_norm': gain(10, (L, MLA_Q_LORA)),
        'mla_w_q_up': nrm(11, (L, MLA_Q_LORA, HEADS * (MLA_NOPE + MLA_ROPE)), MLA_Q_LORA ** -0.5),
        'mla_kv_norm': gain(12, (L, MLA_KV_LORA)),
        'mla_w_kv_up': nrm(13, (L, MLA_KV_LORA, HEADS * (MLA_NOPE + MLA_V)), MLA_KV_LORA ** -0.5),
        'gla_w_gate_up': nrm(14, (L, GLA_RANK, HEADS * GLA_DK), GLA_RANK ** -0.5),
        'gla_gate_bias': nrm(15, (L, HEADS * GLA_DK), 0.1),
        'gla_norm': gain(16, (L, GLA_DV)),
        'fox_f_bias': jax.random.uniform(ks[17], (L, HEADS), f32, 1.0, 3.0),
        'w_branch_up': nrm(18, (L, N_BRANCHES, BRANCH_WIDTH, D), BRANCH_WIDTH ** -0.5),
        'w_gate': nrm(19, (L, N_BRANCHES, D, D), D ** -0.5),
        'b_gate': nrm(20, (L, N_BRANCHES, D), 0.1),
        'w_out': nrm(21, (L, D, D), D ** -0.5),
        'w_mlp_in': nrm(22, (L, D, D_FF), D ** -0.5),
        'w_mlp_out': nrm(23, (L, D_FF, D), D_FF ** -0.5),
    }

def first_block(x, norm_mix_pre, norm_mix_post, norm_mlp_pre, norm_mlp_post, w_in,
              dn_conv, dn_a_log, dn_dt_bias, dn_norm,
              mla_q_norm, mla_w_q_up, mla_kv_norm, mla_w_kv_up,
              gla_w_gate_up, gla_gate_bias, gla_norm, fox_f_bias,
              w_branch_up, w_gate, b_gate, w_out, w_mlp_in, w_mlp_out):
    for l in range(DEPTH):
        x = hybrid_layer(x, norm_mix_pre[l], norm_mix_post[l], norm_mlp_pre[l], norm_mlp_post[l],
                         w_in[l], dn_conv[l], dn_a_log[l], dn_dt_bias[l], dn_norm[l],
                         mla_q_norm[l], mla_w_q_up[l], mla_kv_norm[l], mla_w_kv_up[l],
                         gla_w_gate_up[l], gla_gate_bias[l], gla_norm[l], fox_f_bias[l],
                         w_branch_up[l], w_gate[l], b_gate[l], w_out[l], w_mlp_in[l], w_mlp_out[l])
    return x


CTX_LEN = 256
GRID_W = 64
N_MIXERS = 4
BRANCH_W = D_MODEL // 2
MIX_W = N_MIXERS * BRANCH_W
HEAD_DIM_2 = 64
N_HEADS_A = BRANCH_W // HEAD_DIM_2
A_CONV = 4
RG_C = 8.0
B_CONV = 3
C_CONV = 31
POOL_WINDOWS = (2, 4, 8, 16)
POOL_GROUP = BRANCH_W // len(POOL_WINDOWS)
N_IN_SLOTS = 11
IN_W = N_IN_SLOTS * BRANCH_W
RMS_EPS = 1e-6
LN_EPS = 1e-5


def rms_norm_2(x, g):
    xf = x.astype(jnp.float32)
    y = xf * lax.rsqrt(jnp.mean(xf * xf, axis=-1, keepdims=True) + RMS_EPS)
    return (y * g.astype(jnp.float32)).astype(x.dtype)

def layer_norm(x, g, b):
    xf = x.astype(jnp.float32)
    mu = jnp.mean(xf, axis=-1, keepdims=True)
    xc = xf - mu
    var = jnp.mean(xc * xc, axis=-1, keepdims=True)
    y = xc * lax.rsqrt(var + LN_EPS) * g.astype(jnp.float32) + b.astype(jnp.float32)
    return y.astype(x.dtype)

def depthwise_conv(x, w, pad_left, pad_right):
    k = w[:, None, :].astype(x.dtype)
    return lax.conv_general_dilated(
        x, k, window_strides=(1,), padding=[(pad_left, pad_right)],
        dimension_numbers=('NWC', 'WIO', 'NWC'), feature_group_count=x.shape[-1])

def _rev_bwd(z):
    return jnp.stack([z[0], jnp.flip(z[1], axis=1)])

def rglru(v, lp, h0):
    bsz, t, _ = v.shape
    xc = jnp.stack([depthwise_conv(v, lp['a_conv'][0], A_CONV - 1, 0),
                    depthwise_conv(v, lp['a_conv'][1], 0, A_CONV - 1)])
    xh = xc.reshape(2, bsz, t, N_HEADS_A, HEAD_DIM_2)
    r = jax.nn.sigmoid(jnp.einsum('nbthi,nhij->nbthj', xh, lp['a_wr']).reshape(2, bsz, t, BRANCH_W)
                       + lp['a_br'][:, None, None, :])
    ig = jax.nn.sigmoid(jnp.einsum('nbthi,nhij->nbthj', xh, lp['a_wi']).reshape(2, bsz, t, BRANCH_W)
                        + lp['a_bi'][:, None, None, :])
    log_a = -RG_C * r.astype(jnp.float32) * jax.nn.softplus(-lp['a_lam'].astype(jnp.float32))[:, None, None, :]
    a = jnp.exp(log_a)
    b = jnp.sqrt(-jnp.expm1(2.0 * log_a)) * (ig * xc).astype(jnp.float32)
    a = _rev_bwd(a)
    b = _rev_bwd(b)

    def step(h, ab):
        at, bt = ab
        h = at * h + bt
        return h, h

    h_final, ys = lax.scan(step, h0, (jnp.moveaxis(a, 2, 0), jnp.moveaxis(b, 2, 0)))
    ys = _rev_bwd(jnp.moveaxis(ys, 0, 2))
    return (ys[0] + ys[1]).astype(v.dtype), h_final

def pool_grid(u):
    bsz, s, ch = u.shape
    rows = s // GRID_W
    g = u.reshape(bsz, rows, GRID_W, ch).astype(jnp.float32)
    P = jnp.pad(jnp.cumsum(jnp.cumsum(g, axis=1), axis=2), ((0, 0), (1, 0), (1, 0), (0, 0)))
    r = jnp.arange(rows)
    cidx = jnp.arange(GRID_W)
    outs = []
    for gi, w in enumerate(POOL_WINDOWS):
        Pg = P[..., gi * POOL_GROUP:(gi + 1) * POOL_GROUP]
        r0 = jnp.clip(r - w // 2, 0, rows)
        r1 = jnp.clip(r + w // 2, 0, rows)
        c0 = jnp.clip(cidx - w // 2, 0, GRID_W)
        c1 = jnp.clip(cidx + w // 2, 0, GRID_W)
        Pr1 = Pg[:, r1]
        Pr0 = Pg[:, r0]
        total = Pr1[:, :, c1] - Pr1[:, :, c0] - Pr0[:, :, c1] + Pr0[:, :, c0]
        cnt = ((r1 - r0)[:, None] * (c1 - c0)[None, :]).astype(jnp.float32)
        outs.append(total / cnt[None, :, :, None])
    mean = jnp.concatenate(outs, axis=-1).reshape(bsz, s, ch)
    return mean.astype(u.dtype) - u

def pool_seq(u):
    bsz, t, ch = u.shape
    P = jnp.pad(jnp.cumsum(u.astype(jnp.float32), axis=1), ((0, 0), (1, 0), (0, 0)))
    pos = jnp.arange(t)
    outs = []
    for gi, w in enumerate(POOL_WINDOWS):
        Pg = P[..., gi * POOL_GROUP:(gi + 1) * POOL_GROUP]
        lo = jnp.clip(pos - w // 2, 0, t)
        hi = jnp.clip(pos + w // 2, 0, t)
        outs.append((Pg[:, hi] - Pg[:, lo]) / (hi - lo).astype(jnp.float32)[None, :, None])
    mean = jnp.concatenate(outs, axis=-1)
    return mean.astype(u.dtype) - u

def mix(h, lp, h0, pool_fn):
    proj = jnp.einsum('btd,de->bte', h, lp['w_in'])
    (va, za, bb, bc, bv, zb, ca, cg, zc, dv, zd) = jnp.split(proj, N_IN_SLOTS, axis=-1)
    ya, h_final = rglru(va, lp, h0)
    yb = bb * depthwise_conv(bc * bv, lp['b_conv'], B_CONV // 2, B_CONV // 2)
    u = ca * jax.nn.sigmoid(cg)
    u = depthwise_conv(u, lp['c_conv'], C_CONV // 2, C_CONV // 2)
    u = layer_norm(u, lp['c_ln_g'], lp['c_ln_b'])
    yc = jnp.einsum('btc,ce->bte', jax.nn.silu(u), lp['c_pw']) + lp['c_pw_b']
    p = pool_fn(dv)
    bsz, t, _ = p.shape
    pg = p.reshape(bsz, t, len(POOL_WINDOWS), POOL_GROUP)
    yd = (jnp.einsum('btgi,gij->btgj', pg, lp['d_w']) + lp['d_b']).reshape(bsz, t, BRANCH_W) * lp['d_scale']
    cat = jnp.concatenate([ya * jax.nn.silu(za), yb * jax.nn.silu(zb),
                           yc * jax.nn.silu(zc), yd * jax.nn.silu(zd)], axis=-1)
    return jnp.einsum('bte,ed->btd', cat, lp['w_out']), h_final

def second_inputs(seed: int = 0) -> dict:
    key = jax.random.key(seed)
    ks = jax.random.split(key, 26)
    f32 = jnp.float32
    nrm = lambda k, shape, s: jax.random.normal(k, shape, f32) * s
    u = jax.random.uniform(ks[12], (DEPTH, 2, BRANCH_W), f32, minval=0.9, maxval=0.999)
    pa = u ** (1.0 / RG_C)
    a_lam = jnp.log(pa) - jnp.log1p(-pa)
    return {
        "x": nrm(ks[0], (BATCH, SEQ, D_MODEL), 1.0),
        "c": nrm(ks[1], (BATCH, D_MODEL), 1.0),
        "ctx": nrm(ks[2], (BATCH, CTX_LEN, D_MODEL), 1.0),
        "c_ctx": nrm(ks[3], (D_MODEL,), 1.0),
        "mod_w": nrm(ks[4], (DEPTH, D_MODEL, 3 * D_MODEL), 0.5 * D_MODEL ** -0.5),
        "mod_b": nrm(ks[5], (DEPTH, 3 * D_MODEL), 0.02),
        "norm_g": 1.0 + nrm(ks[6], (DEPTH, D_MODEL), 0.05),
        "w_in": nrm(ks[7], (DEPTH, D_MODEL, IN_W), D_MODEL ** -0.5),
        "w_out": nrm(ks[8], (DEPTH, MIX_W, D_MODEL), MIX_W ** -0.5),
        "a_conv": nrm(ks[9], (DEPTH, 2, A_CONV, BRANCH_W), A_CONV ** -0.5),
        "a_wr": nrm(ks[10], (DEPTH, 2, N_HEADS_A, HEAD_DIM_2, HEAD_DIM_2), HEAD_DIM_2 ** -0.5),
        "a_br": nrm(ks[11], (DEPTH, 2, BRANCH_W), 0.1),
        "a_wi": nrm(ks[13], (DEPTH, 2, N_HEADS_A, HEAD_DIM_2, HEAD_DIM_2), HEAD_DIM_2 ** -0.5),
        "a_bi": nrm(ks[14], (DEPTH, 2, BRANCH_W), 0.1),
        "a_lam": a_lam,
        "b_conv": nrm(ks[15], (DEPTH, B_CONV, BRANCH_W), B_CONV ** -0.5),
        "c_conv": nrm(ks[16], (DEPTH, C_CONV, BRANCH_W), C_CONV ** -0.5),
        "c_ln_g": 1.0 + nrm(ks[17], (DEPTH, BRANCH_W), 0.05),
        "c_ln_b": nrm(ks[18], (DEPTH, BRANCH_W), 0.02),
        "c_pw": nrm(ks[19], (DEPTH, BRANCH_W, BRANCH_W), BRANCH_W ** -0.5),
        "c_pw_b": nrm(ks[20], (DEPTH, BRANCH_W), 0.02),
        "d_w": nrm(ks[21], (DEPTH, len(POOL_WINDOWS), POOL_GROUP, POOL_GROUP), POOL_GROUP ** -0.5),
        "d_b": nrm(ks[22], (DEPTH, len(POOL_WINDOWS), POOL_GROUP), 0.02),
        "d_scale": 1.0 + nrm(ks[23], (DEPTH, BRANCH_W), 0.1),
        "final_g": 1.0 + nrm(ks[24], (D_MODEL,), 0.05),
    }

def second_block(x, c, ctx, c_ctx, mod_w, mod_b, norm_g, w_in, w_out, a_conv, a_wr, a_br, a_wi, a_bi,
              a_lam, b_conv, c_conv, c_ln_g, c_ln_b, c_pw, c_pw_b, d_w, d_b, d_scale, final_g):
    bsz = x.shape[0]
    for l in range(DEPTH):
        last = l == DEPTH - 1
        lp = dict(w_in=w_in[l], w_out=w_out[l], a_conv=a_conv[l], a_wr=a_wr[l], a_br=a_br[l],
                  a_wi=a_wi[l], a_bi=a_bi[l], a_lam=a_lam[l], b_conv=b_conv[l], c_conv=c_conv[l],
                  c_ln_g=c_ln_g[l], c_ln_b=c_ln_b[l], c_pw=c_pw[l], c_pw_b=c_pw_b[l],
                  d_w=d_w[l], d_b=d_b[l], d_scale=d_scale[l])
        mod = jax.nn.silu(c) @ mod_w[l] + mod_b[l]
        shift, scale, gate = jnp.split(mod[:, None, :], 3, axis=-1)
        mod_k = jax.nn.silu(c_ctx) @ mod_w[l] + mod_b[l]
        shift_k, scale_k, gate_k = jnp.split(mod_k, 3)
        hk = rms_norm_2(ctx, norm_g[l]) * (1.0 + scale_k) + shift_k
        h = rms_norm_2(x, norm_g[l]) * (1.0 + scale) + shift
        h0 = jnp.zeros((2, bsz, BRANCH_W), jnp.float32)
        if last:
            vk = jnp.einsum('btd,de->bte', hk, lp['w_in'][:, :BRANCH_W])
            _, state_k = rglru(vk, lp, h0)
        else:
            yk, state_k = mix(hk, lp, h0, pool_seq)
            ctx = ctx + gate_k * yk
        y, _ = mix(h, lp, state_k, pool_grid)
        x = x + gate * y
    return rms_norm_2(x, final_g)


def setup_inputs(seed=0):
    out = dict(first_inputs(seed))
    for name, value in second_inputs(seed + 1).items():
        if name != "x":
            out[name + "_2"] = value
    return out


def reference(
    x, norm_mix_pre, norm_mix_post, norm_mlp_pre, norm_mlp_post, w_in, dn_conv, dn_a_log,
    dn_dt_bias, dn_norm, mla_q_norm, mla_w_q_up, mla_kv_norm, mla_w_kv_up, gla_w_gate_up,
    gla_gate_bias, gla_norm, fox_f_bias, w_branch_up, w_gate, b_gate, w_out, w_mlp_in,
    w_mlp_out, c_2, ctx_2, c_ctx_2, mod_w_2, mod_b_2, norm_g_2, w_in_2, w_out_2, a_conv_2,
    a_wr_2, a_br_2, a_wi_2, a_bi_2, a_lam_2, b_conv_2, c_conv_2, c_ln_g_2, c_ln_b_2, c_pw_2,
    c_pw_b_2, d_w_2, d_b_2, d_scale_2, final_g_2,
):
    x = first_block(
        x, norm_mix_pre, norm_mix_post, norm_mlp_pre, norm_mlp_post, w_in, dn_conv, dn_a_log,
        dn_dt_bias, dn_norm, mla_q_norm, mla_w_q_up, mla_kv_norm, mla_w_kv_up, gla_w_gate_up,
        gla_gate_bias, gla_norm, fox_f_bias, w_branch_up, w_gate, b_gate, w_out, w_mlp_in,
        w_mlp_out,
    )
    return second_block(
        x, c_2, ctx_2, c_ctx_2, mod_w_2, mod_b_2, norm_g_2, w_in_2, w_out_2, a_conv_2, a_wr_2,
        a_br_2, a_wi_2, a_bi_2, a_lam_2, b_conv_2, c_conv_2, c_ln_g_2, c_ln_b_2, c_pw_2,
        c_pw_b_2, d_w_2, d_b_2, d_scale_2, final_g_2,
    )


_drawn_inputs = setup_inputs


def setup_inputs(seed=0):
    import zlib

    import numpy as np

    out = dict(_drawn_inputs(seed))
    spreads = {}
    factors = {'mla_q_norm': 5.526,
     'mla_kv_norm': 3.896,
     'ctx_2': 46.04,
     'mod_b_2': 3.359,
     'norm_g_2': 4.476,
     'a_br_2': 59.477,
     'a_bi_2': 42.465,
     'c_ln_g_2': 174.918,
     'c_ln_b_2': 200.0,
     'c_pw_b_2': 200.0,
     'd_b_2': 37.552,
     'd_scale_2': 8.0,
     'gla_gate_bias': 5.248,
     'c_ctx_2': 8.0}
    for name, (base, spread) in spreads.items():
        noise = np.random.default_rng([zlib.crc32(name.encode()), seed]).standard_normal(out[name].shape)
        drawn = base * np.exp(spread * noise) if base else spread * noise
        out[name] = jnp.asarray(drawn.astype(out[name].dtype))
    for name, factor in factors.items():
        out[name] = (out[name] * factor).astype(out[name].dtype)
    return out
```

```python
from contextlib import ExitStack

import numpy as np

import concourse.bass as bass
from concourse import mybir

F32 = mybir.dt.float32
F32R = mybir.dt.float32r
ALU = mybir.AluOpType
ACT = mybir.ActivationFunctionType
AX_X = mybir.AxisListType.X

P = 128
S = 1024
D = 1024
KT = D // P
HALF = 512
NH = S // HALF
BLK = S // P
HEADS, DH = 4, 64
CH = 64
GDK = 32
ROPE = 32
CTX = 256
EPS = 1e-6
LN_EPS = 1e-5
GRID_W = 64
WINDOWS = (2, 4, 8, 16)
WK = 10


class Steps:

    def __init__(self, c, engine, spec):
        self.c, self.engine, self.sem, self.base = c, engine, c.steps[engine], c.base[engine]
        self.at, self.count, self.order, n = {}, {}, [], 0
        for item in spec:
            what, k = item if isinstance(item, tuple) else (item, 1)
            turns = (what,) if isinstance(what, str) else what
            for m, name in enumerate(turns):
                assert name not in self.at, name
                self.at[name], self.count[name] = (n + m + 1, len(turns)), k
            self.order += list(turns) * k
            n += k * len(turns)
        self.n, self.next = n, 0

    def place(self, name, k=None):
        k = self.count[name] - 1 if k is None else k
        assert 0 <= k < self.count[name], (name, k)
        return self.at[name][0] + k * self.at[name][1]

    def value(self, name, k=None, i=0):
        return i * self.n + (self.base + self.place(name, k))

    def value_before(self, name, i, k=None):
        assert self.base >= self.n
        return i * self.n + (self.base - self.n + self.place(name, k))

    def step(self, name):
        assert self.order[self.next] == name, (self.engine, self.order[self.next], name)
        self.next = (self.next + 1) % self.n
        return self.sem

    def end(self, iterations=1):
        assert self.next == 0, (self.engine, self.order[self.next])
        self.c.base[self.engine] = self.base + iterations * self.n


class Core:

    def __init__(self, nc, ctx):
        self.nc, self.ctx, self.used = nc, ctx, {}
        self.steps = {e: self.sem(f"{e}_steps") for e in ("pe", "act", "vec", "pool", "dma")}
        self.base = {e: 0 for e in (*self.steps, "gemm_act", "gemm_dve")}
        self.loaded = [self.sem(f"weights_loaded_{s}") for s in range(2)]
        self.high_ready = self.sem("high_part_ready")
        self.low_ready = self.sem("low_part_ready")
        self.unit_done = self.sem("unit_multiplied")
        self.act_done = self.sem("unit_evacuated_by_act")
        self.dve_done = self.sem("unit_evacuated_by_dve")
        self.units = 0
        self.loads = [0, 0]
        self.ahead = None
        self.raw = self.sb("weights_raw", [P, 2, WK * P])
        self.parts = self.sb("weights_parts", [P, 2, 2, WK * P], F32R)
        self.psum = ctx.enter_context(nc.psum_tensor("psum", [P, 8, HALF], F32))
        self.scratch_stored = self.sem("scratch_stored")
        self.stored = 0
        self.slot_stored = [self.sem(f"slot_stored_{s}") for s in range(2)]
        self.slots = [0, 0]
        self.residual_loaded = [self.sem(f"residual_loaded_{n}") for n in range(2)]
        self.residuals = [0, 0]

    def sem(self, name):
        return self.ctx.enter_context(self.nc.semaphore(name))

    def sb(self, name, shape, dtype=F32, ctx=None, side="left"):
        self.used[name] = self.used.get(name, 0) + 1
        if self.used[name] > 1:
            name = f"{name}_{self.used[name]}"
        return (ctx or self.ctx).enter_context(self.nc.sbuf_tensor(name, shape, dtype,
                                                                    side=side))

    def banks(self, first, n=2):
        return self.psum[:, first:first + n, :].rearrange("p b n -> p (b n)")


def gemm(nc, c, weights, n_units, kt, rhs, act_per_unit=0, act_epilogue=None,
         dve_per_unit=0, dve_epilogue=None, banks_read_by="act", first=0, unroll=2,
         extra_kt=0, extra_rhs=None, halves=NH, cols=HALF, then=None, background=None):
    background = background or {}
    ready = c.ahead is not None
    assert not ready or c.ahead == (weights.tensor.name, first, kt + extra_kt), c.ahead
    c.ahead = None
    if then:
        assert n_units % 2 == 0
        c.ahead = (then[0].tensor.name, then[1], then[2])
    w = (kt + extra_kt) * P
    u0, l0 = c.units, list(c.loads)
    a0, d0 = c.base["gemm_act"], c.base["gemm_dve"]
    c.units += n_units
    c.loads = [l0[0] + (n_units + 1) // 2, l0[1] + n_units // 2]
    c.base["gemm_act"] += n_units * act_per_unit
    c.base["gemm_dve"] += n_units * dve_per_unit
    assert unroll % 2 == 0 and n_units >= 2

    def act_count(u, k=0):
        return u * act_per_unit + (a0 + k + 1)

    def dve_count(u, k=0):
        return u * dve_per_unit + (d0 + k + 1)

    def units(eng, body):
        whole = n_units // unroll
        for q in range(min(unroll, n_units)):
            body(q, q % 2, q // 2, q, q < 2, 0)
        if whole > 1:
            with eng.Fori(1, whole) as j:
                for q in range(unroll):
                    body(unroll * j + q, q % 2, unroll // 2 * j + q // 2, q, False, j)
        if whole:
            for u in range(unroll * whole, n_units):
                body(u, u % 2, u // 2, u % unroll, False, u // unroll)

    with nc.Block() as block:

        @block.sync
        def _(sp):
            def load(u, s, turn, q, fresh, j):
                if not fresh:
                    sp.wait_ge(c.low_ready, u + (u0 - 1))
                if not (fresh and ready):
                    sp.dma_start(c.raw[:, s, 0:w], weights[u + first]).then_inc(c.loaded[s], 16)
                if "sp" in background:
                    background["sp"](sp, q, j)
            units(sp, load)
            if then:
                for s in range(2):
                    sp.wait_ge(c.low_ready, u0 + n_units - 1 + s)
                    sp.dma_start(c.raw[:, s, 0:then[2] * P],
                                 then[0][then[1] + s]).then_inc(c.loaded[s], 16)

        def pairs(eng, split, epilogue):
            if not ready:
                split(0, 0, 0, True)
            n = (n_units - 1) // unroll

            def group(j, fresh):
                for q in range(unroll):
                    split(unroll * j + q + 1, (q + 1) % 2, unroll // 2 * j + (q + 1) // 2,
                          fresh and q == 0)
                    epilogue(unroll * j + q, q % 2, q, j)
            if n:
                group(0, True)
            if n > 1:
                with eng.Fori(1, n) as j:
                    group(j, False)
            for u in range(n * unroll, n_units):
                if u + 1 < n_units:
                    split(u + 1, (u + 1) % 2, (u + 1) // 2, u == 0)
                elif then:
                    split(n_units, 0, n_units // 2, False, then[2] * P)
                epilogue(u, u % 2, u % unroll, u // unroll)

        @block.scalar
        def _(act):
            def split(u, s, turn, fresh, w=w):
                act.wait_ge(c.loaded[s], 16 * turn + 16 * (l0[s] + 1))
                if not fresh:
                    act.wait_ge(c.unit_done, u + (u0 - 1))
                nc.scalar.copy(c.parts[:, s, 0, 0:w], c.raw[:, s, 0:w]).then_inc(c.high_ready, 1)

            def epilogue(u, s, q, j):
                if "act" in background:
                    background["act"](act, q, j)
                if act_epilogue:
                    act.wait_ge(c.unit_done, u + (u0 + 1))
                    act_epilogue(act, u, s, c.banks(2 * s), act_count, dve_count, q, j)
            pairs(act, split, epilogue)

        @block.vector
        def _(dve):
            def split(u, s, turn, fresh, w=w):
                dve.wait_ge(c.high_ready, u + (u0 + 1))
                nc.vector.tensor_tensor(c.parts[:, s, 1, 0:w], c.raw[:, s, 0:w],
                                        c.parts[:, s, 0, 0:w].bitcast(F32),
                                        ALU.subtract).then_inc(c.low_ready, 1)

            def epilogue(u, s, q, j):
                if "dve" in background:
                    background["dve"](dve, q, j)
                if dve_epilogue:
                    dve.wait_ge(c.unit_done, u + (u0 + 1))
                    dve_epilogue(dve, u, s, c.banks(2 * s), act_count, dve_count, q, j)
            pairs(dve, split, epilogue)

        if "pool" in background:
            @block.gpsimd
            def _(pool):
                background["pool"](pool)

        @block.tensor
        def _(pe):
            def product(bank, s, k0, kt, moving):
                n = 0
                for k in range(kt):
                    at = slice((k0 + k) * P, (k0 + k + 1) * P)
                    for wp, xp in ((0, 0), (0, 1), (1, 0)):
                        for h in range(halves):
                            mm = nc.tensor.matmul(c.psum[:, bank + h, 0:cols],
                                                  c.parts[:, s, wp, at], moving(k, xp, h),
                                                  start=(n < halves),
                                                  stop=(n >= halves * (3 * kt - 1)))
                            n += 1
                return mm

            def unit(u, s, turn, q, fresh, j):
                pe.wait_ge(c.low_ready, u + (u0 + 1))
                if not fresh:
                    if banks_read_by == "act":
                        pe.wait_ge(c.act_done, act_count(u - 2, act_per_unit - 1))
                    else:
                        pe.wait_ge(c.dve_done, dve_count(u - 2, dve_per_unit - 1))
                mm = product(2 * s, s, 0, kt, rhs)
                if extra_kt:
                    mm = product(4 + 2 * s, s, kt, extra_kt,
                                 lambda k, xp, h: extra_rhs(k, xp, h, q))
                mm.then_inc(c.unit_done, 1)
                if "pe" in background:
                    background["pe"](pe, q, j)
            units(pe, unit)


VECTORS = {}


def _columns():
    n = 0
    for name, k in (
        ("norm_mix_pre", 8), ("norm_mix_post", 8), ("norm_mlp_pre", 8), ("norm_mlp_post", 8),
        ("dn_conv", 24), ("b_gate", 32), ("mla_q_norm", 2), ("mla_kv_norm", 1),
        ("gla_gate_bias", 1), ("gla_norm", 1), ("dn_norm", 1), ("row_bias", 1), ("dn_a_log", 1),
        ("fox_f_bias", 1), ("norm_g_2", 8), ("final_g_2", 8), ("mod_b_2", 24), ("c_2", 16),
        ("a_conv_2", 32), ("a_br_2", 8), ("a_bi_2", 8), ("a_lam_2", 8), ("b_conv_2", 12),
        ("c_conv_2", 124), ("c_ln_g_2", 4), ("c_ln_b_2", 4), ("c_pw_b_2", 4), ("d_b_2", 4),
        ("d_scale_2", 4),
    ):
        VECTORS[name] = (n, k)
        n += k
    return n


N_VECTORS = _columns()


def vec(c, name, k=0, n=1):
    start, count = VECTORS[name]
    assert k + n <= count
    return c.vectors[:, start + k:start + k + n]


def bcast(ap, n):
    return ap.unsqueeze(2).broadcast_to([ap.shape[0], ap.shape[1], n])


def over_heads(ap, n=HEADS):
    return ap.unsqueeze(1).broadcast_to([ap.shape[0], n, ap.shape[1]])


def heads(ap, n=HEADS):
    return ap.rearrange("p (h m) -> p h m", h=n)


def store(c, eng, dram, tile):
    c.stored += 16
    eng.dma_start(dram, tile).then_inc(c.scratch_stored, 16)


def store_slot(c, eng, dram, tile, s):
    c.slots[s] += 16
    eng.dma_start(dram, tile).then_inc(c.slot_stored[s], 16)


def wait_slots(c, eng):
    for s in range(2):
        eng.wait_ge(c.slot_stored[s], c.slots[s])


def load_constants(nc, c, t):
    c.ident = c.sb("identity", [P, P])
    c.ones = c.sb("all_ones", [P, P])
    c.head_ones = c.sb("ones_by_head_pair", [P, P])
    c.vectors = c.sb("vectors", [P, N_VECTORS])
    c.eps = c.sb("epsilon", [P, 2])
    c.silu = c.sb("mod_silu", [P, 16])
    dma, vecs = Steps(c, "dma", [("load", 64)]), Steps(c, "vec", [("eps", 2)])
    silu = Steps(c, "act", ["silu"])
    with nc.Block() as block:
        @block.sync
        def _(sp):
            for n, (dst, src) in enumerate((
                (c.ident, t["squares"][0]), (c.ones, t["squares"][1]),
                (c.head_ones, t["squares"][2]), (c.vectors, t["vectors"]),
            )):
                sp.dma_start(dst[:], src).then_inc(dma.sem, 16)
            sp.wait_ge(dma.sem, 64)

        @block.vector
        def _(dve):
            for n, value in enumerate((EPS, LN_EPS)):
                nc.vector.memset(c.eps[:, n:n + 1], value).then_inc(vecs.step("eps"), 1)
        @block.scalar
        def _(act):
            act.wait_ge(dma.sem, 64)
            nc.scalar.activation(c.silu[:], vec(c, "c_2", 0, 16), ACT.Silu).then_inc(
                silu.step("silu"), 1)
    silu.end()
    c.base["dma"] = 64
    vecs.end()


def norm_input(nc, c, t, hidden):
    with ExitStack() as ctx:
        x = c.sb("x_tokens", [P, BLK, D], ctx=ctx)
        junk = c.sb("x_squares", [P, D], ctx=ctx)
        ss = c.sb("x_square_sums", [P, BLK], ctx=ctx)
        root = c.sb("x_rms", [P, BLK], ctx=ctx)
        rstd = c.sb("x_rstd", [P, BLK], ctx=ctx)
        groups = KT * NH
        act = Steps(c, "act", [("square", BLK), "root", ("high", groups)])
        vecs = Steps(c, "vec", ["rstd", ("scaled", BLK), ("low", groups)])
        pes = Steps(c, "pe", [("turned", groups)])
        base = c.base["dma"]
        c.base["dma"] += 16 * 2
        xb = t["x"].rearrange("(b p) d -> p b d", p=P)
        with nc.Block() as block:
            @block.sync
            def _(sp):
                for n in range(2):
                    b = slice(n * BLK // 2, (n + 1) * BLK // 2)
                    sp.dma_start(x[:, b, :], xb[:, b, :]).then_inc(c.steps["dma"], 16)

            @block.scalar
            def _(a):
                a.wait_ge(c.steps["dma"], base + 32)
                for b in range(BLK):
                    if b:
                        a.wait_ge(act.sem, act.value("square", b - 1))
                    nc.scalar.activation(junk[:], x[:, b, :], ACT.Square,
                                         accum_out=ss[:, b:b + 1]).then_inc(act.step("square"), 1)
                a.wait_ge(act.sem, act.value("square"))
                nc.scalar.activation(root[:], ss[:], ACT.Sqrt, scale=1.0 / D,
                                     bias=c.eps[:, 0:1]).then_inc(act.step("root"), 1)
                for k in range(KT):
                    for h in range(NH):
                        g = k * NH + h
                        a.wait_ge(pes.sem, pes.value("turned", g))
                        nc.scalar.activation(
            hidden[:, k, 0, h * HALF:(h + 1) * HALF], c.psum[:, g % 4, :], ACT.Copy,
            scale=vec(c, "norm_mix_pre", k)).then_inc(act.step("high"), 1)

            @block.vector
            def _(v):
                v.wait_ge(act.sem, act.value("root"))
                nc.vector.reciprocal(rstd[:], root[:]).then_inc(vecs.step("rstd"), 1)
                v.wait_ge(vecs.sem, vecs.value("rstd"))
                for b in range(BLK):
                    nc.vector.tensor_scalar(x[:, b, :], x[:, b, :],
                                            rstd[:, b:b + 1], None, ALU.mult).then_inc(
                        vecs.step("scaled"), 1)
                for k in range(KT):
                    for h in range(NH):
                        g = k * NH + h
                        v.wait_ge(act.sem, act.value("high", g))
                        cols = slice(h * HALF, (h + 1) * HALF)
                        nc.vector.scalar_tensor_tensor(
            hidden[:, k, 1, cols], c.psum[:, g % 4, :], vec(c, "norm_mix_pre", k),
            hidden[:, k, 0, cols].bitcast(F32), ALU.mult, ALU.subtract).then_inc(
                            vecs.step("low"), 1)

            @block.tensor
            def _(p):
                p.wait_ge(vecs.sem, vecs.value("scaled"))
                for k in range(KT):
                    for h in range(NH):
                        g = k * NH + h
                        if g >= 4:
                            p.wait_ge(vecs.sem, vecs.value("low", g - 4))
                        for q in range(4):
                            mm = nc.tensor.transpose(c.psum[:, g % 4, q * P:(q + 1) * P],
                                                     x[:, 4 * h + q, k * P:(k + 1) * P], c.ident[:])
                        mm.then_inc(pes.step("turned"), 1)
        for s in (act, vecs, pes):
            s.end()


def project(nc, c, weights, first, n_units, hidden, out, then=None, act_epilogue=None,
            **options):
    def evacuate(act, u, s, result, act_count, dve_count, q, j):
        nc.scalar.copy(out[:, bass.ds(u, 1), :].rearrange("p a n -> p (a n)"),
                       result).then_inc(c.act_done, 1)
    gemm(nc, c, weights, n_units, KT, lambda k, part, h: hidden[:, k, part, h * HALF:(h + 1) * HALF],
         act_per_unit=1, act_epilogue=act_epilogue or evacuate, first=first, then=then, **options)


MOD_LOADS = 8


def project_and_modulate(nc, c, t, hidden, proj, times, plus, gate):
    with ExitStack() as ctx:
        w = c.sb("mod_weights", [P, 2, 3 * D], ctx=ctx)
        mod = c.sb("mod_out", [P, 24, 2], ctx=ctx)
        loaded = [c.sem(f"mod_weights_loaded_{s}") for s in range(2)]
        pes = Steps(c, "pe", [("unit", 2)])

        def load(sp, q, j):
            if not isinstance(j, int) or j:
                sp.wait_ge(pes.sem, pes.value_before("unit", j, q))
            sp.dma_start(w[:, q, :], t["mod_w"][2 * j + q]).then_inc(loaded[q], 16)

        def multiply(pe, q, j):
            pe.wait_ge(loaded[q], 16 * j + 16)
            for x in range(3):
                at = 12 * j + (6 * q + 2 * x)
                for k in range(KT):
                    mm = nc.tensor.matmul(c.psum[:, 6, bass.ds(at, 2)],
                                          w[:, q, x * D + k * P:x * D + (k + 1) * P],
                                          c.silu[:, 2 * k:2 * k + 2], start=(k == 0),
                                          stop=(k == KT - 1))
            mm.then_inc(pes.step("unit"), 1)
        project(nc, c, t["w_in"], 2, MOD_LOADS, hidden, proj, (t["w_in"], 10, KT),
                background={"sp": load, "pe": multiply})
        pes.end(MOD_LOADS // 2)
        vecs = Steps(c, "vec", ["mod", "scale", "times", "plus", "gate"])
        with nc.Block() as block:
            @block.vector
            def _(v):
                nc.vector.tensor_tensor(
    mod[:], c.psum[:, 6, 0:48].rearrange("p (u w) -> p u w", w=2),
    bcast(vec(c, "mod_b_2", 0, 24), 2), ALU.add).then_inc(vecs.step("mod"), 1)
                v.wait_ge(vecs.sem, vecs.value("mod"))
                nc.vector.tensor_scalar(mod[:, 8:16, :], mod[:, 8:16, :], 1.0,
                                        None, ALU.add).then_inc(vecs.step("scale"), 1)
                v.wait_ge(vecs.sem, vecs.value("scale"))
                nc.vector.tensor_tensor(
  times[:], mod[:, 8:16, :], bcast(vec(c, "norm_g_2", 0, 8), 2), ALU.mult).then_inc(
                    vecs.step("times"), 1)
                nc.vector.tensor_copy(plus[:], mod[:, 0:8, :]).then_inc(vecs.step("plus"), 1)
                nc.vector.tensor_copy(gate[:], mod[:, 16:24, 0]).then_inc(vecs.step("gate"), 1)
        vecs.end()


def tokens_to_channels(nc, c, o_tok, out_dram, gate=None, gain=None, norm=False):
    with ExitStack() as ctx:
        o = c.sb("branch_channels", [P, 2, S], ctx=ctx)
        sq = c.sb("branch_squares", [P, BLK * HEADS, DH], ctx=ctx) if norm else None
        ss = c.sb("branch_square_sums", [P, BLK * HEADS], ctx=ctx) if norm else None
        root = c.sb("branch_rms", [P, BLK * HEADS], ctx=ctx) if norm else None
        rstd = c.sb("branch_rstd", [P, BLK * HEADS], ctx=ctx) if norm else None
        silu = c.sb("branch_silu", [P, 2, S], ctx=ctx) if norm else None
        act = Steps(c, "act", (["square", "root", "silu"] if norm else []) + [("unused", 0)])
        vecs = Steps(c, "vec", (["sums", "rstd", "scaled"] if norm else []) + [("out", 4)])
        pes = Steps(c, "pe", [("turned", 4)])
        view = o_tok.rearrange("p b (h d) -> p (b h) d", d=DH)
        with nc.Block() as block:
            if norm:
                @block.scalar
                def _(a):
                    nc.scalar.activation(sq[:], view, ACT.Square).then_inc(act.step("square"), 1)
                    a.wait_ge(vecs.sem, vecs.value("sums"))
                    nc.scalar.activation(root[:], ss[:], ACT.Sqrt, scale=1.0 / DH,
                                         bias=c.eps[:, 0:1]).then_inc(act.step("root"), 1)
                    nc.scalar.activation(silu[:], gate, ACT.Silu).then_inc(act.step("silu"), 1)

            @block.vector
            def _(v):
                if norm:
                    v.wait_ge(act.sem, act.value("square"))
                    nc.vector.tensor_reduce(ss[:], sq[:], AX_X, ALU.add).then_inc(
                        vecs.step("sums"), 1)
                    v.wait_ge(act.sem, act.value("root"))
                    nc.vector.reciprocal(rstd[:], root[:]).then_inc(vecs.step("rstd"), 1)
                    v.wait_ge(vecs.sem, vecs.value("rstd"))
                    nc.vector.tensor_tensor(view, view, bcast(rstd[:], DH),
                                            ALU.mult).then_inc(vecs.step("scaled"), 1)
                    v.wait_ge(act.sem, act.value("silu"))
                for g in range(4):
                    t, h = g // 2, g % 2
                    cols = slice(h * HALF, (h + 1) * HALF)
                    v.wait_ge(pes.sem, pes.value("turned", g))
                    if norm:
                        nc.vector.scalar_tensor_tensor(
            o[:, t, cols], c.psum[:, g, :], gain, silu[:, t, cols],
            ALU.mult, ALU.mult).then_inc(vecs.step("out"), 1)
                    else:
                        nc.vector.tensor_copy(o[:, t, cols], c.psum[:, g, :]).then_inc(
                            vecs.step("out"), 1)

            @block.tensor
            def _(p):
                if norm:
                    p.wait_ge(vecs.sem, vecs.value("scaled"))
                for g in range(4):
                    t, h = g // 2, g % 2
                    for q in range(4):
                        mm = nc.tensor.transpose(c.psum[:, g, q * P:(q + 1) * P],
                                                 o_tok[:, 4 * h + q, t * P:(t + 1) * P], c.ident[:])
                    mm.then_inc(pes.step("turned"), 1)

            @block.sync
            def _(sp):
                sp.wait_ge(vecs.sem, vecs.value("out"))
                store(c, sp, out_dram, o[:])
                sp.wait_ge(c.scratch_stored, c.stored)
        for s in (act, vecs, pes):
            s.end()


def channels_to_tokens(nc, c, src, dst):
    pes = Steps(c, "pe", [("turned", 4)])
    vecs = Steps(c, "vec", [("kept", 4)])
    with nc.Block() as block:
        @block.tensor
        def _(p):
            for g in range(4):
                for q in range(2):
                    for t in range(2):
                        mm = nc.tensor.transpose(
                            c.psum[:, g, (2 * q + t) * P:(2 * q + t + 1) * P],
                            src[:, t, (2 * g + q) * P:(2 * g + q + 1) * P], c.ident[:])
                mm.then_inc(pes.step("turned"), 1)

        @block.vector
        def _(v):
            for g in range(4):
                v.wait_ge(pes.sem, pes.value("turned", g))
                nc.vector.tensor_copy(
   dst[:, 2 * g:2 * g + 2, :].rearrange("p b n -> p (b n)"), c.psum[:, g, :]).then_inc(
                    vecs.step("kept"), 1)
    pes.end()
    vecs.end()


LEVELS = 6
DN_MASKS = 9


def delta_net(nc, c, t, hidden, small, modulated):
    with ExitStack() as ctx:
        proj = c.sb("dn_projected", [P, 8, S], ctx=ctx)
        project_and_modulate(nc, c, t, hidden, proj, *modulated)
        o_tok = c.sb("dn_out_tokens", [P, BLK + 1, 256], ctx=ctx)
        with ExitStack() as inner:
            rows = c.sb("dn_rows", [P, S], ctx=inner)
            g_tok = c.sb("dn_decay_tokens", [P, BLK, HEADS], ctx=inner)
            delta_net_inputs(nc, c, t, proj, rows, g_tok, small)
            delta_net_chunks(nc, c, t, proj, rows, g_tok, o_tok)
        tokens_to_channels(nc, c, o_tok[:, 1:, :], t["branch"][0], gate=proj[:, 6:8, :],
                           gain=vec(c, "dn_norm"), norm=True)


def delta_net_inputs(nc, c, t, proj, rows, g_tok, small):
    with ExitStack() as ctx:
        conv = c.sb("dn_conv_out", [P, 2, S], ctx=ctx)
        sq = c.sb("dn_squares", [P, 2, S], ctx=ctx)
        root = c.sb("dn_norms", [P, 2, S], ctx=ctx)
        restart = c.sb("dn_chunk_restart", [P, S], ctx=ctx)
        soft = c.sb("dn_softplus", [P, S], ctx=ctx)
        rate = c.sb("dn_rate", [P, 1], ctx=ctx)
        act = Steps(c, "act", [("silu", 6), ("square", 4), "beta", "abs", "exp", "ln", "rate",
                               ("root", 4), "kept", "decay", "tail"])
        vecs = Steps(c, "vec", ["zero", ("conv", 24), "relu", "soft", "g", "gc", "to_end",
                                (("rstd", "unit"), 4), ("g_tok", 2)])
        pes = Steps(c, "pe", [("sums", 4), ("turned", 2)])
        d0 = c.base["dma"]
        c.base["dma"] += 16
        gl = slice(32, 36)
        with nc.Block() as block:
            @block.sync
            def _(sp):
                sp.dma_start(restart[:], t["restart"].partition_broadcast(P)).then_inc(
                    c.steps["dma"], 16)

            @block.scalar
            def _(a):
                for n in range(6):
                    a.wait_ge(vecs.sem, vecs.value("conv", 4 * n + 3))
                    nc.scalar.activation(proj[:, n, :], conv[:, n % 2, :], ACT.Silu).then_inc(
                        act.step("silu"), 1)
                for n in range(4):
                    a.wait_ge(act.sem, act.value("silu", n))
                    if n >= 2:
                        a.wait_ge(pes.sem, pes.value("sums", n - 2))
                    nc.scalar.activation(sq[:, n % 2, :], proj[:, n, :],
                                         ACT.Square).then_inc(act.step("square"), 1)
                a.wait_ge(vecs.sem, vecs.value("zero"))
                nc.scalar.activation(rows[0:4, :], small[0:4, 0, :], ACT.Sigmoid).then_inc(
                    act.step("beta"), 1)
                nc.scalar.activation(soft[gl, :], small[gl, 0, :], ACT.Abs,
                                     bias=vec(c, "row_bias")[gl, :]).then_inc(act.step("abs"), 1)
                a.wait_ge(act.sem, act.value("abs"))
                nc.scalar.activation(soft[gl, :], soft[gl, :], ACT.Exp, scale=-1.0).then_inc(
                    act.step("exp"), 1)
                a.wait_ge(act.sem, act.value("exp"))
                nc.scalar.activation(soft[gl, :], soft[gl, :], ACT.Ln, bias=1.0).then_inc(
                    act.step("ln"), 1)
                nc.scalar.activation(rate[gl, :], vec(c, "dn_a_log")[gl, :],
                                     ACT.Exp).then_inc(act.step("rate"), 1)
                for n in range(4):
                    a.wait_ge(pes.sem, pes.value("sums", n))
                    if n >= 2:
                        a.wait_ge(vecs.sem, vecs.value("unit", n - 2))
                    nc.scalar.activation(root[:, n % 2, :], c.banks(2 * n),
                                         ACT.Sqrt, bias=c.eps[:, 0:1]).then_inc(act.step("root"), 1)
                a.wait_ge(vecs.sem, vecs.value("to_end"))
                nc.scalar.copy(rows[96:100, :], soft[gl, :]).then_inc(act.step("kept"), 1)
                nc.scalar.activation(rows[gl, :], soft[gl, :], ACT.Exp).then_inc(
                    act.step("decay"), 1)
                nc.scalar.activation(rows[64:68, :], small[gl, 0, :], ACT.Exp).then_inc(
                    act.step("tail"), 1)

            @block.vector
            def _(v):
                nc.vector.memset(rows[:], 0.0).then_inc(vecs.step("zero"), 1)
                for n in range(6):
                    w = [vec(c, "dn_conv", 4 * n + k) for k in range(4)]
                    dst = conv[:, n % 2, :]
                    if n >= 2:
                        v.wait_ge(act.sem, act.value("silu", n - 2))
                    nc.vector.tensor_scalar(dst, proj[:, n, :], w[3], None,
                                            ALU.mult).then_inc(vecs.step("conv"), 1)
                    for s in (1, 2, 3):
                        v.wait_ge(vecs.sem, vecs.value("conv", 4 * n + s - 1))
                        nc.vector.scalar_tensor_tensor(
           dst[:, s:], proj[:, n, 0:S - s], w[3 - s], dst[:, s:], ALU.mult,
           ALU.add).then_inc(vecs.step("conv"), 1)
                v.wait_ge(act.sem, act.value("rate"))
                nc.vector.tensor_scalar(small[gl, 0, :], small[gl, 0, :],
                                        vec(c, "row_bias")[gl, :], 0.0, ALU.add,
                                        ALU.max).then_inc(vecs.step("relu"), 1)
                v.wait_ge(vecs.sem, vecs.value("relu"))
                nc.vector.tensor_tensor(small[gl, 0, :], small[gl, 0, :],
                                        soft[gl, :], ALU.add).then_inc(vecs.step("soft"), 1)
                v.wait_ge(vecs.sem, vecs.value("soft"))
                nc.vector.tensor_scalar(small[gl, 0, :], small[gl, 0, :],
                                        rate[gl, :], -1.0, ALU.mult, ALU.mult).then_inc(
                    vecs.step("g"), 1)
                v.wait_ge(vecs.sem, vecs.value("g"))
                v.wait_ge(c.steps["dma"], d0 + 16)
                nc.vector.tensor_tensor_scan(soft[gl, :], restart[gl, :],
                                             small[gl, 0, :], 0.0, ALU.mult, ALU.add).then_inc(
                    vecs.step("gc"), 1)
                v.wait_ge(vecs.sem, vecs.value("gc"))
                by_chunk = soft[gl, :].rearrange("p (n m) -> p n m", m=CH)
                nc.vector.tensor_tensor(
 small[gl, 0, :].rearrange("p (n m) -> p n m", m=CH),
 by_chunk[:, :, CH - 1:CH].broadcast_to([4, S // CH, CH]), by_chunk,
 ALU.subtract).then_inc(vecs.step("to_end"), 1)
                for n in range(4):
                    v.wait_ge(act.sem, act.value("root", n))
                    nc.vector.reciprocal(root[:, n % 2, :], root[:, n % 2, :]).then_inc(
                        vecs.step("rstd"), 1)
                    v.wait_ge(vecs.sem, vecs.value("rstd", n))
                    nc.vector.scalar_tensor_tensor(
       proj[:, n, :], proj[:, n, :], DH ** -0.5 if n < 2 else 1.0,
       root[:, n % 2, :], ALU.mult, ALU.mult).then_inc(vecs.step("unit"), 1)
                for g in range(2):
                    v.wait_ge(pes.sem, pes.value("turned", g))
                    nc.vector.tensor_copy(
      g_tok[:, 4 * g:4 * g + 4, :],
      heads(c.psum[:, g, :])[:, :, 96:100]).then_inc(vecs.step("g_tok"), 1)

            @block.tensor
            def _(p):
                for n in range(4):
                    p.wait_ge(act.sem, act.value("square", n))
                    for h in range(NH):
                        mm = nc.tensor.matmul(c.psum[:, 2 * n + h, :], c.head_ones[:],
                                              sq[:, n % 2, h * HALF:(h + 1) * HALF],
                                              start=True, stop=True)
                    mm.then_inc(pes.step("sums"), 1)
                p.wait_ge(act.sem, act.value("tail"))
                for g in range(2):
                    for q in range(4):
                        b = 4 * g + q
                        mm = nc.tensor.transpose(c.psum[:, g, q * P:(q + 1) * P],
                                                 rows[:, b * P:(b + 1) * P], c.ident[:])
                    mm.then_inc(pes.step("turned"), 1)
        for s in (act, vecs, pes):
            s.end()


def place(h):
    return 2 * (h % 2) + h // 2


def by_parity(tile):
    return tile[:].rearrange("p (a m) n -> p a (m n)", a=2)


def delta_net_chunks(nc, c, t, proj, rows, g_tok, o_tok):
    with ExitStack() as ctx:
        def sb(name, *shape):
            return c.sb("dn_" + name, [P, *shape], ctx=ctx)
        masks = sb("masks", DN_MASKS, P)
        select = sb("row_selectors", 10, P)
        ks, qs, kb, kbe, kt, vb = (sb(n, 2, P) for n in
                                   ("k", "q", "k_beta", "k_beta_decay", "k_tail", "v_beta"))
        twice = lambda *a: (sb(*a), sb(*a))
        qds, all_ends, qks = twice("q_decay", 2, P), twice("chunk_decay", 2, 2), \
            twice("qk_turned", HEADS, P)
        dec_t, dec = sb("decay_turned", HEADS, P), sb("decay", HEADS, P)
        a_t, a_0 = sb("a_turned", HEADS, P), sb("a", HEADS, P)
        a_lev = sb("a_levels_turned", LEVELS - 1, HEADS * P)
        inv, inv_t = sb("inverse", HEADS, P), sb("inverse_turned", HEADS, P)
        prod = a_0
        toks, vb_tok = twice("keys_by_token", HEADS * P), sb("values_by_token", 256)
        w_ts, us, v_new = twice("w_turned", 2, P), twice("u", 256), sb("v_new", 256)
        state, fading = sb("state", 2, P), sb("state_decayed", 2, P)
        levels = range(1, LEVELS)
        carried = {"pe": {1: "read0", 2: "add0", 3: "read1", 4: "add1"},
                   "vec": {n + 1: [f"{x}{n // 2}" for x in (("v_new", "fade"),
                                                            ("state_a", "state_b"))[n % 2]]
                           for n in range(4)}}
        pes = Steps(c, "pe", ["rows", "kk", "tok", "qk_odd"]
                    + sum([[f"a_inverse{n}"] + ([carried["pe"][n]] if n < 5 else [])
                           + [f"grow{n}"] for n in levels], []) + ["uw"])
        act = Steps(c, "act", ["k", "q", "decay_turned", "decay", "keys_tok", "values_tok"]
                    + [f"a_inverse{n}" for n in levels[:-1]] + ["out", f"a_inverse{LEVELS - 1}"])
        vecs = Steps(c, "vec", ["k_beta", "v_beta", "q_decay", "k_tail", "k_beta_decay", "ends",
                                "diff", "upper", "lower", "a_turned", "a", "qk_even", "qk_odd",
                                "a_level0", "inverse0", "a_level0t", "turned0"]
                     + sum([[f"turned{n}", f"inverse{n}"] + carried["vec"][n]
                            for n in levels[:-1]], [])
                     + [f"turned{LEVELS - 1}", "w", "u"])
        pool = Steps(c, "pool", [f"level{n}" for n in levels])
        d0 = c.base["dma"]
        c.base["dma"] += 32
        c.base["pool"] += pool.n
        pool.base += pool.n
        ps = c.psum
        ends_view = lambda: ps[:, 0, 256:512].rearrange("p (a j n) -> p a j n", a=2, j=2)

        def hp(h):
            return slice(64 * (h % 2), 64 * (h % 2) + 64)

        def blocks(eng, body):
            with eng.Fori(0, BLK // 2) as pair:
                for parity in range(2):
                    body(2 * pair + parity, parity)

        def read(j, par):
            r = slice(CH * j, CH * j + CH)
            for pair in range(2):
                to = slice(pair * P, (pair + 1) * P)
                nc.tensor.matmul(ps[r, 6, to], w_ts[par][:, pair, r], state[:, pair, :],
                                 start=True, stop=True)
                last = nc.tensor.matmul(ps[r, 7, to], qds[par][:, pair, r], state[:, pair, :],
                                        start=(pair == 0), stop=False, skip_group_check=True)
            return last

        def add(j, par):
            r = slice(CH * j, CH * j + CH)
            for pair in range(2):
                to = slice(pair * P, (pair + 1) * P)
                nc.tensor.matmul(ps[:, 6, 256 + pair * P:256 + (pair + 1) * P],
                                 toks[par][r, 256 + pair * P:256 + (pair + 1) * P],
                                 v_new[r, to], start=True, stop=True)
            for h in range(HEADS):
                to = slice(64 * h, 64 * h + 64)
                last = nc.tensor.matmul(ps[r, 7, to], qks[par][r, place(h), r], v_new[r, to],
                                        start=False, stop=(h == HEADS - 1), skip_group_check=True)
            return last

        def new_values(j, par):
            r = slice(CH * j, CH * j + CH)
            return nc.vector.tensor_tensor(v_new[r, :], us[par][r, :], ps[r, 6, 0:256],
                                           ALU.subtract)

        def fade(j, par):
            return nc.vector.tensor_tensor(fading[:], state[:], bcast(all_ends[par][:, :, j], P),
                                           ALU.mult)

        def new_state(half):
            q = slice(64 * half, 64 * half + 64)
            new = ps[:, 6, 256:512].rearrange("p (a n) -> p a n", a=2)
            return nc.vector.tensor_tensor(state[q, :, q], fading[q, :, q], new[q, :, q], ALU.add)

        with nc.Block() as block:
            @block.sync
            def _(sp):
                sp.dma_start(masks[:], t["dn_masks"]).then_inc(c.steps["dma"], 16)
                sp.dma_start(select[:], t["selectors"]).then_inc(c.steps["dma"], 16)
                sp.wait_ge(c.steps["dma"], d0 + 32)

            @block.gpsimd
            def _(g):
                for tile in (w_ts[1], us[1], toks[1], qds[1], qks[1], all_ends[1]):
                    nc.gpsimd.memset(tile[:], 0.0)
                nc.gpsimd.memset(state[:], 0.0).then_inc(pool.sem, pool.n)
                g.wait_ge(c.steps["dma"], d0 + 32)

                def body(i, par):
                    for n in levels:
                        g.wait_ge(vecs.sem, vecs.value("a_turned", i=i))
                        if n == 1:
                            g.wait_ge(pes.sem, pes.value_before(f"a_inverse{LEVELS - 1}", i))
                        nc.gpsimd.tensor_tensor(
      heads(a_lev[:, n - 1, :]), a_t[:], over_heads(masks[:, 3 + n, :]),
      ALU.mult).then_inc(pool.step(f"level{n}"), 1)
                blocks(g, body)

            @block.scalar
            def _(a):
                def body(i, par):
                    cols = bass.ds(i * P, P)
                    a.wait_ge(pes.sem, pes.value_before("uw", i))
                    nc.scalar.copy(ks[:], proj[:, 2:4, cols]).then_inc(act.step("k"), 1)
                    nc.scalar.copy(qs[:], proj[:, 0:2, cols]).then_inc(act.step("q"), 1)
                    a.wait_ge(vecs.sem, vecs.value("upper", i=i))
                    nc.scalar.activation(dec_t[:], dec_t[:], ACT.Exp).then_inc(
                        act.step("decay_turned"), 1)
                    a.wait_ge(vecs.sem, vecs.value("lower", i=i))
                    nc.scalar.activation(dec[:], dec[:], ACT.Exp, scale=-1.0).then_inc(
                        act.step("decay"), 1)
                    a.wait_ge(pes.sem, pes.value("tok", i=i))
                    nc.scalar.copy(toks[par][:], ps[:, 0, :]).then_inc(act.step("keys_tok"), 1)
                    nc.scalar.copy(vb_tok[:], ps[:, 1, 0:256]).then_inc(act.step("values_tok"), 1)
                    for n in levels:
                        if n == LEVELS - 1:
                            a.wait_ge(pes.sem, pes.value("add1", i=i))
                            nc.scalar.copy(
                 o_tok[:, bass.ds(i, 1), :].rearrange("p b n -> p (b n)"),
                 ps[:, 7, 0:256]).then_inc(act.step("out"), 1)
                        a.wait_ge(pes.sem, pes.value(f"a_inverse{n}", i=i))
                        nc.scalar.copy(prod[:], heads(ps[:, 3, :])).then_inc(
                            act.step(f"a_inverse{n}"), 1)
                blocks(a, body)

            @block.vector
            def _(v):
                v.wait_ge(c.steps["dma"], d0 + 32)
                v.wait_ge(pool.sem, pool.base)

                def body(i, par):
                    cols = bass.ds(i * P, P)
                    tt = nc.vector.tensor_tensor
                    before = 1 - par
                    qd, ends, qk = qds[par], all_ends[par], qks[par]
                    beta, decay = ps[:, 0, 0:256].rearrange("p (a n) -> p a n", a=2), \
                        ps[:, 0, 256:512].rearrange("p (a n) -> p a n", a=2)
                    tail = ps[:, 1, 0:256].rearrange("p (a n) -> p a n", a=2)
                    v.wait_ge(pes.sem, pes.value("rows", i=i))
                    v.wait_ge(act.sem, act.value("q", i=i))
                    tt(kb[:], ks[:], beta, ALU.mult).then_inc(vecs.step("k_beta"), 1)
                    tt(vb[:], proj[:, 4:6, cols], beta, ALU.mult).then_inc(vecs.step("v_beta"), 1)
                    tt(qd[:], qs[:], decay, ALU.mult).then_inc(vecs.step("q_decay"), 1)
                    tt(kt[:], ks[:], tail, ALU.mult).then_inc(vecs.step("k_tail"), 1)
                    v.wait_ge(vecs.sem, vecs.value("k_beta", i=i))
                    tt(kbe[:], kb[:], decay, ALU.mult).then_inc(vecs.step("k_beta_decay"), 1)
                    nc.vector.tensor_copy(ends[:], ends_view()[:, :, :, CH - 1]).then_inc(
                        vecs.step("ends"), 1)
                    gi = g_tok[:, bass.ds(i, 1), :].rearrange("p b h -> p (b h)")
                    tt(dec[:], heads(ps[:, 2, :]), bcast(gi, P), ALU.subtract).then_inc(
                        vecs.step("diff"), 1)
                    v.wait_ge(vecs.sem, vecs.value("diff", i=i))
                    tt(dec_t[:], dec[:], over_heads(masks[:, 0, :]), ALU.add).then_inc(
                        vecs.step("upper"), 1)
                    tt(dec[:], dec[:], over_heads(masks[:, 1, :]), ALU.add).then_inc(
                        vecs.step("lower"), 1)
                    v.wait_ge(pes.sem, pes.value("kk", i=i))
                    v.wait_ge(act.sem, act.value("decay", i=i))
                    tt(by_parity(a_t), ps[:, 3:6:2, 0:256], by_parity(dec_t),
                       ALU.mult).then_inc(vecs.step("a_turned"), 1)
                    tt(by_parity(a_0), ps[:, 3:6:2, 256:512], by_parity(dec),
                       ALU.mult).then_inc(vecs.step("a"), 1)
                    tt(by_parity(qk)[:, 0, :], ps[:, 4, 0:256],
                       by_parity(dec_t)[:, 0, :], ALU.mult).then_inc(vecs.step("qk_even"), 1)
                    v.wait_ge(pes.sem, pes.value("qk_odd", i=i))
                    tt(by_parity(qk)[:, 1, :], ps[:, 2, 0:256],
                       by_parity(dec_t)[:, 1, :], ALU.mult).then_inc(vecs.step("qk_odd"), 1)
                    v.wait_ge(vecs.sem, vecs.value("a", i=i))
                    tt(a_0[:], a_0[:], over_heads(masks[:, 2, :]), ALU.mult).then_inc(
                        vecs.step("a_level0"), 1)
                    v.wait_ge(vecs.sem, vecs.value("a_level0", i=i))
                    tt(inv[:], over_heads(c.ident[:]), a_0[:], ALU.subtract).then_inc(
                        vecs.step("inverse0"), 1)
                    tt(inv_t[:], a_t[:], over_heads(masks[:, 3, :]),
                       ALU.mult).then_inc(vecs.step("a_level0t"), 1)
                    v.wait_ge(vecs.sem, vecs.value("a_level0t", i=i))
                    tt(inv_t[:], over_heads(c.ident[:]), inv_t[:],
                       ALU.subtract).then_inc(vecs.step("turned0"), 1)
                    for n in levels:
                        v.wait_ge(pes.sem, pes.value(f"grow{n}", i=i))
                        tt(inv_t[:], inv_t[:], heads(ps[:, 5, :]),
                           ALU.subtract).then_inc(vecs.step(f"turned{n}"), 1)
                        if n == LEVELS - 1:
                            break
                        tt(inv[:], inv[:], heads(ps[:, 4, :]),
                           ALU.subtract).then_inc(vecs.step(f"inverse{n}"), 1)
                        j = (n - 1) // 2
                        if n % 2:
                            v.wait_ge(pes.sem, pes.value(f"read{j}", i=i))
                            new_values(j, before).then_inc(vecs.step(f"v_new{j}"), 1)
                            fade(j, before).then_inc(vecs.step(f"fade{j}"), 1)
                        else:
                            v.wait_ge(pes.sem, pes.value(f"add{j}", i=i))
                            v.wait_ge(vecs.sem, vecs.value(f"fade{j}", i=i))
                            new_state(0).then_inc(vecs.step(f"state_a{j}"), 1)
                            new_state(1).then_inc(vecs.step(f"state_b{j}"), 1)
                    v.wait_ge(pes.sem, pes.value("uw", i=i))
                    nc.vector.tensor_copy(
          w_ts[par][:], ps[:, 2, 256:512].rearrange("p (a n) -> p a n", a=2)).then_inc(
                        vecs.step("w"), 1)
                    nc.vector.tensor_copy(us[par][:], ps[:, 2, 0:256]).then_inc(vecs.step("u"), 1)
                blocks(v, body)

            @block.tensor
            def _(p):
                p.wait_ge(c.steps["dma"], d0 + 32)
                mm = nc.tensor.matmul

                def body(i, par):
                    cols = bass.ds(i * P, P)
                    before = 1 - par
                    tok = toks[par]
                    p.wait_ge(vecs.sem, vecs.value_before("u", i))
                    for kind in range(3):
                        for pair in range(2):
                            n = 2 * kind + pair
                            mm(ps[:, n // 4, (n % 4) * P:(n % 4 + 1) * P], select[:, n, :],
                               rows[:, cols], start=True, stop=True)
                    for h in range(HEADS):
                        last = mm(ps[:, 2, h * P:(h + 1) * P], select[:, 6 + h, :], rows[:, cols],
                                  start=True, stop=True)
                    last.then_inc(pes.step("rows"), 1)
                    p.wait_ge(act.sem, act.value("q", i=i))
                    p.wait_ge(vecs.sem, vecs.value("k_beta", i=i))
                    for h in range(HEADS):
                        bank, m = 3 + 2 * (h % 2), h // 2
                        to, to_2 = slice(m * P, (m + 1) * P), slice(256 + m * P, 384 + m * P)
                        mm(ps[:, bank, to], ks[hp(h), m, :], kb[hp(h), m, :], start=True, stop=True)
                        last = mm(ps[:, bank, to_2], kb[hp(h), m, :], ks[hp(h), m, :],
                                  start=True, stop=True)
                        if h % 2 == 0:
                            mm(ps[:, 4, to], ks[hp(h), m, :], qs[hp(h), m, :], start=True,
                               stop=True)
                    last.then_inc(pes.step("kk"), 1)
                    p.wait_ge(vecs.sem, vecs.value("ends", i=i))
                    for n, src in enumerate((kbe, kt, vb)):
                        for pair in range(2):
                            q = 2 * n + pair
                            last = nc.tensor.transpose(ps[:, q // 4, (q % 4) * P:(q % 4 + 1) * P],
                                                       src[:, pair, :], c.ident[:])
                    last.then_inc(pes.step("tok"), 1)
                    p.wait_ge(vecs.sem, vecs.value("diff", i=i))
                    for m in range(2):
                        last = mm(ps[:, 2, m * P:(m + 1) * P], ks[hp(1), m, :], qs[hp(1), m, :],
                                  start=True, stop=True)
                    last.then_inc(pes.step("qk_odd"), 1)
                    for n in levels:
                        p.wait_ge(pool.sem, pool.value(f"level{n}", i=i))
                        p.wait_ge(vecs.sem,
                                  vecs.value("turned0" if n == 1 else f"inverse{n - 1}", i=i))
                        for h in range(HEADS):
                            last = mm(ps[:, 3, h * P:(h + 1) * P],
                                      a_lev[:, n - 1, h * P:(h + 1) * P], inv[:, h, :], start=True,
                                      stop=True)
                        last.then_inc(pes.step(f"a_inverse{n}"), 1)
                        j = (n - 1) // 2
                        if n < LEVELS - 1 and n % 2:
                            if j:
                                p.wait_ge(vecs.sem, vecs.value("state_b0", i=i))
                            else:
                                p.wait_ge(act.sem, act.value_before("out", i))
                            read(j, before).then_inc(pes.step(f"read{j}"), 1)
                        elif n < LEVELS - 1:
                            p.wait_ge(vecs.sem, vecs.value(f"v_new{j}", i=i))
                            add(j, before).then_inc(pes.step(f"add{j}"), 1)
                        p.wait_ge(act.sem, act.value(f"a_inverse{n}", i=i))
                        for h in range(HEADS):
                            to = slice(h * P, (h + 1) * P)
                            last = mm(ps[:, 5, to], prod[:, h, :], inv_t[:, h, :], start=True,
                                      stop=True)
                            if n < LEVELS - 1:
                                last = mm(ps[:, 4, to], inv_t[:, h, :], prod[:, h, :], start=True,
                                          stop=True)
                        last.then_inc(pes.step(f"grow{n}"), 1)
                    p.wait_ge(vecs.sem, vecs.value(f"turned{LEVELS - 1}", i=i))
                    p.wait_ge(act.sem, act.value("values_tok", i=i))
                    for h in range(HEADS):
                        mm(ps[:, 2, 64 * h:64 * h + 64], inv_t[:, place(h), :],
                           vb_tok[:, 64 * h:64 * h + 64], start=True, stop=True)
                        last = mm(ps[hp(h), 2, 256 + P * (h // 2):256 + P * (h // 2) + P],
                                  tok[:, 64 * h:64 * h + 64], inv_t[:, place(h), :],
                                  start=True, stop=True)
                    last.then_inc(pes.step("uw"), 1)
                blocks(p, body)
        for s in (act, vecs, pes, pool):
            s.end(BLK)

        pes = Steps(c, "pe", ["read0", "add0", "read1", "add1"])
        vecs = Steps(c, "vec", ["v_new0", "fade0", "state_a0", "state_b0", "v_new1"])
        act = Steps(c, "act", ["out"])
        par = (BLK - 1) % 2
        with nc.Block() as block:
            @block.tensor
            def _(p):
                read(0, par).then_inc(pes.step("read0"), 1)
                p.wait_ge(vecs.sem, vecs.value("v_new0"))
                add(0, par).then_inc(pes.step("add0"), 1)
                p.wait_ge(vecs.sem, vecs.value("state_b0"))
                read(1, par).then_inc(pes.step("read1"), 1)
                p.wait_ge(vecs.sem, vecs.value("v_new1"))
                add(1, par).then_inc(pes.step("add1"), 1)

            @block.vector
            def _(v):
                v.wait_ge(pes.sem, pes.value("read0"))
                new_values(0, par).then_inc(vecs.step("v_new0"), 1)
                fade(0, par).then_inc(vecs.step("fade0"), 1)
                v.wait_ge(pes.sem, pes.value("add0"))
                v.wait_ge(vecs.sem, vecs.value("fade0"))
                new_state(0).then_inc(vecs.step("state_a0"), 1)
                new_state(1).then_inc(vecs.step("state_b0"), 1)
                v.wait_ge(pes.sem, pes.value("read1"))
                new_values(1, par).then_inc(vecs.step("v_new1"), 1)

            @block.scalar
            def _(a):
                a.wait_ge(pes.sem, pes.value("add1"))
                nc.scalar.copy(o_tok[:, BLK, :], ps[:, 7, 0:256]).then_inc(act.step("out"), 1)
        for s in (act, vecs, pes):
            s.end()


def gated_linear(nc, c, t, hidden, small):
    with ExitStack() as ctx:
        proj = c.sb("gla_projected", [P, 6, S], ctx=ctx)
        project(nc, c, t["w_in"], 13, 6, hidden, proj, (t["w_in"], 19, KT))
        o_tok = c.sb("gla_out_tokens", [P, BLK, 256], ctx=ctx)
        with ExitStack() as inner:
            v_tok = c.sb("gla_value_tokens", [P, BLK, 256], ctx=inner)
            channels_to_tokens(nc, c, proj[:, 2:4, :], v_tok)
            q_in, k_in, k_tail = (c.sb(n, [P, S], ctx=inner)
                                  for n in ("gla_q_in", "gla_k_in", "gla_k_tail"))
            ends = c.sb("gla_chunk_decay", [P, S // CH], ctx=inner)
            gated_linear_inputs(nc, c, t, proj, small, q_in, k_in, k_tail, ends)
            gated_linear_chunks(nc, c, t, q_in, k_in, k_tail, ends, v_tok, o_tok)
        tokens_to_channels(nc, c, o_tok, t["branch"][2], gate=proj[:, 4:6, :],
                           gain=vec(c, "gla_norm"), norm=True)


def gated_linear_inputs(nc, c, t, proj, small, q_in, k_in, k_tail, ends):
    with ExitStack() as ctx:
        restart = c.sb("gla_chunk_restart", [P, S], ctx=ctx)
        gate_up = c.sb("gla_gate_up", [32, P], ctx=ctx)
        soft = c.sb("gla_softplus", [P, S], ctx=ctx)
        b = c.sb("gla_log_decay", [P, S], ctx=ctx)
        act = Steps(c, "act", ["abs", "exp", "ln", "grow", "shrink", "tail"])
        vecs = Steps(c, "vec", ["neg", "log", "sum", "to_end", "ends", "q_in", "k_in", "k_tail"])
        pes = Steps(c, "pe", ["gate"])
        d0 = c.base["dma"]
        c.base["dma"] += 32
        tau = 1.0 / 16
        with nc.Block() as block:
            @block.sync
            def _(sp):
                sp.dma_start(restart[:], t["restart"].partition_broadcast(P)).then_inc(
                    c.steps["dma"], 16)
                sp.dma_start(gate_up[:], t["gla_gate_up"]).then_inc(c.steps["dma"], 16)

            @block.tensor
            def _(p):
                p.wait_ge(c.steps["dma"], d0 + 32)
                for h in range(NH):
                    mm = nc.tensor.matmul(c.psum[:, h, :], gate_up[:],
                                          small[0:32, 1, h * HALF:(h + 1) * HALF], start=True,
                                          stop=True)
                mm.then_inc(pes.step("gate"), 1)

            @block.scalar
            def _(a):
                bias = vec(c, "gla_gate_bias")
                a.wait_ge(pes.sem, pes.value("gate"))
                nc.scalar.activation(soft[:], c.banks(0), ACT.Abs, bias=bias).then_inc(
                    act.step("abs"), 1)
                a.wait_ge(act.sem, act.value("abs"))
                nc.scalar.activation(soft[:], soft[:], ACT.Exp, scale=-1.0).then_inc(
                    act.step("exp"), 1)
                a.wait_ge(act.sem, act.value("exp"))
                nc.scalar.activation(soft[:], soft[:], ACT.Ln, bias=1.0).then_inc(act.step("ln"), 1)
                a.wait_ge(vecs.sem, vecs.value("sum"))
                nc.scalar.activation(q_in[:], b[:], ACT.Exp, scale=tau).then_inc(
                    act.step("grow"), 1)
                nc.scalar.activation(k_in[:], b[:], ACT.Exp, scale=-tau).then_inc(
                    act.step("shrink"), 1)
                a.wait_ge(vecs.sem, vecs.value("to_end"))
                nc.scalar.activation(k_tail[:], k_tail[:], ACT.Exp, scale=tau).then_inc(
                    act.step("tail"), 1)

            @block.vector
            def _(v):
                v.wait_ge(act.sem, act.value("abs"))
                nc.vector.tensor_scalar(b[:], c.banks(0), vec(c, "gla_gate_bias"),
                                        0.0, ALU.add, ALU.min).then_inc(vecs.step("neg"), 1)
                v.wait_ge(vecs.sem, vecs.value("neg"))
                v.wait_ge(act.sem, act.value("ln"))
                nc.vector.tensor_tensor(soft[:], b[:], soft[:], ALU.subtract).then_inc(
                    vecs.step("log"), 1)
                v.wait_ge(vecs.sem, vecs.value("log"))
                v.wait_ge(c.steps["dma"], d0 + 32)
                nc.vector.tensor_tensor_scan(b[:], restart[:], soft[:], 0.0,
                                             ALU.mult, ALU.add).then_inc(vecs.step("sum"), 1)
                v.wait_ge(vecs.sem, vecs.value("sum"))
                chunks = b[:].rearrange("p (n m) -> p n m", m=CH)
                nc.vector.tensor_tensor(
 k_tail[:].rearrange("p (n m) -> p n m", m=CH),
 chunks[:, :, CH - 1:CH].broadcast_to([P, S // CH, CH]), chunks, ALU.subtract).then_inc(
                    vecs.step("to_end"), 1)
                v.wait_ge(act.sem, act.value("grow"))
                nc.vector.tensor_copy(
   ends[:], q_in[:].rearrange("p (n m) -> p n m", m=CH)[:, :, CH - 1]).then_inc(
                    vecs.step("ends"), 1)
                v.wait_ge(vecs.sem, vecs.value("ends"))
                nc.vector.scalar_tensor_tensor(q_in[:], q_in[:], GDK ** -0.5,
                                               proj[:, 0, :], ALU.mult, ALU.mult).then_inc(
                    vecs.step("q_in"), 1)
                v.wait_ge(act.sem, act.value("shrink"))
                nc.vector.tensor_tensor(k_in[:], k_in[:], proj[:, 1, :], ALU.mult).then_inc(
                    vecs.step("k_in"), 1)
                v.wait_ge(act.sem, act.value("tail"))
                nc.vector.tensor_tensor(k_tail[:], k_tail[:], proj[:, 1, :],
                                        ALU.mult).then_inc(vecs.step("k_tail"), 1)
        for s in (act, vecs, pes):
            s.end()


def gated_linear_chunks(nc, c, t, q_in, k_in, k_tail, ends, v_tok, o_tok):
    with ExitStack() as ctx:
        def sb(name, *shape):
            return c.sb("gla_" + name, [P, *shape], ctx=ctx)
        masks = sb("masks", P + 256)
        qb, kb, tb, vb = sb("q_block", P), sb("k_block", P), sb("tail_block", P), sb("v_block", 256)
        attn, tail_tok, added = sb("attention", HEADS, P), sb("tail_tokens", P), sb("added", 256)
        state = sb("state", 2, 256)
        act = Steps(c, "act", ["q", "v", "out"])
        vecs = Steps(c, "vec", ["k", "tail", "attn", "tail_tok", "added0", "state0", "added1",
                                "state1"])
        pes = Steps(c, "pe", ["attn", "turned", "kv0", "kv1", "read0", "read1", "out"])
        d0 = c.base["dma"]
        c.base["dma"] += 16
        z0 = c.base["pool"]
        c.base["pool"] += 1
        ps = c.psum
        with nc.Block() as block:
            @block.sync
            def _(sp):
                sp.dma_start(masks[:], t["gla_masks"]).then_inc(c.steps["dma"], 16)

            @block.gpsimd
            def _(g):
                nc.gpsimd.memset(state[:], 0.0).then_inc(c.steps["pool"], 1)

            @block.scalar
            def _(a):
                with a.Fori(0, BLK) as i:
                    a.wait_ge(pes.sem, pes.value_before("out", i))
                    nc.scalar.copy(qb[:], q_in[:, bass.ds(i * P, P)]).then_inc(act.step("q"), 1)
                    nc.scalar.copy(vb[:], v_tok[:, bass.ds(i, 1), :].rearrange(
           "p b n -> p (b n)")).then_inc(act.step("v"), 1)
                    a.wait_ge(pes.sem, pes.value("out", i=i))
                    nc.scalar.copy(o_tok[:, bass.ds(i, 1), :].rearrange(
         "p b n -> p (b n)"), ps[:, 7, 0:256]).then_inc(act.step("out"), 1)

            @block.vector
            def _(v):
                v.wait_ge(c.steps["dma"], d0 + 16)
                v.wait_ge(c.steps["pool"], z0 + 1)
                with v.Fori(0, BLK) as i:
                    v.wait_ge(pes.sem, pes.value_before("turned", i))
                    nc.vector.tensor_copy(kb[:], k_in[:, bass.ds(i * P, P)]).then_inc(
                        vecs.step("k"), 1)
                    nc.vector.tensor_copy(tb[:], k_tail[:, bass.ds(i * P, P)]).then_inc(
                        vecs.step("tail"), 1)
                    v.wait_ge(pes.sem, pes.value("attn", i=i))
                    v.wait_ge(pes.sem, pes.value_before("out", i))
                    nc.vector.tensor_tensor(
       attn[:], ps[:, 0:4, 0:P], over_heads(masks[:, 0:P]), ALU.mult).then_inc(vecs.step("attn"), 1)
                    v.wait_ge(pes.sem, pes.value("turned", i=i))
                    nc.vector.tensor_copy(tail_tok[:], ps[:, 4, 0:P]).then_inc(
                        vecs.step("tail_tok"), 1)
                    for j in range(2):
                        v.wait_ge(pes.sem, pes.value(f"kv{j}", i=i))
                        if j:
                            v.wait_ge(vecs.sem, vecs.value("state0", i=i))
                        nc.vector.tensor_tensor(
      added[:], ps[:, 5 + j, 0:256], masks[:, P:], ALU.mult).then_inc(vecs.step(f"added{j}"), 1)
                        v.wait_ge(vecs.sem, vecs.value(f"added{j}", i=i))
                        if j:
                            v.wait_ge(pes.sem, pes.value("read0", i=i))
                        nc.vector.scalar_tensor_tensor(
      state[:, 1 - j, :], state[:, j, :], ends[:, bass.ds(2 * i + j, 1)],
      added[:], ALU.mult, ALU.add).then_inc(vecs.step(f"state{j}"), 1)

            @block.tensor
            def _(p):
                p.wait_ge(c.steps["pool"], z0 + 1)
                with p.Fori(0, BLK) as i:
                    mm = nc.tensor.matmul
                    p.wait_ge(act.sem, act.value("q", i=i))
                    p.wait_ge(vecs.sem, vecs.value("k", i=i))
                    for h in range(HEADS):
                        r = slice(32 * h, 32 * h + 32)
                        last = mm(ps[:, h, 0:P], kb[r, :], qb[r, :], start=True, stop=True)
                    last.then_inc(pes.step("attn"), 1)
                    p.wait_ge(vecs.sem, vecs.value("tail", i=i))
                    nc.tensor.transpose(ps[:, 4, 0:P], tb[:], c.ident[:]).then_inc(
                        pes.step("turned"), 1)
                    p.wait_ge(vecs.sem, vecs.value("tail_tok", i=i))
                    p.wait_ge(act.sem, act.value("v", i=i))
                    for j in range(2):
                        r = slice(CH * j, CH * j + CH)
                        mm(ps[:, 5 + j, 0:256], tail_tok[r, :], vb[r, :],
                           start=True, stop=True).then_inc(pes.step(f"kv{j}"), 1)
                    p.wait_ge(act.sem, act.value_before("out", i))
                    p.wait_ge(vecs.sem, vecs.value_before("state1", i))
                    for j in range(2):
                        r = slice(CH * j, CH * j + CH)
                        if j:
                            p.wait_ge(vecs.sem, vecs.value("state0", i=i))
                        mm(ps[r, 7, 0:256], qb[:, r], state[:, j, :],
                           start=True, stop=False, skip_group_check=True).then_inc(
                            pes.step(f"read{j}"), 1)
                    p.wait_ge(vecs.sem, vecs.value("attn", i=i))
                    for h in range(HEADS):
                        to = slice(64 * h, 64 * h + 64)
                        last = mm(ps[:, 7, to], attn[:, h, :], vb[:, to], start=False,
                                  stop=(h == HEADS - 1), skip_group_check=True)
                    last.then_inc(pes.step("out"), 1)
        for s in (act, vecs, pes):
            s.end(BLK)


def latent_attention(nc, c, t, hidden, small):
    with ExitStack() as ctx:
        o_tok = c.sb("mla_out_tokens", [P, BLK, 256], ctx=ctx)
        v_tok = c.sb("mla_value_tokens", [P, BLK, 256], ctx=ctx)
        q, k = (c.sb(n, [P, HEADS, S], ctx=ctx) for n in ("mla_q", "mla_k"))
        with ExitStack() as inner:
            latent = c.sb("mla_latent", [P, 3, S], ctx=inner)
            project(nc, c, t["w_in"], 10, 3, hidden, latent)
            latent_inputs(nc, c, t, latent, small, q, k, v_tok)
        attend(nc, c, t, 0, 96, q, k, v_tok, o_tok)
        tokens_to_channels(nc, c, o_tok, t["branch"][1])


def latent_inputs(nc, c, t, latent, small, q, k, v_tok):
    with ExitStack() as ctx:
        sq = c.sb("mla_squares", [P, 3, S], ctx=ctx)
        root = c.sb("mla_norms", [P, 2, S], ctx=ctx)
        rope = c.sb("mla_rope", [P, S], ctx=ctx)
        part = c.sb("mla_rotated", [P, 3, S], ctx=ctx)
        w_q = c.sb("mla_w_q", [P, 2, HEADS * P], ctx=ctx)
        w_kv = c.sb("mla_w_kv", [P, 512], ctx=ctx)
        act = Steps(c, "act", [("square", 3), ("root", 2), ("k", HEADS), ("plain", HEADS),
                               ("k_pe", HEADS)])
        vecs = Steps(c, "vec", ["pe_cos", "pe_sin", "pe", ("rstd", 2), ("unit", 3),
                                (("cos", "sin", "rot"), HEADS), ("v", 4)])
        pes = Steps(c, "pe", [("sums", 2), ("k", 2), ("q", HEADS), ("v", 4)])
        d0 = c.base["dma"]
        c.base["dma"] += 48
        cosr, sinr = slice(64, 96), slice(96, 128)
        scale = (DH + ROPE) ** -0.5
        with nc.Block() as block:
            @block.sync
            def _(sp):
                for dst, src in ((rope[:], t["rope"]), (w_q[:], t["mla_w_q"]),
                                 (w_kv[:], t["mla_w_kv"])):
                    sp.dma_start(dst, src).then_inc(c.steps["dma"], 16)

            @block.scalar
            def _(a):
                for n in range(3):
                    nc.scalar.activation(sq[:, n, :], latent[:, n, :], ACT.Square).then_inc(
                        act.step("square"), 1)
                for n in range(2):
                    a.wait_ge(pes.sem, pes.value("sums", n))
                    nc.scalar.activation(root[:, n, :], c.banks(2 * n), ACT.Sqrt,
                                         scale=1.0 / (256 if n == 0 else 128),
                                         bias=c.eps[:, 0:1]).then_inc(act.step("root"), 1)
                for h in range(HEADS):
                    a.wait_ge(pes.sem, pes.value("k", h // 2))
                    r = slice(64 * (h % 2), 64 * (h % 2) + 64)
                    nc.scalar.copy(k[0:64, h, :], c.banks(4 + 2 * (h // 2))[r, :]).then_inc(
                        act.step("k"), 1)
                for h in range(HEADS):
                    a.wait_ge(pes.sem, pes.value("q", h))
                    nc.scalar.mul(q[0:64, h, :], c.banks(2 * (h % 2))[0:64, :],
                                   scale).then_inc(act.step("plain"), 1)
                a.wait_ge(vecs.sem, vecs.value("pe"))
                for h in range(HEADS):
                    nc.scalar.copy(k[cosr, h, :], part[cosr, 0, :]).then_inc(act.step("k_pe"), 1)

            @block.vector
            def _(v):
                mult = lambda out, x, y: nc.vector.tensor_tensor(out, x, y, ALU.mult)
                v.wait_ge(c.steps["dma"], d0 + 48)
                mult(part[cosr, 0, :], small[cosr, 0, :], rope[cosr, :]).then_inc(
                    vecs.step("pe_cos"), 1)
                mult(part[cosr, 1, :], small[sinr, 0, :], rope[sinr, :]).then_inc(
                    vecs.step("pe_sin"), 1)
                v.wait_ge(vecs.sem, vecs.value("pe_sin"))
                nc.vector.tensor_tensor(part[cosr, 0, :], part[cosr, 0, :],
                                        part[cosr, 1, :], ALU.add).then_inc(vecs.step("pe"), 1)
                for n in range(2):
                    v.wait_ge(act.sem, act.value("root", n))
                    nc.vector.reciprocal(root[:, n, :], root[:, n, :]).then_inc(
                        vecs.step("rstd"), 1)
                v.wait_ge(vecs.sem, vecs.value("rstd"))
                for n in range(3):
                    gain = vec(c, "mla_q_norm", n) if n < 2 else vec(c, "mla_kv_norm")
                    nc.vector.scalar_tensor_tensor(
       latent[:, n, :], latent[:, n, :], gain, root[:, n // 2, :], ALU.mult,
       ALU.mult).then_inc(vecs.step("unit"), 1)
                for h in range(HEADS):
                    v.wait_ge(pes.sem, pes.value("q", h))
                    b = c.banks(2 * (h % 2))
                    nc.vector.scalar_tensor_tensor(
        q[cosr, h, :], b[cosr, :], scale, rope[cosr, :], ALU.mult, ALU.mult).then_inc(
                        vecs.step("cos"), 1)
                    if h:
                        v.wait_ge(vecs.sem, vecs.value("rot", h - 1))
                    nc.vector.scalar_tensor_tensor(
        part[cosr, 2, :], b[sinr, :], scale, rope[sinr, :], ALU.mult, ALU.mult).then_inc(
                        vecs.step("sin"), 1)
                    v.wait_ge(vecs.sem, vecs.value("sin", h))
                    nc.vector.tensor_tensor(q[cosr, h, :], q[cosr, h, :],
                                            part[cosr, 2, :], ALU.add).then_inc(vecs.step("rot"), 1)
                for g in range(4):
                    v.wait_ge(pes.sem, pes.value("v", g))
                    nc.vector.tensor_copy(
          v_tok[:, 2 * g:2 * g + 2, :].rearrange("p b n -> p (b n)"), c.psum[:, g, :]).then_inc(
                        vecs.step("v"), 1)

            @block.tensor
            def _(p):
                mm = nc.tensor.matmul
                p.wait_ge(act.sem, act.value("square"))
                for h in range(NH):
                    cols = slice(h * HALF, (h + 1) * HALF)
                    for n in range(2):
                        last = mm(c.psum[:, h, :], c.ones[:], sq[:, n, cols], start=(n == 0),
                                  stop=(n == 1))
                last.then_inc(pes.step("sums"), 1)
                for h in range(NH):
                    last = mm(c.psum[:, 2 + h, :], c.ones[:], sq[:, 2, h * HALF:(h + 1) * HALF],
                              start=True, stop=True)
                last.then_inc(pes.step("sums"), 1)
                p.wait_ge(vecs.sem, vecs.value("unit"))
                p.wait_ge(c.steps["dma"], d0 + 48)
                for n in range(2):
                    for x in range(NH):
                        last = mm(c.psum[:, 4 + 2 * n + x, :], w_kv[:, n * P:(n + 1) * P],
                                  latent[:, 2, x * HALF:(x + 1) * HALF], start=True, stop=True)
                    last.then_inc(pes.step("k"), 1)
                for h in range(HEADS):
                    if h >= 2:
                        p.wait_ge(act.sem, act.value("plain", h - 2))
                        p.wait_ge(vecs.sem, vecs.value("sin", h - 2))
                    for x in range(NH):
                        for n in range(2):
                            last = mm(c.psum[:, 2 * (h % 2) + x, :], w_q[:, n, h * P:(h + 1) * P],
                                      latent[:, n, x * HALF:(x + 1) * HALF], start=(n == 0),
                                      stop=(n == 1))
                    last.then_inc(pes.step("q"), 1)
                p.wait_ge(act.sem, act.value("plain"))
                p.wait_ge(vecs.sem, vecs.value("sin"))
                for g in range(4):
                    for q2 in range(2):
                        b = 2 * g + q2
                        last = mm(c.psum[:, g, q2 * 256:(q2 + 1) * 256],
                                  latent[:, 2, b * P:(b + 1) * P], w_kv[:, 256:512], start=True,
                                  stop=True)
                    last.then_inc(pes.step("v"), 1)
        for s in (act, vecs, pes):
            s.end()


def forgetting_attention(nc, c, t, hidden, small):
    with ExitStack() as ctx:
        o_tok = c.sb("fox_out_tokens", [P, BLK, 256], ctx=ctx)
        v_tok = c.sb("fox_value_tokens", [P, BLK, 256], ctx=ctx)
        q, k = (c.sb(n, [P, HEADS, S], ctx=ctx) for n in ("fox_q", "fox_k"))
        with ExitStack() as inner:
            proj = c.sb("fox_projected", [P, 6, S], ctx=inner)
            project(nc, c, t["w_in"], 19, 6, hidden, proj, (t["w_gate"], 0, WK))
            channels_to_tokens(nc, c, proj[:, 4:6, :], v_tok)
            forgetting_inputs(nc, c, proj, small, q, k)
        attend(nc, c, t, 1, 97, q, k, v_tok, o_tok)
        tokens_to_channels(nc, c, o_tok, t["branch"][3])


def forgetting_inputs(nc, c, proj, small, q, k):
    with ExitStack() as ctx:
        soft = c.sb("fox_softplus", [P, S], ctx=ctx)
        ones = c.sb("fox_ones", [P, S], ctx=ctx)
        total = c.sb("fox_forget_sum", [P, S], ctx=ctx)
        act = Steps(c, "act", ["abs", "exp", "ln", ("q", HEADS), ("k", HEADS), ("f_q", HEADS),
                               ("f_k", HEADS)])
        vecs = Steps(c, "vec", ["neg", "log", "sum"])
        pool = Steps(c, "pool", ["ones", "q_zero", "k_zero", "q_one", "k_one"])
        f, bias = small[:, 1, :], vec(c, "fox_f_bias")
        with nc.Block() as block:
            @block.gpsimd
            def _(g):
                nc.gpsimd.memset(ones[:], 1.0).then_inc(pool.step("ones"), 1)
                g.wait_ge(pool.sem, pool.value("ones"))
                nc.gpsimd.memset(q[64:97, :, :], 0.0).then_inc(pool.step("q_zero"), 1)
                g.wait_ge(pool.sem, pool.value("q_zero"))
                nc.gpsimd.memset(k[64:97, :, :], 0.0).then_inc(pool.step("k_zero"), 1)
                g.wait_ge(pool.sem, pool.value("k_zero"))
                nc.gpsimd.memset(q[96:97, :, :], 1.0).then_inc(pool.step("q_one"), 1)
                g.wait_ge(pool.sem, pool.value("q_one"))
                nc.gpsimd.memset(k[64:65, :, :], 1.0).then_inc(pool.step("k_one"), 1)

            @block.scalar
            def _(a):
                nc.scalar.activation(soft[:], f, ACT.Abs, bias=bias).then_inc(act.step("abs"), 1)
                a.wait_ge(act.sem, act.value("abs"))
                nc.scalar.activation(soft[:], soft[:], ACT.Exp, scale=-1.0).then_inc(
                    act.step("exp"), 1)
                a.wait_ge(act.sem, act.value("exp"))
                nc.scalar.activation(soft[:], soft[:], ACT.Ln, bias=1.0).then_inc(act.step("ln"), 1)
                for h in range(HEADS):
                    r = slice(64 * (h % 2), 64 * (h % 2) + 64)
                    nc.scalar.mul(q[0:64, h, :], proj[r, h // 2, :], DH ** -0.5).then_inc(
                        act.step("q"), 1)
                for h in range(HEADS):
                    r = slice(64 * (h % 2), 64 * (h % 2) + 64)
                    nc.scalar.copy(k[0:64, h, :], proj[r, 2 + h // 2, :]).then_inc(act.step("k"), 1)
                a.wait_ge(vecs.sem, vecs.value("sum"))
                a.wait_ge(pool.sem, pool.value("k_one"))
                for h in range(HEADS):
                    nc.scalar.copy(q[64:65, h, :], total[32 * h:32 * h + 1, :]).then_inc(
                        act.step("f_q"), 1)
                for h in range(HEADS):
                    nc.scalar.mul(k[96:97, h, :], total[32 * h:32 * h + 1, :], -1.0).then_inc(
                        act.step("f_k"), 1)

            @block.vector
            def _(v):
                nc.vector.tensor_scalar(total[:], f, bias, 0.0, ALU.add, ALU.min).then_inc(
                    vecs.step("neg"), 1)
                v.wait_ge(vecs.sem, vecs.value("neg"))
                v.wait_ge(act.sem, act.value("ln"))
                nc.vector.tensor_tensor(soft[:], total[:], soft[:], ALU.subtract).then_inc(
                    vecs.step("log"), 1)
                v.wait_ge(vecs.sem, vecs.value("log"))
                v.wait_ge(pool.sem, pool.value("ones"))
                nc.vector.tensor_tensor_scan(total[:], ones[:], soft[:], 0.0,
                                             ALU.mult, ALU.add).then_inc(vecs.step("sum"), 1)
        for s in (act, vecs, pool):
            s.end()


def attend(nc, c, t, which_mask, rows, q, k, v_tok, o_tok):
    with ExitStack() as ctx:
        mask = c.sb("attention_mask", [P, P], ctx=ctx)
        prob = c.sb("attention_probs", [P, 2, S], ctx=ctx)
        turned = c.sb("attention_probs_turned", [P, 2, S], ctx=ctx)
        neg_max = c.sb("attention_neg_max", [P, 2], ctx=ctx)
        sums = c.sb("attention_sums", [P, BLK * HEADS], ctx=ctx)
        turns = range(BLK * HEADS)
        last_turn = turns[-1]
        pe_spec, act_spec, vec_spec = ["scores0"], [], []
        for n in range(len(turns) + 1):
            if n < last_turn:
                pe_spec.append(f"scores{n + 1}")
            if n <= last_turn:
                pe_spec.append(f"turned{n}")
                act_spec += [f"exp{n}", f"low{n}"]
                vec_spec += [f"mask{n}", f"max{n}"]
                if n // 4 >= 4:
                    vec_spec.append(f"high{n}")
            if n:
                pe_spec.append(f"values{n - 1}")
                if n % 4 == 0:
                    vec_spec += [f"inverse{n // 4 - 1}", f"out{n // 4 - 1}"]
        pes, act = Steps(c, "pe", pe_spec), Steps(c, "act", act_spec)
        vecs = Steps(c, "vec", vec_spec)
        d0 = c.base["dma"]
        c.base["dma"] += 16

        def scores(n, keys):
            return c.banks(2 * (n % 2))[:, keys]

        with nc.Block() as block:
            @block.sync
            def _(sp):
                sp.dma_start(mask[:], t["attention_masks"][:, which_mask, :]).then_inc(
                    c.steps["dma"], 16)

            @block.scalar
            def _(a):
                for n in turns:
                    nk = (n // 4 + 1) * P
                    a.wait_ge(vecs.sem, vecs.value(f"max{n}"))
                    if n >= 2:
                        a.wait_ge(pes.sem, pes.value(f"turned{n - 2}"))
                    nc.scalar.activation(
     prob[:, n % 2, 0:nk], scores(n, slice(0, nk)), ACT.Exp,
     bias=neg_max[:, n % 2:n % 2 + 1], accum_out=sums[:, n:n + 1]).then_inc(act.step(f"exp{n}"), 1)
                    a.wait_ge(pes.sem, pes.value(f"turned{n}"))
                    if n >= 2:
                        a.wait_ge(pes.sem, pes.value(f"values{n - 2}"))
                    m = min(nk, HALF)
                    nc.scalar.copy(turned[:, n % 2, 0:m], c.psum[:, 4, 0:m]).then_inc(
                        act.step(f"low{n}"), 1)

            @block.vector
            def _(v):
                v.wait_ge(c.steps["dma"], d0 + 16)

                def finish(b):
                    s = slice(4 * b, 4 * b + 4)
                    v.wait_ge(act.sem, act.value(f"exp{4 * b + 3}"))
                    nc.vector.reciprocal(sums[:, s], sums[:, s]).then_inc(
                        vecs.step(f"inverse{b}"), 1)
                    v.wait_ge(pes.sem, pes.value(f"values{4 * b + 3}"))
                    v.wait_ge(vecs.sem, vecs.value(f"inverse{b}"))
                    nc.vector.tensor_tensor(
    heads(o_tok[:, b, :]), heads(c.psum[:, 6 + b % 2, 0:256]),
    bcast(sums[:, s], DH), ALU.mult).then_inc(vecs.step(f"out{b}"), 1)

                for n in turns:
                    nk = (n // 4 + 1) * P
                    v.wait_ge(pes.sem, pes.value(f"scores{n}"))
                    own = scores(n, slice(nk - P, nk))
                    nc.vector.tensor_tensor(own, own, mask[:], ALU.add).then_inc(
                        vecs.step(f"mask{n}"), 1)
                    v.wait_ge(vecs.sem, vecs.value(f"mask{n}"))
                    if n >= 2:
                        v.wait_ge(act.sem, act.value(f"exp{n - 2}"))
                    nc.vector.tensor_reduce(
    neg_max[:, n % 2:n % 2 + 1], scores(n, slice(0, nk)), AX_X, ALU.max,
    negate=True).then_inc(vecs.step(f"max{n}"), 1)
                    if n // 4 >= 4:
                        v.wait_ge(pes.sem, pes.value(f"turned{n}"))
                        if n >= 2:
                            v.wait_ge(pes.sem, pes.value(f"values{n - 2}"))
                        nc.vector.tensor_copy(
       turned[:, n % 2, HALF:nk], c.psum[:, 5, 0:nk - HALF]).then_inc(vecs.step(f"high{n}"), 1)
                    if n and n % 4 == 0:
                        finish(n // 4 - 1)
                finish(BLK - 1)

            @block.tensor
            def _(p):
                mm = nc.tensor.matmul

                def score(n):
                    b, h = n // 4, n % 4
                    if n >= 2:
                        p.wait_ge(act.sem, act.value(f"exp{n - 2}"))
                    for x in range(0, (b + 1) * P, HALF):
                        m = min(HALF, (b + 1) * P - x)
                        last = mm(c.psum[:, 2 * (n % 2) + x // HALF, 0:m],
                                  q[0:rows, h, b * P:(b + 1) * P], k[0:rows, h, x:x + m],
                                  start=True, stop=True)
                    last.then_inc(pes.step(f"scores{n}"), 1)

                score(0)
                for n in range(len(turns) + 1):
                    if n < last_turn:
                        score(n + 1)
                    if n <= last_turn:
                        p.wait_ge(act.sem, act.value(f"exp{n}"))
                        if n:
                            p.wait_ge(act.sem, act.value(f"low{n - 1}"))
                            if (n - 1) // 4 >= 4:
                                p.wait_ge(vecs.sem, vecs.value(f"high{n - 1}"))
                        for x in range(n // 4 + 1):
                            last = nc.tensor.transpose(
                                c.psum[:, 4 + x // 4, x % 4 * P:(x % 4 + 1) * P],
                                prob[:, n % 2, x * P:(x + 1) * P], c.ident[:])
                        last.then_inc(pes.step(f"turned{n}"), 1)
                    if n:
                        m = n - 1
                        b, h = m // 4, m % 4
                        p.wait_ge(act.sem, act.value(f"low{m}"))
                        if b >= 4:
                            p.wait_ge(vecs.sem, vecs.value(f"high{m}"))
                        if b >= 2 and h == 0:
                            p.wait_ge(vecs.sem, vecs.value(f"out{b - 2}"))
                        for x in range(b + 1):
                            last = mm(c.psum[:, 6 + b % 2, 64 * h:64 * h + 64],
                                      turned[:, m % 2, x * P:(x + 1) * P],
                                      v_tok[:, x, 64 * h:64 * h + 64], start=(x == 0),
                                      stop=(x == b))
                        last.then_inc(pes.step(f"values{m}"), 1)
        for s in (act, vecs, pes):
            s.end()


def gate_and_merge(nc, c, t, hidden, merged):
    with ExitStack() as ctx:
        o = c.sb("branches", [P, 8, 2, S], F32R, ctx=ctx)
        with ExitStack() as inner:
            plain = c.sb("branch_plain", [P, 2, S], ctx=inner)
            act, vecs = Steps(c, "act", [("high", 4)]), Steps(c, "vec", [("low", 4)])
            d0 = c.base["dma"]
            c.base["dma"] += 64
            with nc.Block() as block:
                @block.sync
                def _(sp):
                    for i in range(4):
                        if i:
                            sp.wait_ge(vecs.sem, vecs.value("low", i - 1))
                        sp.dma_start(plain[:], t["branch"][i]).then_inc(c.steps["dma"], 16)

                @block.scalar
                def _(a):
                    for i in range(4):
                        a.wait_ge(c.steps["dma"], d0 + 16 * i + 16)
                        nc.scalar.copy(o[:, 2 * i:2 * i + 2, 0, :], plain[:]).then_inc(
                            act.step("high"), 1)

                @block.vector
                def _(v):
                    for i in range(4):
                        v.wait_ge(act.sem, act.value("high", i))
                        nc.vector.tensor_tensor(
            o[:, 2 * i:2 * i + 2, 1, :], plain[:],
            o[:, 2 * i:2 * i + 2, 0, :].bitcast(F32), ALU.subtract).then_inc(vecs.step("low"), 1)
            act.end()
            vecs.end()
        gate = c.sb("gate", [P, 2, S], ctx=ctx)
        start = VECTORS["b_gate"][0]

        def sigmoid(act, u, s, result, act_count, dve_count, q, j):
            if not isinstance(u, int) or u >= 2:
                act.wait_ge(c.dve_done, dve_count(u - 2, 1))
            nc.scalar.activation(gate[:, s, :], result, ACT.Sigmoid,
                                 bias=c.vectors[:, bass.ds(u + start, 1)]).then_inc(c.act_done, 1)

        def add(dve, u, s, result, act_count, dve_count, q, j):
            dve.wait_ge(c.act_done, act_count(u))
            out = merged[:, bass.ds(j, 1), :].rearrange("p a n -> p (a n)")
            to = gate[:, s, :] if q else out
            nc.vector.tensor_tensor(to, gate[:, s, :], c.banks(4 + 2 * s),
                                    ALU.mult).then_inc(c.dve_done, 1 if q else 2)
            if q:
                dve.wait_ge(c.dve_done, dve_count(u))
                nc.vector.tensor_tensor(out, out, gate[:, s, :], ALU.add).then_inc(c.dve_done, 1)

        gemm(nc, c, t["w_gate"], 32, KT, lambda k, x, h: hidden[:, k, x, h * HALF:(h + 1) * HALF],
             act_per_unit=1, act_epilogue=sigmoid, dve_per_unit=2, dve_epilogue=add,
             banks_read_by="dve", unroll=4, extra_kt=2, then=(t["w_out"], 0, KT),
             extra_rhs=lambda k, x, h, i: o[:, 2 * i + k, x, h * HALF:(h + 1) * HALF])


def split(nc, c, src, dst):
    n = src.shape[1]
    act, vecs = Steps(c, "act", [("high", n)]), Steps(c, "vec", [("low", n)])
    with nc.Block() as block:
        @block.scalar
        def _(a):
            for k in range(n):
                nc.scalar.copy(dst[:, k, 0, :], src[:, k, :]).then_inc(act.step("high"), 1)

        @block.vector
        def _(v):
            for k in range(n):
                v.wait_ge(act.sem, act.value("high", k))
                nc.vector.tensor_tensor(dst[:, k, 1, :], src[:, k, :],
                                        dst[:, k, 0, :].bitcast(F32), ALU.subtract).then_inc(
                    vecs.step("low"), 1)
    act.end()
    vecs.end()


def one(tile, u):
    return tile[:, bass.ds(u, 1), :].rearrange("p a n -> p (a n)")


def sum_squares(nc, c, y, sq, total, add):
    def square(act, u, s, result, act_count, dve_count, q, j):
        if not isinstance(u, int) or u >= 2:
            act.wait_ge(c.dve_done, dve_count(u - 2, 1))
        act.wait_ge(c.dve_done, dve_count(u, 0))
        nc.scalar.activation(sq[:, s, :], one(y, u), ACT.Square).then_inc(c.act_done, 1)

    def keep(dve, u, s, result, act_count, dve_count, q, j):
        if add:
            nc.vector.tensor_tensor(one(y, u), one(y, u), result, ALU.add).then_inc(c.dve_done, 1)
        else:
            nc.vector.tensor_copy(one(y, u), result).then_inc(c.dve_done, 1)
        dve.wait_ge(c.act_done, act_count(u))
        if not isinstance(u, int) or u:
            dve.wait_ge(c.dve_done, dve_count(u - 1, 1))
        nc.vector.tensor_tensor(total[:], total[:], sq[:, s, :], ALU.add).then_inc(c.dve_done, 1)
    return dict(act_per_unit=1, act_epilogue=square, dve_per_unit=2, dve_epilogue=keep,
                banks_read_by="dve")


def clear(nc, c, tile):
    vecs = Steps(c, "vec", ["zero"])
    with nc.Block() as block:
        @block.vector
        def _(v):
            nc.vector.memset(tile, 0.0).then_inc(vecs.step("zero"), 1)
    vecs.end()


def add_residual(nc, c, t, y, total, factor, x_tokens, x_dram, keep_dram, out=None, times=None,
                 plus=None, final=False, defer=False, loaded=None):
    with ExitStack() as ctx:
        x = loaded or c.sb("residual_in", [P, KT, S], ctx=ctx)
        sq = c.sb("residual_squares", [P, 2, S], ctx=ctx)
        rstd = c.sb("residual_rstd", [P, 2, S], ctx=ctx)
        normed = c.sb("residual_normed", [P, 2, S], ctx=ctx)
        if final:
            tail = [("normed", KT)]
        elif defer:
            tail = []
        else:
            tail = ["normed0"] + [f"{n}" for k in range(1, KT)
                                  for n in (f"normed{k}", f"low{k - 1}")] + [f"low{KT - 1}"]
        where = total[:] if defer else rstd[:, 1, :]
        post = total is not None
        rows_base = list(c.slots)
        act = Steps(c, "act", (["root1"] if post else [])
                    + [(("square", "high") if defer else "square", KT), "root2"]
                    + ([("rows", BLK)] if final else [] if defer else [("high", KT)]))
        if post:
            adds = sum([[f"scaled{k}"] + ([f"added{k - 1}"] if k else [])
                        + ([f"low{k - 2}"] if defer and k > 1 else []) for k in range(KT)], [])
            adds += [f"added{KT - 1}"] + ([f"low{KT - 2}", f"low{KT - 1}"] if defer else [])
        else:
            adds = [f"added{k}" for k in range(KT)]
        vecs = Steps(c, "vec", (["rstd1"] if post else []) + adds + ["rstd2"] + tail)
        turns = KT if x_tokens is not None else 0
        order = sum([([f"turned{k}"] if k < turns else []) + ([f"sum2{k - 3}"] if k > 2 else [])
                     for k in range(KT + 3)], [])
        pes = Steps(c, "pe", (["sum1"] if post else []) + order
                    + ([("rows", BLK)] if final else []))
        ps = c.psum
        with nc.Block() as block:
            @block.sync
            def _(sp):
                if loaded is None:
                    load_residual(c, sp, x, x_dram if x_tokens is None else x_tokens,
                                  x_tokens is not None)
                if keep_dram is not None:
                    sp.wait_ge(vecs.sem, vecs.value(f"added{KT - 1}"))
                    store(c, sp, keep_dram, y[:])
                    sp.wait_ge(c.scratch_stored, c.stored)
                if final:
                    for b in range(BLK):
                        sp.wait_ge(act.sem, act.value("rows", b))
                        store_slot(c, sp, t["out"][b * P:(b + 1) * P, :], sq[:, b % 2, :], b % 2)
                    wait_slots(c, sp)

            @block.scalar
            def _(a):
                def root(name, bank, to):
                    nc.scalar.activation(to, c.banks(bank), ACT.Sqrt,
                                         scale=1.0 / D, bias=c.eps[:, 0:1]).then_inc(
                        act.step(name), 1)
                if post:
                    a.wait_ge(pes.sem, pes.value("sum1"))
                    root("root1", 0, rstd[:, 0, :])
                for k in range(KT):
                    a.wait_ge(vecs.sem, vecs.value(f"added{k}"))
                    if k >= 2:
                        a.wait_ge(pes.sem, pes.value(f"sum2{k - 2}"))
                    nc.scalar.activation(sq[:, k % 2, :], y[:, k, :], ACT.Square).then_inc(
                        act.step("square"), 1)
                    if defer:
                        nc.scalar.activation(out[:, k, 0, :], y[:, k, :], ACT.Copy,
                                             scale=times(k)).then_inc(act.step("high"), 1)
                a.wait_ge(pes.sem, pes.value(f"sum2{KT - 1}"))
                root("root2", 6, where)
                if final:
                    for b in range(BLK):
                        a.wait_ge(pes.sem, pes.value("rows", b))
                        if b >= 2:
                            a.wait_ge(c.slot_stored[b % 2], rows_base[b % 2] + 16 * (b // 2))
                        nc.scalar.copy(sq[:, b % 2, :], c.banks(2 * (b % 2))).then_inc(
                            act.step("rows"), 1)
                elif not defer:
                    for k in range(KT):
                        a.wait_ge(vecs.sem, vecs.value(f"normed{k}"))
                        if plus is None:
                            nc.scalar.copy(out[:, k, 0, :], normed[:, k % 2, :]).then_inc(
                                act.step("high"), 1)
                        else:
                            nc.scalar.activation(
                out[:, k, 0, :], normed[:, k % 2, :], ACT.Identity, bias=plus(k)).then_inc(
                                act.step("high"), 1)

            @block.vector
            def _(v):
                if post:
                    v.wait_ge(act.sem, act.value("root1"))
                    nc.vector.reciprocal(rstd[:, 0, :], rstd[:, 0, :]).then_inc(
                        vecs.step("rstd1"), 1)
                    v.wait_ge(vecs.sem, vecs.value("rstd1"))
                stt = nc.vector.scalar_tensor_tensor

                def added(k):
                    v.wait_ge(vecs.sem, vecs.value(f"scaled{k}"))
                    if x_tokens is not None:
                        v.wait_ge(pes.sem, pes.value(f"turned{k}"))
                        other = c.banks(2 + 2 * (k % 2))
                    else:
                        wait_residual(c, v, k)
                        other = x[:, k, :]
                    nc.vector.tensor_tensor(y[:, k, :], y[:, k, :], other,
                                            ALU.add).then_inc(vecs.step(f"added{k}"), 1)

                def low_deferred(k):
                    v.wait_ge(act.sem, act.value("high", k))
                    stt(out[:, k, 1, :], y[:, k, :], times(k),
                        out[:, k, 0, :].bitcast(F32), ALU.mult, ALU.subtract).then_inc(
                        vecs.step(f"low{k}"), 1)
                if post:
                    for k in range(KT + 2):
                        if k < KT:
                            stt(y[:, k, :], y[:, k, :], factor(k),
                                rstd[:, 0, :], ALU.mult, ALU.mult).then_inc(
                                vecs.step(f"scaled{k}"), 1)
                        if 0 < k <= KT:
                            added(k - 1)
                        if defer and k > 1:
                            low_deferred(k - 2)
                else:
                    for k in range(KT):
                        wait_residual(c, v, k)
                        stt(y[:, k, :], y[:, k, :], factor(k), x[:, k, :],
                            ALU.mult, ALU.add).then_inc(vecs.step(f"added{k}"), 1)
                v.wait_ge(act.sem, act.value("root2"))
                nc.vector.reciprocal(where, where).then_inc(vecs.step("rstd2"), 1)
                v.wait_ge(vecs.sem, vecs.value("rstd2"))

                def low(k):
                    v.wait_ge(act.sem, act.value("high", k))
                    high = out[:, k, 0, :].bitcast(F32)
                    if plus is None:
                        nc.vector.tensor_tensor(
        out[:, k, 1, :], normed[:, k % 2, :], high, ALU.subtract).then_inc(vecs.step(f"low{k}"), 1)
                    else:
                        stt(out[:, k, 1, :], normed[:, k % 2, :], plus(k),
                            high, ALU.add, ALU.subtract).then_inc(vecs.step(f"low{k}"), 1)
                for k in range(0 if defer else KT):
                    if final:
                        stt(x[:, k, :], y[:, k, :], times(k), rstd[:, 1, :],
                            ALU.mult, ALU.mult).then_inc(vecs.step("normed"), 1)
                        continue
                    if k >= 2:
                        v.wait_ge(vecs.sem, vecs.value(f"low{k - 2}"))
                    stt(normed[:, k % 2, :], y[:, k, :], times(k),
                        rstd[:, 1, :], ALU.mult, ALU.mult).then_inc(vecs.step(f"normed{k}"), 1)
                    if k:
                        low(k - 1)
                if not final and not defer:
                    low(KT - 1)

            @block.tensor
            def _(p):
                mm = nc.tensor.matmul
                if post:
                    for h in range(NH):
                        last = mm(ps[:, h, :], c.ones[:], total[:, h * HALF:(h + 1) * HALF],
                                  start=True, stop=True)
                    last.then_inc(pes.step("sum1"), 1)

                def turn(k):
                    if k >= 2:
                        p.wait_ge(vecs.sem, vecs.value(f"added{k - 2}"))
                    if k % 4 == 0:
                        wait_residual(c, p, k)
                    for b in range(BLK):
                        last = nc.tensor.transpose(
                            ps[:, 2 + 2 * (k % 2) + b // 4, b % 4 * P:(b % 4 + 1) * P],
                            x[:, b, k * P:(k + 1) * P], c.ident[:])
                    last.then_inc(pes.step(f"turned{k}"), 1)

                def add(k):
                    p.wait_ge(act.sem, act.value("square", k))
                    for h in range(NH):
                        last = mm(ps[:, 6 + h, :], c.ones[:], sq[:, k % 2, h * HALF:(h + 1) * HALF],
                                  start=(k == 0), stop=(k == KT - 1))
                    last.then_inc(pes.step(f"sum2{k}"), 1)
                for k in range(KT + 3):
                    if k < turns:
                        turn(k)
                    if k > 2:
                        add(k - 3)
                if final:
                    p.wait_ge(vecs.sem, vecs.value("normed"))
                    for b in range(BLK):
                        if b >= 2:
                            p.wait_ge(act.sem, act.value("rows", b - 2))
                        for k in range(KT):
                            last = nc.tensor.transpose(
                                ps[:, 2 * (b % 2) + k // 4, k % 4 * P:(k % 4 + 1) * P],
                                x[:, k, b * P:(b + 1) * P], c.ident[:])
                        last.then_inc(pes.step("rows"), 1)
        for s in (act, vecs, pes):
            s.end()


def load_residual(c, sp, x, source, tokens):
    for n in range(2):
        c.residuals[n] += 16
        at = slice(n * HALF, (n + 1) * HALF) if tokens else slice(n * KT // 2, (n + 1) * KT // 2)
        to, src = (x[:, :, at], source[:, :, at]) if tokens else (x[:, at, :], source[:, at, :])
        sp.dma_start(to, src).then_inc(c.residual_loaded[n], 16)


def wait_residual(c, eng, k):
    n = k * 2 // KT
    eng.wait_ge(c.residual_loaded[n], c.residuals[n])


FF_CHUNKS = 4


def mlp(nc, c, t, h, y, total, sq):
    rstd = total[:]
    with ExitStack() as ctx:
        u_parts = c.sb("mlp_hidden", [P, KT, 2, S], F32R, ctx=ctx)

        def relu(dve, u, s, result, act_count, dve_count, q, j):
            nc.vector.scalar_tensor_tensor(sq[:, s, :], result, 0.0, rstd, ALU.max,
                                           ALU.mult).then_inc(c.dve_done, 1)
            dve.wait_ge(c.act_done, act_count(u, 1))
            low, high = (u_parts[:, bass.ds(u, 1), x, :].rearrange("p a n -> p (a n)")
                         for x in (1, 0))
            nc.vector.tensor_tensor(low, sq[:, s, :], high.bitcast(F32),
                                    ALU.subtract).then_inc(c.dve_done, 1)

        def square(act, u, s, result, act_count, dve_count, q, j):
            act.wait_ge(c.dve_done, dve_count(u))
            nc.scalar.activation(sq[:, s, :], sq[:, s, :], ACT.Square).then_inc(c.act_done, 1)
            act.wait_ge(c.act_done, act_count(u))
            nc.scalar.copy(u_parts[:, bass.ds(u, 1), 0, :].rearrange("p a n -> p (a n)"),
                           sq[:, s, :]).then_inc(c.act_done, 1)

        def add(dve, u, s, result, act_count, dve_count, q, j):
            nc.vector.tensor_tensor(one(y, u), one(y, u), result, ALU.add).then_inc(c.dve_done, 1)

        def copy(dve, u, s, result, act_count, dve_count, q, j):
            nc.vector.tensor_copy(one(y, u), result).then_inc(c.dve_done, 1)

        for chunk in range(FF_CHUNKS):
            gemm(nc, c, t["w_mlp_in"], KT, KT, lambda k, x, n: h[:, k, x, n * HALF:(n + 1) * HALF],
                 act_per_unit=2, act_epilogue=square, dve_per_unit=2, dve_epilogue=relu,
                 banks_read_by="dve", first=KT * chunk,
                 then=(t["w_mlp_out"], KT * chunk, KT))
            if chunk < FF_CHUNKS - 1:
                how = dict(dve_per_unit=1, dve_epilogue=add if chunk else copy, banks_read_by="dve")
            else:
                clear(nc, c, total[:])
                how = sum_squares(nc, c, y, sq, total, True)
            gemm(nc, c, t["w_mlp_out"], KT, KT,
                 lambda k, x, n: u_parts[:, k, x, n * HALF:(n + 1) * HALF], first=KT * chunk,
                 then=(t["w_mlp_in"], KT * (chunk + 1), KT) if chunk < FF_CHUNKS - 1
                 else (t["w_in_2"], 0, KT), **how)


def branches(nc, c, t, merged_ctx, modulated):
    with ExitStack() as ctx:
        hidden = c.sb("hidden", [P, KT, 2, S], F32R, ctx=ctx)
        norm_input(nc, c, t, hidden)
        with ExitStack() as inner:
            small = c.sb("small_projections", [P, 2, S], ctx=inner)
            project(nc, c, t["w_in"], 0, 2, hidden, small, (t["w_in"], 2, KT))
            delta_net(nc, c, t, hidden, small, modulated)
            latent_attention(nc, c, t, hidden, small)
            gated_linear(nc, c, t, hidden, small)
            forgetting_attention(nc, c, t, hidden, small)
        merged = c.sb("merged", [P, KT, S], ctx=merged_ctx, side="right")
        gate_and_merge(nc, c, t, hidden, merged)
    return merged


def mix_out(nc, c, t, merged, merged_ctx, y, total, sq, x_ctx):
    with ExitStack() as ctx:
        parts = c.sb("merged_parts", [P, KT, 2, S], F32R, ctx=ctx)
        split(nc, c, merged, parts)
        merged_ctx.close()
        x = c.sb("mlp_residual", [P, KT, S], ctx=x_ctx, side="right")
        with nc.Block() as block:
            @block.sync
            def _(sp):
                load_residual(c, sp, x, t["x"].rearrange("(b p) d -> p b d", p=P), True)
        clear(nc, c, total[:])
        gemm(nc, c, t["w_out"], KT, KT, lambda k, x, n: parts[:, k, x, n * HALF:(n + 1) * HALF],
             then=(t["w_mlp_in"], 0, KT), **sum_squares(nc, c, y, sq, total, False))
    return x


PAD = 3
EXT = S + PAD + CTX
MIX = 4


def context_values(nc, c, t, times, plus, v_ctx):
    with ExitStack() as ctx:
        x = c.sb("ctx_tokens", [P, 2, D], ctx=ctx)
        junk = c.sb("ctx_squares", [P, D], ctx=ctx)
        ss = c.sb("ctx_square_sums", [P, 2], ctx=ctx)
        root = c.sb("ctx_rms", [P, 2], ctx=ctx)
        rstd = c.sb("ctx_rstd", [P, 2], ctx=ctx)
        plain = c.sb("ctx_plain", [P, 2, CTX], ctx=ctx)
        parts = c.sb("ctx_parts", [P, KT, 2, CTX], F32R, ctx=ctx)
        act = Steps(c, "act", [("square", 2), "root", (("plain", "high"), KT)])
        vecs = Steps(c, "vec", ["rstd", ("scaled", 2), ("low", KT)])
        pes = Steps(c, "pe", [("turned", KT)])
        d0 = c.base["dma"]
        c.base["dma"] += 16
        with nc.Block() as block:
            @block.sync
            def _(sp):
                sp.dma_start(x[:], t["ctx"].rearrange("(b p) d -> p b d", p=P)).then_inc(
                    c.steps["dma"], 16)

            @block.scalar
            def _(a):
                a.wait_ge(c.steps["dma"], d0 + 16)
                for b in range(2):
                    if b:
                        a.wait_ge(act.sem, act.value("square", 0))
                    nc.scalar.activation(junk[:], x[:, b, :], ACT.Square,
                                         accum_out=ss[:, b:b + 1]).then_inc(act.step("square"), 1)
                a.wait_ge(act.sem, act.value("square"))
                nc.scalar.activation(root[:], ss[:], ACT.Sqrt, scale=1.0 / D,
                                     bias=c.eps[:, 0:1]).then_inc(act.step("root"), 1)
                for k in range(KT):
                    a.wait_ge(pes.sem, pes.value("turned", k))
                    if k >= 2:
                        a.wait_ge(vecs.sem, vecs.value("low", k - 2))
                    nc.scalar.activation(
       plain[:, k % 2, :], c.psum[:, k % 4, 0:CTX], ACT.Identity,
       scale=times[:, k, 1:2], bias=plus[:, k, 1:2]).then_inc(act.step("plain"), 1)
                    a.wait_ge(act.sem, act.value("plain", k))
                    nc.scalar.copy(parts[:, k, 0, :], plain[:, k % 2, :]).then_inc(
                        act.step("high"), 1)

            @block.vector
            def _(v):
                v.wait_ge(act.sem, act.value("root"))
                nc.vector.reciprocal(rstd[:], root[:]).then_inc(vecs.step("rstd"), 1)
                v.wait_ge(vecs.sem, vecs.value("rstd"))
                for b in range(2):
                    nc.vector.tensor_scalar(x[:, b, :], x[:, b, :],
                                            rstd[:, b:b + 1], None, ALU.mult).then_inc(
                        vecs.step("scaled"), 1)
                for k in range(KT):
                    v.wait_ge(act.sem, act.value("high", k))
                    nc.vector.tensor_tensor(parts[:, k, 1, :], plain[:, k % 2, :],
                                            parts[:, k, 0, :].bitcast(F32),
                                            ALU.subtract).then_inc(vecs.step("low"), 1)

            @block.tensor
            def _(p):
                p.wait_ge(vecs.sem, vecs.value("scaled"))
                for k in range(KT):
                    if k >= 4:
                        p.wait_ge(act.sem, act.value("plain", k - 4))
                    for b in range(2):
                        mm = nc.tensor.transpose(c.psum[:, k % 4, b * P:(b + 1) * P],
                                                 x[:, b, k * P:(k + 1) * P], c.ident[:])
                    mm.then_inc(pes.step("turned"), 1)
        for s in (act, vecs, pes):
            s.end()

        def evacuate(act, u, s, result, act_count, dve_count, q, j):
            nc.scalar.copy(one(v_ctx, u), c.psum[:, 2 * s, 0:CTX]).then_inc(c.act_done, 1)
        gemm(nc, c, t["w_in_2"], MIX, KT, lambda k, x, h: parts[:, k, x, :], act_per_unit=1,
             act_epilogue=evacuate, halves=1, cols=CTX, then=(t["w_in_2"], 0, KT))


def decay_rates(nc, c, rate):
    with ExitStack() as ctx:
        e, s, q, poly, relu = (c.sb("lru_" + n, [P, 8], ctx=ctx)
                               for n in ("exp", "ratio", "ratio_square", "series", "relu"))
        lam = vec(c, "a_lam_2", 0, 8)
        act = Steps(c, "act", ["abs", "exp"])
        terms = [1.0 / n for n in range(15, 0, -2)]
        vecs = Steps(c, "vec", ["plus2", "inverse", "ratio", "square", "first",
                                (("times", "plus"), len(terms) - 1), "odd", "relu", "sum", "rate",
                                "minus"])
        with nc.Block() as block:
            @block.scalar
            def _(a):
                nc.scalar.activation(e[:], lam, ACT.Abs).then_inc(act.step("abs"), 1)
                a.wait_ge(act.sem, act.value("abs"))
                nc.scalar.activation(e[:], e[:], ACT.Exp, scale=-1.0).then_inc(act.step("exp"), 1)

            @block.vector
            def _(v):
                ts, tt = nc.vector.tensor_scalar, nc.vector.tensor_tensor

                def do(name, ins):
                    ins.then_inc(vecs.step(name), 1)
                    v.wait_ge(vecs.sem, vecs.base + (vecs.next or vecs.n))
                v.wait_ge(act.sem, act.value("exp"))
                do("plus2", ts(s[:], e[:], 2.0, None, ALU.add))
                do("inverse", nc.vector.reciprocal(s[:], s[:]))
                do("ratio", tt(s[:], s[:], e[:], ALU.mult))
                do("square", tt(q[:], s[:], s[:], ALU.mult))
                do("first", nc.vector.memset(poly[:], terms[0]))
                for x in terms[1:]:
                    do("times", tt(poly[:], poly[:], q[:], ALU.mult))
                    do("plus", ts(poly[:], poly[:], x, None, ALU.add))
                do("odd", tt(poly[:], poly[:], s[:], ALU.mult))
                do("relu", ts(relu[:], lam, -1.0, 0.0, ALU.mult, ALU.max))
                do("sum", nc.vector.scalar_tensor_tensor(poly[:], poly[:], 2.0, relu[:], ALU.mult,
                                                         ALU.add))
                do("rate", ts(rate[:, 0, :], poly[:], -8.0, None, ALU.mult))
                do("minus", ts(rate[:, 1, :], poly[:], 8.0, None, ALU.mult))
        act.end()
        vecs.end()


def recurrence_branch(nc, c, t, h, y, v_ctx):
    project(nc, c, t["w_in_2"], 0, 2 * MIX, h, y, (t["w_in_2"], 24, KT))
    with ExitStack() as ctx:
        def sb(name, *shape):
            return c.sb("lru_" + name, [P, *shape], ctx=ctx)
        rate = sb("rate", 2, 8)
        decay_rates(nc, c, rate)
        padded = sb("padded", 2, EXT + 2 * PAD)
        xc, r, ig = sb("convolved", 2, EXT), sb("r", 2, EXT), sb("gated_input", 2, EXT)
        a = sb("a", 2, EXT)
        run_ctx = sb("context_run", CTX)
        ys = sb("sum", 2, S)
        w = sb("gate_weights", 2, 2, MIX, P)
        items = [(p, d, x) for p in range(2) for d in range(2) for x in range(2)]
        tag = ["".join(map(str, i)) for i in items]
        groups = ["00", "01", "10", "11"]
        a_spec, v_spec = [], ["zero"]
        pads = lambda p: [f"pad{p}{x}{y}" for x in range(2) for y in ("x", "ctx")]
        convolved = lambda g: [f"{n}{g}{x}" for x in range(2) for n in ("c0", "c1", "c2", "c3")]
        v_spec += convolved("00")
        for g in groups:
            if g == "00":
                a_spec += pads(0)
            a_spec += [f"{n}{g}{x}" for x in range(2) for n in ("r", "ig")]
            a_spec += [f"{n}{g}{x}" for x in range(2) for n in ("a", "tanh", "square")]
            if g == "01":
                a_spec += pads(1)
            a_spec += [f"root{g}{x}" for x in range(2)]
            v_spec += [f"{n}{g}{x}" for n in ("in", "one") for x in range(2)]
            if g != "11":
                v_spec += convolved(groups[groups.index(g) + 1])
            v_spec += [f"{n}{g}{x}" for x in range(2)
                       for n in ("b", "sctx", "scan") + (("add",) if g[1] == "1" else ())]
            if g[1] == "1":
                a_spec += [f"silu{g[0]}{x}" for x in range(2)]
                v_spec += [f"out{g[0]}{x}" for x in range(2)]
        act, vecs = Steps(c, "act", a_spec), Steps(c, "vec", v_spec)
        pes = Steps(c, "pe", [f"gates{n}" for n in tag])
        d0 = c.base["dma"]
        c.base["dma"] += 16
        s0 = list(c.slots)
        lat, con = slice(0, S), slice(S + PAD, EXT)
        bank3 = lambda n: c.psum[:, 3 * n:3 * n + 3, :].rearrange("p b n -> p (b n)")[:, 0:EXT]
        with nc.Block() as block:
            @block.sync
            def _(sp):
                sp.dma_start(w[:], t["lru_w"]).then_inc(c.steps["dma"], 16)
                for p in range(2):
                    for x in range(2):
                        sp.wait_ge(vecs.sem, vecs.value(f"out{p}{x}"))
                        store_slot(c, sp, t["cat"][2 * p + x], ys[:, x, :], x)
                wait_slots(c, sp)

            @block.scalar
            def _(e):
                def pad(p):
                    if p == 0:
                        e.wait_ge(vecs.sem, vecs.value("zero"))
                    else:
                        e.wait_ge(vecs.sem, vecs.value("c3011"))
                    for x in range(2):
                        nc.scalar.copy(padded[:, x, PAD:PAD + S],
                                       y[:, 2 * p + x, :]).then_inc(act.step(f"pad{p}{x}x"), 1)
                        nc.scalar.copy(
   padded[:, x, 2 * PAD + S:2 * PAD + S + CTX], v_ctx[:, 2 * p + x, :]).then_inc(
                            act.step(f"pad{p}{x}ctx"), 1)
                pad(0)
                for g in groups:
                    p, d = int(g[0]), int(g[1])
                    for x in range(2):
                        m = 4 * d + 2 * p + x
                        e.wait_ge(pes.sem, pes.value(f"gates{g}{x}"))
                        if g != "00":
                            e.wait_ge(vecs.sem, vecs.value(f"b{groups[groups.index(g) - 1]}{x}"))
                        nc.scalar.activation(
        r[:, x, :], bank3(0), ACT.Sigmoid, bias=vec(c, "a_br_2", m)).then_inc(
                            act.step(f"r{g}{x}"), 1)
                        if g != "00":
                            e.wait_ge(vecs.sem,
                                      vecs.value(f"{'scan' if d else 'add'}{groups[groups.index(g) - 1]}{x}"))
                        nc.scalar.activation(
       ig[:, x, :], bank3(1), ACT.Sigmoid, bias=vec(c, "a_bi_2", m)).then_inc(
                            act.step(f"ig{g}{x}"), 1)
                    for x in range(2):
                        m = 4 * d + 2 * p + x
                        e.wait_ge(act.sem, act.value(f"r{g}{x}"))
                        nc.scalar.activation(a[:, x, :], r[:, x, :], ACT.Exp,
                                             scale=rate[:, 0, m:m + 1]).then_inc(
                            act.step(f"a{g}{x}"), 1)
                        e.wait_ge(act.sem, act.value(f"a{g}{x}"))
                        nc.scalar.activation(
     r[:, x, :], r[:, x, :], ACT.Tanh, scale=rate[:, 1, m:m + 1]).then_inc(
                            act.step(f"tanh{g}{x}"), 1)
                        e.wait_ge(vecs.sem, vecs.value(f"in{g}{x}"))
                        nc.scalar.activation(xc[:, x, :], a[:, x, :],
                                             ACT.Square).then_inc(act.step(f"square{g}{x}"), 1)
                    if g == "01":
                        pad(1)
                    for x in range(2):
                        e.wait_ge(vecs.sem, vecs.value(f"one{g}{x}"))
                        nc.scalar.activation(r[:, x, :], r[:, x, :],
                                             ACT.Sqrt).then_inc(act.step(f"root{g}{x}"), 1)
                    if d == 1:
                        for x in range(2):
                            nc.scalar.activation(
         y[:, MIX + 2 * p + x, :], y[:, MIX + 2 * p + x, :], ACT.Silu).then_inc(
                                act.step(f"silu{p}{x}"), 1)

            @block.vector
            def _(v):
                tt, stt = nc.vector.tensor_tensor, nc.vector.scalar_tensor_tensor
                nc.vector.memset(padded[:], 0.0).then_inc(vecs.step("zero"), 1)

                def convolve(g):
                    p, d = int(g[0]), int(g[1])
                    for x in range(2):
                        m = 2 * p + x
                        taps = [vec(c, "a_conv_2", 16 * d + 4 * m + k) for k in range(4)]
                        v.wait_ge(act.sem, act.value(f"pad{p}{x}ctx"))
                        at = PAD if d else 0
                        if g != "00":
                            v.wait_ge(vecs.sem, vecs.value(f"one{groups[groups.index(g) - 1]}{x}"))
                        nc.vector.tensor_scalar(
      xc[:, x, :], padded[:, x, at:at + EXT], taps[0], None, ALU.mult).then_inc(
                            vecs.step(f"c0{g}{x}"), 1)
                        for k in range(1, 4):
                            v.wait_ge(vecs.sem, vecs.value(f"c{k - 1}{g}{x}"))
                            stt(
        xc[:, x, :], padded[:, x, at + k:at + k + EXT], taps[k],
        xc[:, x, :], ALU.mult, ALU.add).then_inc(vecs.step(f"c{k}{g}{x}"), 1)

                convolve("00")
                for g in groups:
                    p, d = int(g[0]), int(g[1])
                    for x in range(2):
                        v.wait_ge(act.sem, act.value(f"ig{g}{x}"))
                        v.wait_ge(vecs.sem, vecs.value(f"c3{g}{x}"))
                        tt(ig[:, x, :], ig[:, x, :], xc[:, x, :], ALU.mult).then_inc(
                            vecs.step(f"in{g}{x}"), 1)
                    for x in range(2):
                        v.wait_ge(act.sem, act.value(f"square{g}{x}"))
                        stt(r[:, x, :], xc[:, x, :], 1.0, r[:, x, :],
                            ALU.add, ALU.mult).then_inc(vecs.step(f"one{g}{x}"), 1)
                    if g != "11":
                        convolve(groups[groups.index(g) + 1])
                    for x in range(2):
                        v.wait_ge(act.sem, act.value(f"root{g}{x}"))
                        v.wait_ge(vecs.sem, vecs.value(f"in{g}{x}"))
                        tt(ig[:, x, :], ig[:, x, :], r[:, x, :], ALU.mult).then_inc(
                            vecs.step(f"b{g}{x}"), 1)
                        v.wait_ge(vecs.sem, vecs.value(f"b{g}{x}"))

                        def run(tile, cols):
                            view = tile[:, x, cols] if cols is not None else tile
                            return view[:, ::-1] if d else view
                        if g != "00" or x:
                            v.wait_ge(vecs.sem,
                                      vecs.value("scan" + (f"{g}0" if x else f"{groups[groups.index(g) - 1]}1")))
                        out_ctx = run_ctx[:, ::-1] if d else run_ctx[:]
                        nc.vector.tensor_tensor_scan(
    out_ctx, run(a, con), run(ig, con), 0.0, ALU.mult, ALU.add).then_inc(
                            vecs.step(f"sctx{g}{x}"), 1)
                        v.wait_ge(vecs.sem, vecs.value(f"sctx{g}{x}"))
                        first = run_ctx[:, 0:1] if d else run_ctx[:, CTX - 1:CTX]
                        if d == 0 and p:
                            v.wait_ge(c.slot_stored[x], s0[x] + 16)
                        to = run(ys, lat) if d == 0 else run(ig, lat)
                        nc.vector.tensor_tensor_scan(
    to, run(a, lat), run(ig, lat), first, ALU.mult, ALU.add).then_inc(vecs.step(f"scan{g}{x}"), 1)
                        v.wait_ge(vecs.sem, vecs.value(f"scan{g}{x}"))
                        if d:
                            tt(ys[:, x, :], ys[:, x, :], ig[:, x, lat],
                               ALU.add).then_inc(vecs.step(f"add{g}{x}"), 1)
                    if d:
                        for x in range(2):
                            v.wait_ge(act.sem, act.value(f"silu{p}{x}"))
                            v.wait_ge(vecs.sem, vecs.value(f"add{g}{x}"))
                            tt(ys[:, x, :], ys[:, x, :],
                               y[:, MIX + 2 * p + x, :], ALU.mult).then_inc(
                                vecs.step(f"out{p}{x}"), 1)

            @block.tensor
            def _(e):
                e.wait_ge(c.steps["dma"], d0 + 16)
                for n, (p, d, x) in enumerate(items):
                    e.wait_ge(vecs.sem, vecs.value(f"c3{tag[n]}"))
                    if n:
                        e.wait_ge(act.sem, act.value(f"ig{tag[n - 1]}"))
                    for kind in range(2):
                        for q, (lo, hi) in enumerate(((0, HALF), (HALF, S), (S, EXT))):
                            last = nc.tensor.matmul(c.psum[:, 3 * kind + q, 0:hi - lo],
                                                    w[:, kind, d, 2 * p + x, :], xc[:, x, lo:hi],
                                                    start=True, stop=True)
                    last.then_inc(pes.step(f"gates{tag[n]}"), 1)
        for s in (act, vecs, pes):
            s.end()


def glu_input(nc, c, t, h, y):
    def evacuate(act, u, s, result, act_count, dve_count, q, j):
        if q == 0:
            nc.scalar.copy(one(y, j), result).then_inc(c.act_done, 1)
        else:
            nc.scalar.activation(one(y[:, MIX:2 * MIX, :], j), result,
                                 ACT.Sigmoid).then_inc(c.act_done, 1)

    def times(dve, u, s, result, act_count, dve_count, q, j):
        dve.wait_ge(c.act_done, act_count(u))
        if q:
            nc.vector.tensor_tensor(one(y, j), one(y, j), one(y[:, MIX:2 * MIX, :], j),
                                    ALU.mult).then_inc(c.dve_done, 1)
    project(nc, c, t["w_in_2"], 24, 2 * MIX, h, None, (t["w_in_2"], 8, KT), act_epilogue=evacuate,
            dve_epilogue=times)


TAPS = 31


def two_convolutions(nc, c, t, h, y):
    half = TAPS // 2
    order = [half] + [k for k in range(TAPS) if k != half]

    start3, start31 = VECTORS["b_conv_2"][0], VECTORS["c_conv_2"][0]
    with ExitStack() as ctx:
        z = c.sb("gated_conv_projected", [P, 4, S], ctx=ctx)
        conv = c.sb("gated_conv_out", [P, S], ctx=ctx)
        result_b = c.sb("gated_conv_branch", [P, MIX, S], ctx=ctx)
        vecs = Steps(c, "vec", [("tap", 24), "cv", "mid", "left", ("last", TAPS - 24), "right", "b",
                                "out"])

        def weight(first, j, step, k):
            return c.vectors[:, bass.ds(j * step + (first + k), 1)]

        def tap(dve, j, name, n, k):
            x, to = one(y, j), one(y[:, MIX:2 * MIX, :], j)
            w, s = weight(start31, j, TAPS, order[k]), order[k] - half
            if k == 0:
                ins = nc.vector.tensor_scalar(to, x, w, None, ALU.mult)
            else:
                if n:
                    dve.wait_ge(vecs.sem, vecs.value(name, n - 1, i=j))
                else:
                    dve.wait_ge(vecs.sem, vecs.value("tap", 23, i=j))
                at = to[:, max(0, -s):S - max(0, s)]
                ins = nc.vector.scalar_tensor_tensor(at, x[:, max(0, s):S - max(0, -s)], w, at,
                                                     ALU.mult, ALU.add)
            ins.then_inc(vecs.step(name), 1)

        def taps(dve, q, j):
            for n, k in enumerate(range(8 * q, min(8 * q + 8, TAPS))):
                if q < 3:
                    tap(dve, j, "tap", 8 * q + n, k)
                else:
                    tap(dve, j, "last", n, k)

        def evacuate(act, u, s, result, act_count, dve_count, q, j):
            if not isinstance(j, int) or j:
                act.wait_ge(vecs.sem, vecs.value_before("out", j))
            nc.scalar.activation(z[:, q, :], result,
                                 ACT.Silu if q == 3 else ACT.Copy).then_inc(c.act_done, 1)

        def combine(dve, u, s, result, act_count, dve_count, q, j):
            tt, stt = nc.vector.tensor_tensor, nc.vector.scalar_tensor_tensor
            b, x, val, gate = (z[:, n, :] for n in range(4))
            w = [weight(start3, j, 3, k) for k in range(3)]
            if q == 2:
                dve.wait_ge(c.act_done, act_count(u))
                tt(x, x, val, ALU.mult).then_inc(vecs.step("cv"), 1)
                dve.wait_ge(vecs.sem, vecs.value("cv", i=j))
                nc.vector.tensor_scalar(conv[:], x, w[1], None, ALU.mult).then_inc(
                    vecs.step("mid"), 1)
                dve.wait_ge(vecs.sem, vecs.value("mid", i=j))
                stt(conv[:, 1:], x[:, 0:S - 1], w[0], conv[:, 1:], ALU.mult,
                    ALU.add).then_inc(vecs.step("left"), 1)
            if q == 3:
                dve.wait_ge(c.act_done, act_count(u))
                dve.wait_ge(vecs.sem, vecs.value("left", i=j))
                stt(conv[:, 0:S - 1], x[:, 1:], w[2], conv[:, 0:S - 1],
                    ALU.mult, ALU.add).then_inc(vecs.step("right"), 1)
                dve.wait_ge(vecs.sem, vecs.value("right", i=j))
                tt(one(result_b, j), b, conv[:], ALU.mult).then_inc(vecs.step("b"), 1)
                dve.wait_ge(vecs.sem, vecs.value("b", i=j))
                tt(one(result_b, j), one(result_b, j), gate, ALU.mult).then_inc(vecs.step("out"), 1)

        stored = c.sem("gated_conv_stored")

        def keep(pool):
            with pool.Fori(0, MIX) as j:
                pool.wait_ge(vecs.sem, vecs.value("out", i=j))
                pool.dma_start(t["cat"][j + MIX], one(result_b, j)).then_inc(stored, 16)
            pool.wait_ge(stored, 16 * MIX)
        project(nc, c, t["w_in_2"], 8, 4 * MIX, h, None, (t["w_in_2"], 32, KT),
                act_epilogue=evacuate, dve_epilogue=combine, unroll=4,
                background={"dve": taps, "pool": keep})
        vecs.end(MIX)


def glu_conv_branch(nc, c, t, h, h_ctx, y):
    u, gate = y[:, MIX:2 * MIX, :], y[:, 0:MIX, :]
    with ExitStack() as ctx:
        parts = c.sb("glu_parts", [P, MIX, 2, S], F32R, ctx=ctx)
        with ExitStack() as inner:
            sq = c.sb("glu_squares", [P, MIX, S], ctx=inner)
            stat = c.sb("glu_statistics", [P, S], ctx=inner)
            act = Steps(c, "act", [("square", MIX), "root"])
            vecs = Steps(c, "vec", [("centred", MIX), "rstd", ("normed", MIX)])
            pes = Steps(c, "pe", ["mean", "variance"])

            def sums(pe, name, bank, src):
                for x in range(NH):
                    for m in range(MIX):
                        mm = nc.tensor.matmul(c.psum[:, bank + x, :], c.ones[:],
                                              src[:, m, x * HALF:(x + 1) * HALF],
                                              start=(m == 0), stop=(m == MIX - 1))
                mm.then_inc(pes.step(name), 1)

            def on_pe(pe, q, j):
                if q == 0:
                    sums(pe, "mean", 4, u)
                if q == 2:
                    pe.wait_ge(act.sem, act.value("square"))
                    sums(pe, "variance", 6, sq)

            def on_act(a, q, j):
                if q == 2:
                    for m in range(MIX):
                        a.wait_ge(vecs.sem, vecs.value("centred", m))
                        nc.scalar.activation(sq[:, m, :], u[:, m, :], ACT.Square).then_inc(
                            act.step("square"), 1)
                if q == 3:
                    a.wait_ge(pes.sem, pes.value("variance"))
                    nc.scalar.activation(stat[:], c.banks(6), ACT.Sqrt,
                                         scale=1.0 / (MIX * P), bias=c.eps[:, 1:2]).then_inc(
                        act.step("root"), 1)

            def on_dve(v, q, j):
                stt = nc.vector.scalar_tensor_tensor
                if q == 1:
                    v.wait_ge(pes.sem, pes.value("mean"))
                    for m in range(MIX):
                        stt(u[:, m, :], c.banks(4), -1.0 / (MIX * P),
                            u[:, m, :], ALU.mult, ALU.add).then_inc(vecs.step("centred"), 1)
                if q == 3:
                    v.wait_ge(act.sem, act.value("root"))
                    nc.vector.reciprocal(stat[:], stat[:]).then_inc(vecs.step("rstd"), 1)
                    v.wait_ge(vecs.sem, vecs.value("rstd"))
                    for m in range(MIX):
                        stt(u[:, m, :], u[:, m, :], vec(c, "c_ln_g_2", m),
                            stat[:], ALU.mult, ALU.mult).then_inc(vecs.step("normed"), 1)

            def evacuate(a, n, s, result, act_count, dve_count, q, j):
                nc.scalar.activation(gate[:, n, :], result, ACT.Silu).then_inc(c.act_done, 1)
            project(nc, c, t["w_in_2"], 32, MIX, h, None, (t["w_in_2"], 36, KT),
                    act_epilogue=evacuate, unroll=4,
                    background={"pe": on_pe, "act": on_act, "dve": on_dve})
            for x in (act, vecs, pes):
                x.end()
        tiles = c.sb("pool_projected", [P, 2 * MIX, S], ctx=ctx)
        act, vecs = Steps(c, "act", [("silu", MIX), ("high", MIX)]), Steps(c, "vec", [("low", MIX)])

        def silu_and_high(a, q, j):
            if q == 0:
                for m in range(MIX):
                    nc.scalar.activation(u[:, m, :], u[:, m, :], ACT.Silu,
                                         bias=vec(c, "c_ln_b_2", m)).then_inc(act.step("silu"), 1)
            if q == 1:
                for m in range(MIX):
                    a.wait_ge(act.sem, act.value("silu", m))
                    nc.scalar.copy(parts[:, m, 0, :], u[:, m, :]).then_inc(act.step("high"), 1)

        def low(v, q, j):
            if q == 2:
                for m in range(MIX):
                    v.wait_ge(act.sem, act.value("high", m))
                    nc.vector.tensor_tensor(parts[:, m, 1, :], u[:, m, :],
                                            parts[:, m, 0, :].bitcast(F32),
                                            ALU.subtract).then_inc(vecs.step("low"), 1)
        project(nc, c, t["w_in_2"], 36, MIX, h, tiles, (t["w_in_2"], 40, KT), unroll=4,
                background={"act": silu_and_high, "dve": low})
        act.end()
        vecs.end()

        def silu(a, n, s, result, act_count, dve_count, q, j):
            nc.scalar.activation(tiles[:, MIX + n, :], result, ACT.Silu).then_inc(c.act_done, 1)
        project(nc, c, t["w_in_2"], 40, MIX, h, None, (t["c_pw"], 0, MIX), unroll=4,
                act_epilogue=silu)
        h_ctx.close()
        product_and_pool(nc, c, t, parts, u, gate, tiles)


def product_and_pool(nc, c, t, parts, u, gate, tiles):
    bias = VECTORS["c_pw_b_2"][0]

    def plus_bias(act, n, s, result, act_count, dve_count, q, j):
        nc.scalar.activation(one(u, n), result, ACT.Identity,
                             bias=c.vectors[:, bass.ds(n + bias, 1)]).then_inc(c.act_done, 1)

    def gated(dve, n, s, result, act_count, dve_count, q, j):
        dve.wait_ge(c.act_done, act_count(n))
        nc.vector.tensor_tensor(one(u, n), one(u, n), one(gate, n),
                                ALU.mult).then_inc(c.dve_done, 1)
    gemm(nc, c, t["c_pw"], MIX, MIX, lambda k, x, h2: parts[:, k, x, h2 * HALF:(h2 + 1) * HALF],
         act_per_unit=1, act_epilogue=plus_bias, dve_per_unit=1, dve_epilogue=gated,
         then=(t["w_out_2"], 0, KT))
    pool_branch(nc, c, t, tiles, u)


def pool_branch(nc, c, t, y, glu):
    rows, width, edge = S // GRID_W, GRID_W, max(WINDOWS) // 2
    with ExitStack() as ctx:
        tall = c.sb("pool_rows", [P, 3, rows + 2 * edge, width], ctx=ctx)
        wide = c.sb("pool_columns", [P, 3, rows, width + 2 * edge], ctx=ctx)
        share = c.sb("pool_share", [P, 2, S], ctx=ctx)
        w = c.sb("pool_weights", [P, MIX, P], ctx=ctx)
        v_spec = ["zero_tall", "zero_wide"]
        for g, win in enumerate(WINDOWS):
            v_spec += [f"in{g}"] + [f"row{g}_{k}" for k in range(g + 1)]
            v_spec += [f"column{g}_{k}" for k in range(g + 1)] + [f"mean{g}", f"less{g}"]
        v_spec += [f"{n}{g}" for g in range(MIX) for n in ("bias", "out")]
        vecs = Steps(c, "vec", v_spec)
        pes = Steps(c, "pe", [("product", MIX)])
        d = [c.sem(f"pool_share_loaded_{s}") for s in range(2)]
        d0 = c.base["dma"]
        c.base["dma"] += 16
        with nc.Block() as block:
            @block.sync
            def _(sp):
                sp.dma_start(w[:], t["d_w"]).then_inc(c.steps["dma"], 16)
                store(c, sp, t["cat"][2 * MIX:3 * MIX].rearrange("n p s -> p n s"), glu)
                for g in range(MIX):
                    if g >= 2:
                        sp.wait_ge(vecs.sem, vecs.value(f"mean{g - 2}"))
                    sp.dma_start(share[:, g % 2, :],
                                 t["pool_shares"][g].partition_broadcast(P)).then_inc(d[g % 2], 16)
                for g in range(MIX):
                    sp.wait_ge(vecs.sem, vecs.value(f"out{g}"))
                    store(c, sp, t["cat"][3 * MIX + g], y[:, g, :])
                sp.wait_ge(c.scratch_stored, c.stored)

            @block.vector
            def _(v):
                tt = nc.vector.tensor_tensor

                def do(name, ins):
                    ins.then_inc(vecs.step(name), 1)
                    v.wait_ge(vecs.sem, vecs.value(name))
                do("zero_tall", nc.vector.memset(tall[:], 0.0))
                do("zero_wide", nc.vector.memset(wide[:], 0.0))
                for g, win in enumerate(WINDOWS):
                    grid = y[:, g, :].rearrange("p (r w) -> p r w", w=width)
                    do(f"in{g}", nc.vector.tensor_copy(tall[:, 0, edge:edge + rows, :], grid))
                    first, src = edge - win // 2, 0
                    for k in range(g + 1):
                        step, n = 2 ** k, rows + win - 2 ** (k + 1)
                        a, b = (tall[:, src, first + x:first + x + n, :] for x in (0, step))
                        if k == g:
                            to = wide[:, 0, :, edge:edge + width]
                        else:
                            to = tall[:, 1 + k % 2, first:first + n, :]
                        do(f"row{g}_{k}", tt(to, a, b, ALU.add))
                        src = 1 + k % 2
                    src = 0
                    for k in range(g + 1):
                        step, n = 2 ** k, width + win - 2 ** (k + 1)
                        a, b = (wide[:, src, :, first + x:first + x + n] for x in (0, step))
                        do(f"column{g}_{k}", tt(wide[:, 1 + k % 2, :, first:first + n], a, b,
                                                ALU.add))
                        src = 1 + k % 2
                    v.wait_ge(d[g % 2], 16 * (g // 2 + 1))
                    total = wide[:, src, :, first:first + width]
                    sh = share[:, g % 2, :].rearrange("p (r w) -> p r w", w=width)
                    do(f"mean{g}", tt(tall[:, 1, 0:rows, :], total, sh, ALU.mult))
                    do(f"less{g}", tt(grid, tall[:, 1, 0:rows, :], grid, ALU.subtract))
                for g in range(MIX):
                    v.wait_ge(pes.sem, pes.value("product", g))
                    do(f"bias{g}", nc.vector.tensor_scalar(
                        y[:, g, :], c.banks(2 * g), vec(c, "d_b_2", g), vec(c, "d_scale_2", g),
                        ALU.add, ALU.mult))
                    do(f"out{g}", tt(y[:, g, :], y[:, g, :], y[:, MIX + g, :], ALU.mult))

            @block.tensor
            def _(p):
                p.wait_ge(c.steps["dma"], d0 + 16)
                for g in range(MIX):
                    p.wait_ge(vecs.sem, vecs.value(f"less{g}"))
                    for n in range(NH):
                        mm = nc.tensor.matmul(c.psum[:, 2 * g + n, :], w[:, g, :],
                                              y[:, g, n * HALF:(n + 1) * HALF], start=True,
                                              stop=True)
                    mm.then_inc(pes.step("product"), 1)
        for s in (vecs, pes):
            s.end()


def mixer_out(nc, c, t, y):
    with ExitStack() as ctx:
        x = c.sb("mixed", [P, KT, S], ctx=ctx)
        parts = c.sb("mixed_parts", [P, KT, 2, S], F32R, ctx=ctx)

        def copy(dve, u, s, result, act_count, dve_count, q, j):
            nc.vector.tensor_copy(one(y, u), result).then_inc(c.dve_done, 1)

        def add(dve, u, s, result, act_count, dve_count, q, j):
            nc.vector.tensor_tensor(one(y, u), one(y, u), result, ALU.add).then_inc(c.dve_done, 1)
        for half in range(2):
            load_tiles(nc, c, x, t["cat"][KT * half:KT * half + KT])
            split(nc, c, x, parts)
            gemm(nc, c, t["w_out_2"], KT, KT,
                 lambda k, p, n: parts[:, k, p, n * HALF:(n + 1) * HALF], first=KT * half,
                 then=None if half else (t["w_out_2"], KT, KT), dve_per_unit=1, dve_epilogue=add if half else copy, banks_read_by="dve")


def load_tiles(nc, c, tiles, dram):
    d0 = c.base["dma"]
    c.base["dma"] += 16
    with nc.Block() as block:
        @block.sync
        def _(sp):
            sp.dma_start(tiles[:], dram.rearrange("n p s -> p n s")).then_inc(c.steps["dma"], 16)
            sp.wait_ge(c.steps["dma"], d0 + 16)


def build(nc, t):
    with ExitStack() as ctx:
        c = Core(nc, ctx)
        scratch = {"branch": [4, P, 2, S], "x_mid": [P, KT, S], "x_second": [P, KT, S],
                   "cat": [4 * MIX, P, S]}
        for name, shape in scratch.items():
            t[name] = nc.dram_tensor(f"{name}_scratch", shape, F32, kind="Internal").ap()
        load_constants(nc, c, t)
        merged_ctx = ctx.enter_context(ExitStack())
        times, plus = c.sb("mod_times", [P, KT, 2]), c.sb("mod_plus", [P, KT, 2])
        gate = c.sb("mod_gate", [P, KT])
        merged = branches(nc, c, t, merged_ctx, (times, plus, gate))
        y = c.sb("y", [P, KT, S])
        with ExitStack() as mix_ctx:
            with ExitStack() as sums_ctx:
                total = c.sb("square_totals", [P, S], ctx=sums_ctx)
                sq = c.sb("squares", [P, 2, S], ctx=sums_ctx)
                with ExitStack() as mlp_ctx:
                    x_ctx = ctx.enter_context(ExitStack())
                    x = mix_out(nc, c, t, merged, merged_ctx, y, total, sq, x_ctx)
                    h = c.sb("mlp_in", [P, KT, 2, S], F32R, ctx=mlp_ctx)
                    add_residual(nc, c, t, y, total, lambda k: vec(c, "norm_mix_post", k),
                                 True, None, t["x_mid"], out=h,
                                 times=lambda k: vec(c, "norm_mlp_pre", k), defer=True, loaded=x)
                    x_ctx.close()
                    mlp(nc, c, t, h, y, total, sq)
                h = c.sb("mixer_in", [P, KT, 2, S], F32R, ctx=mix_ctx, side="right")
                add_residual(nc, c, t, y, total, lambda k: vec(c, "norm_mlp_post", k), None,
                             t["x_mid"], t["x_second"], out=h, times=lambda k: times[:, k, 0:1],
                             plus=lambda k: plus[:, k, 0:1])
            with ExitStack() as inner:
                v_ctx = c.sb("ctx_values", [P, MIX, CTX], ctx=inner)
                context_values(nc, c, t, times, plus, v_ctx)
                recurrence_branch(nc, c, t, h, y, v_ctx)
            glu_input(nc, c, t, h, y)
            two_convolutions(nc, c, t, h, y)
            glu_conv_branch(nc, c, t, h, mix_ctx, y)
        mixer_out(nc, c, t, y)
        add_residual(nc, c, t, y, None, lambda k: gate[:, k:k + 1], None, t["x_second"], None,
                     times=lambda k: vec(c, "final_g_2", k), final=True)


def unit_columns():
    names = ("dn_q", "dn_k", "dn_v", "dn_z", "dn_b", "dn_a", "mla_cq", "mla_ckv", "mla_kpe",
             "gla_q", "gla_k", "gla_v", "gla_g", "gla_lr", "fox_q", "fox_k", "fox_v", "fox_f")
    sizes = (256, 256, 256, 256, 4, 4, 256, 128, 32, 128, 128, 256, 256, 16, 256, 256, 256, 4)
    at = dict(zip(names, np.cumsum((0, *sizes))[:-1]))
    kpe = at["mla_kpe"] + np.arange(ROPE)
    swap = np.roll(np.arange(ROPE), ROPE // 2)
    small_1, small_2 = np.full(P, -1), np.full(P, -1)
    order = np.array([0, 2, 1, 3])
    small_1[0:4] = at["dn_b"] + order
    small_1[32:36] = at["dn_a"] + order
    small_1[64:96], small_1[96:128] = kpe, kpe[swap]
    small_2[0:128:32] = at["fox_f"] + np.arange(4)
    small_2[1:17] = at["gla_lr"] + np.arange(16)
    units = [small_1, small_2]
    for name, size in zip(names, sizes):
        if size >= P:
            units += [at[name] + P * n + np.arange(P) for n in range(size // P)]
    return units


def in_units(w, columns=None):
    k, n = w.shape
    if columns is not None:
        w = np.concatenate([w, np.zeros((k, 1), w.dtype)], axis=1)[:, np.concatenate(columns)]
        n = w.shape[1]
    w = w.reshape(k // P, P, n // P, P)
    return np.ascontiguousarray(w.transpose(2, 1, 0, 3)).reshape(n // P, P, -1)


def by_partition(v):
    v = np.asarray(v)
    return v.reshape(-1, P).T


def constants():
    i = np.arange(P)
    row, col = i[:, None], i[None, :]
    chunk = row // CH == col // CH
    f = np.float32
    squares = np.stack([row == col, np.ones((P, P)), chunk]).astype(f)
    masks = [np.where(chunk & (col >= row), 0, -1e30), np.where(chunk & (col <= row), 0, 1e30)]
    for level in range(LEVELS):
        b = 2 ** level
        m = (row // (2 * b) == col // (2 * b)) & (row // b % 2 == 1) & (col // b % 2 == 0)
        masks += [m, m.T] if level == 0 else [m.T]
    select = np.zeros((P, 10, P), f)
    for kind in range(3):
        for pair in range(2):
            for half in range(2):
                select[32 * kind + place(2 * pair + half), 2 * kind + pair, 64 * half:64 * half + 64] = 1
    for h in range(HEADS):
        select[96 + h, 6 + h, :] = 1
    out = {
        "squares": squares,
        "dn_masks": np.ascontiguousarray(np.stack(masks).astype(f).transpose(1, 0, 2)),
        "selectors": select,
        "restart": (np.arange(S) % CH != 0).astype(f),
    }
    pos = np.arange(S, dtype=f)
    inv = (1.0 / (f(10000.0) ** (np.arange(0, ROPE, 2, dtype=f) / f(ROPE)))).astype(f)
    ang = np.concatenate([inv, inv])[:, None] * pos[None, :]
    sign = np.where(np.arange(ROPE) < ROPE // 2, -1, 1)[:, None]
    rope = np.zeros((P, S), f)
    rope[64:96], rope[96:128] = np.cos(ang), sign * np.sin(ang)
    out["rope"] = rope
    block = row // CH >= col // CH
    out["attention_masks"] = np.ascontiguousarray(
        np.stack([np.where(block, 0, -1e30), np.where(row >= col, 0, -1e30)]).astype(f).transpose(1, 0, 2))
    upper = (chunk & (row <= col)).astype(f)
    kv = np.zeros((P, 256), f)
    for h in range(HEADS):
        kv[32 * h:32 * h + 32, 64 * h:64 * h + 64] = 1
    out["gla_masks"] = np.concatenate([upper, kv], axis=1)
    counts = []
    for w in WINDOWS:
        def n(size):
            p = np.arange(size)
            return np.clip(p + w // 2, 0, size) - np.clip(p - w // 2, 0, size)
        counts.append((n(S // GRID_W)[:, None] * n(GRID_W)[None, :]).reshape(S))
    out["pool_shares"] = (1 / np.stack(counts)).astype(f)
    return out


def lay_out(inputs):
    a = {k: np.asarray(v) for k, v in inputs.items()}
    f = np.float32
    out = constants()
    out["x"] = a["x"][0]
    out["w_in"] = in_units(a["w_in"][0], unit_columns())
    gate = np.stack([in_units(w) for w in a["w_gate"][0]], axis=1)
    up = np.stack([in_units(w) for w in a["w_branch_up"][0]], axis=1)
    out["w_gate"] = np.concatenate([gate, up], axis=3).reshape(32, P, -1)
    out["w_out"] = in_units(a["w_out"][0])
    out["w_mlp_in"] = in_units(a["w_mlp_in"][0])
    out["w_mlp_out"] = np.concatenate([in_units(w) for w in a["w_mlp_out"][0].reshape(4, D, D)])
    slots = a["w_in_2"][0].reshape(D, 11, MIX * P)
    tile = lambda s, m: slots[:, s, m * P:(m + 1) * P]
    order = [(s, m) for s in (0, 1) for m in range(MIX)]
    order += [(s, m) for m in range(MIX) for s in (2, 3, 4, 5)]
    order += [(s, m) for m in range(MIX) for s in (6, 7)]
    order += [(s, m) for s in (8, 9, 10) for m in range(MIX)]
    out["w_in_2"] = in_units(np.concatenate([tile(s, m) for s, m in order], axis=1))
    out["w_out_2"] = np.concatenate([in_units(w) for w in a["w_out_2"][0].reshape(2, D, D)])
    out["c_pw"] = in_units(a["c_pw_2"][0])
    mod = in_units(a["mod_w_2"][0]).reshape(MOD_LOADS, 3, P, D)
    out["mod_w"] = mod.transpose(0, 2, 1, 3).reshape(MOD_LOADS, P, 3 * D)
    out["d_w"] = a["d_w_2"][0].transpose(1, 0, 2)
    out["ctx"] = a["ctx_2"][0]
    lru = np.zeros((2, 2, MIX, P, P), f)
    for kind, name in enumerate(("a_wr_2", "a_wi_2")):
        w = a[name][0].reshape(2, MIX, 2, CH, CH)
        for x in range(2):
            lru[kind, :, :, CH * x:CH * x + CH, CH * x:CH * x + CH] = w[:, :, x]
    out["lru_w"] = lru.transpose(3, 0, 1, 2, 4)
    vectors = np.zeros((P, N_VECTORS), f)

    def put(name, value):
        start, count = VECTORS[name]
        assert value.shape == (P, count), (name, value.shape)
        vectors[:, start:start + count] = value

    for name in ("norm_mix_pre", "norm_mix_post", "norm_mlp_pre", "norm_mlp_post", "mla_q_norm",
                 "mla_kv_norm", "gla_gate_bias", "norm_g_2", "final_g_2", "mod_b_2", "a_br_2",
                 "a_bi_2", "a_lam_2", "c_ln_g_2", "c_ln_b_2", "c_pw_b_2", "d_b_2", "d_scale_2"):
        put(name, by_partition(a[name]))

    def taps(w, tiles):
        return w.reshape(w.shape[0], tiles, P).transpose(2, 1, 0).reshape(P, -1)

    put("dn_conv", taps(a["dn_conv"][0], 6))
    put("b_conv_2", taps(a["b_conv_2"][0], 4))
    put("c_conv_2", taps(a["c_conv_2"][0], 4))
    put("a_conv_2", np.concatenate([taps(a["a_conv_2"][0, d], 4) for d in range(2)], axis=1))
    put("b_gate", a["b_gate"][0].reshape(4, KT, P).transpose(2, 1, 0).reshape(P, 32))
    put("gla_norm", np.concatenate([a["gla_norm"][0]] * 2)[:, None])
    put("dn_norm", np.concatenate([a["dn_norm"][0]] * 2)[:, None])
    c2 = np.stack([a["c_2"][0], a["c_ctx_2"]])
    put("c_2", c2.reshape(2, KT, P).transpose(2, 1, 0).reshape(P, 16))
    for name, src in (("row_bias", "dn_dt_bias"), ("dn_a_log", "dn_a_log")):
        column = np.zeros((P, 1), f)
        column[32:36, 0] = a[src][0][[0, 2, 1, 3]]
        put(name, column)
    column = np.zeros((P, 1), f)
    column[0:128:32, 0] = a["fox_f_bias"][0]
    put("fox_f_bias", column)
    out["vectors"] = vectors
    up = np.zeros((32, P), f)
    up[1:17] = a["gla_w_gate_up"][0]
    out["gla_gate_up"] = up
    head = np.concatenate([np.arange(DH + ROPE), DH + np.roll(np.arange(ROPE), ROPE // 2)])
    cols = np.concatenate([h * (DH + ROPE) + head for h in range(HEADS)])
    out["mla_w_q"] = a["mla_w_q_up"][0][:, cols].reshape(2, P, HEADS * P).transpose(1, 0, 2)
    kv = a["mla_w_kv_up"][0].reshape(P, HEADS, 2, DH).transpose(0, 2, 1, 3)
    out["mla_w_kv"] = kv.reshape(P, 512)
    return {k: np.ascontiguousarray(v) for k, v in out.items()}


def kernel(**inputs):
    import concourse.bacc as bacc
    from concourse.bass_utils import run_bass_kernel_spmd

    arrays = lay_out(inputs)
    nc = bacc.Bacc("TRN2", target_bir_lowering=False, num_devices=1)
    t = {k: nc.dram_tensor(f"in_{k}", v.shape, F32, kind="ExternalInput").ap()
         for k, v in arrays.items()}
    t["out"] = nc.dram_tensor("out_tokens", [S, D], F32, kind="ExternalOutput").ap()
    build(nc, t)
    r = run_bass_kernel_spmd(nc, [{f"in_{k}": v for k, v in arrays.items()}], core_ids=[0])
    return r.results[0]["out_tokens"].reshape(1, S, D)
```

```python
from contextlib import ExitStack

import numpy as np

import concourse.bass as bass
from concourse import mybir

F32 = mybir.dt.float32
F32R = mybir.dt.float32r
ALU = mybir.AluOpType
ACT = mybir.ActivationFunctionType
AX_X = mybir.AxisListType.X

P = 128
S = 1024
D = 1024
KT = D // P
HALF = 512
NH = S // HALF
BLK = S // P
HEADS, DH = 4, 64
CH = 64
GDK = 32
ROPE = 32
CTX = 256
EPS = 1e-6
LN_EPS = 1e-5
GRID_W = 64
WINDOWS = (2, 4, 8, 16)
WK = 10


class Steps:

    def __init__(self, c, engine, spec):
        self.c, self.engine, self.sem, self.base = c, engine, c.steps[engine], c.base[engine]
        self.at, self.count, self.order, n = {}, {}, [], 0
        for item in spec:
            what, k = item if isinstance(item, tuple) else (item, 1)
            turns = (what,) if isinstance(what, str) else what
            for m, name in enumerate(turns):
                assert name not in self.at, name
                self.at[name], self.count[name] = (n + m + 1, len(turns)), k
            self.order += list(turns) * k
            n += k * len(turns)
        self.n, self.next = n, 0

    def place(self, name, k=None):
        k = self.count[name] - 1 if k is None else k
        assert 0 <= k < self.count[name], (name, k)
        return self.at[name][0] + k * self.at[name][1]

    def value(self, name, k=None, i=0):
        return i * self.n + (self.base + self.place(name, k))

    def value_before(self, name, i, k=None):
        assert self.base >= self.n
        return i * self.n + (self.base - self.n + self.place(name, k))

    def step(self, name):
        assert self.order[self.next] == name, (self.engine, self.order[self.next], name)
        self.next = (self.next + 1) % self.n
        return self.sem

    def end(self, iterations=1):
        assert self.next == 0, (self.engine, self.order[self.next])
        self.c.base[self.engine] = self.base + iterations * self.n


class Core:

    def __init__(self, nc, ctx):
        self.nc, self.ctx, self.used = nc, ctx, {}
        self.steps = {e: self.sem(f"{e}_steps") for e in ("pe", "act", "vec", "pool", "dma")}
        self.base = {e: 0 for e in (*self.steps, "gemm_act", "gemm_dve")}
        self.loaded = [self.sem(f"weights_loaded_{s}") for s in range(2)]
        self.high_ready = self.sem("high_part_ready")
        self.low_ready = self.sem("low_part_ready")
        self.unit_done = self.sem("unit_multiplied")
        self.act_done = self.sem("unit_evacuated_by_act")
        self.dve_done = self.sem("unit_evacuated_by_dve")
        self.units = 0
        self.loads = [0, 0]
        self.ahead = None
        self.raw = self.sb("weights_raw", [P, 2, WK * P])
        self.parts = self.sb("weights_parts", [P, 2, 2, WK * P], F32R)
        self.psum = ctx.enter_context(nc.psum_tensor("psum", [P, 8, HALF], F32))
        self.scratch_stored = self.sem("scratch_stored")
        self.stored = 0
        self.slot_stored = [self.sem(f"slot_stored_{s}") for s in range(2)]
        self.slots = [0, 0]
        self.residual_loaded = [self.sem(f"residual_loaded_{n}") for n in range(2)]
        self.residuals = [0, 0]

    def sem(self, name):
        return self.ctx.enter_context(self.nc.semaphore(name))

    def sb(self, name, shape, dtype=F32, ctx=None, side="left"):
        self.used[name] = self.used.get(name, 0) + 1
        if self.used[name] > 1:
            name = f"{name}_{self.used[name]}"
        return (ctx or self.ctx).enter_context(self.nc.sbuf_tensor(name, shape, dtype,
                                                                    side=side))

    def banks(self, first, n=2):
        return self.psum[:, first:first + n, :].rearrange("p b n -> p (b n)")


def gemm(nc, c, weights, n_units, kt, rhs, act_per_unit=0, act_epilogue=None,
         dve_per_unit=0, dve_epilogue=None, banks_read_by="act", first=0, unroll=2,
         extra_kt=0, extra_rhs=None, halves=NH, cols=HALF, then=None, background=None, pool_cuts=False):
    background = background or {}
    ready = c.ahead is not None
    assert not ready or c.ahead == (weights.tensor.name, first, kt + extra_kt), c.ahead
    c.ahead = None
    if then:
        assert n_units % 2 == 0
        c.ahead = (then[0].tensor.name, then[1], then[2])
    w = (kt + extra_kt) * P
    u0, l0 = c.units, list(c.loads)
    a0, d0 = c.base["gemm_act"], c.base["gemm_dve"]
    c.units += n_units
    c.loads = [l0[0] + (n_units + 1) // 2, l0[1] + n_units // 2]
    c.base["gemm_act"] += n_units * act_per_unit
    c.base["gemm_dve"] += n_units * dve_per_unit
    assert unroll % 2 == 0 and n_units >= 2

    def act_count(u, k=0):
        return u * act_per_unit + (a0 + k + 1)

    def dve_count(u, k=0):
        return u * dve_per_unit + (d0 + k + 1)

    def units(eng, body):
        whole = n_units // unroll
        for q in range(min(unroll, n_units)):
            body(q, q % 2, q // 2, q, q < 2, 0)
        if whole > 1:
            with eng.Fori(1, whole) as j:
                for q in range(unroll):
                    body(unroll * j + q, q % 2, unroll // 2 * j + q // 2, q, False, j)
        if whole:
            for u in range(unroll * whole, n_units):
                body(u, u % 2, u // 2, u % unroll, False, u // unroll)

    with nc.Block() as block:

        @block.sync
        def _(sp):
            def load(u, s, turn, q, fresh, j):
                if not fresh:
                    sp.wait_ge(c.low_ready, u + (u0 - 1))
                if not (fresh and ready):
                    sp.dma_start(c.raw[:, s, 0:w], weights[u + first]).then_inc(c.loaded[s], 16)
                if "sp" in background:
                    background["sp"](sp, q, j)
            units(sp, load)
            if then:
                for s in range(2):
                    sp.wait_ge(c.low_ready, u0 + n_units - 1 + s)
                    sp.dma_start(c.raw[:, s, 0:then[2] * P],
                                 then[0][then[1] + s]).then_inc(c.loaded[s], 16)

        def pairs(eng, split, epilogue):
            if not ready:
                split(0, 0, 0, True)
            n = (n_units - 1) // unroll

            def group(j, fresh):
                for q in range(unroll):
                    split(unroll * j + q + 1, (q + 1) % 2, unroll // 2 * j + (q + 1) // 2,
                          fresh and q == 0)
                    epilogue(unroll * j + q, q % 2, q, j)
            if n:
                group(0, True)
            if n > 1:
                with eng.Fori(1, n) as j:
                    group(j, False)
            for u in range(n * unroll, n_units):
                if u + 1 < n_units:
                    split(u + 1, (u + 1) % 2, (u + 1) // 2, u == 0)
                elif then:
                    split(n_units, 0, n_units // 2, False, then[2] * P)
                epilogue(u, u % 2, u % unroll, u // unroll)

        @block.scalar
        def _(act):
            def split(u, s, turn, fresh, w=w):
                act.wait_ge(c.loaded[s], 16 * turn + 16 * (l0[s] + 1))
                if not fresh:
                    act.wait_ge(c.unit_done, u + (u0 - 1))
                nc.scalar.copy(c.parts[:, s, 0, 0:w], c.raw[:, s, 0:w]).then_inc(c.high_ready, 1)

            def epilogue(u, s, q, j):
                if "act" in background:
                    background["act"](act, q, j)
                if act_epilogue:
                    act.wait_ge(c.unit_done, u + (u0 + 1))
                    act_epilogue(act, u, s, c.banks(2 * s), act_count, dve_count, q, j)
            pairs(act, split, epilogue)

        @block.vector
        def _(dve):
            def split(u, s, turn, fresh, w=w):
                if pool_cuts:
                    return
                dve.wait_ge(c.high_ready, u + (u0 + 1))
                nc.vector.tensor_tensor(c.parts[:, s, 1, 0:w], c.raw[:, s, 0:w],
                                        c.parts[:, s, 0, 0:w].bitcast(F32),
                                        ALU.subtract).then_inc(c.low_ready, 1)

            def epilogue(u, s, q, j):
                if "dve" in background:
                    background["dve"](dve, q, j)
                if dve_epilogue:
                    dve.wait_ge(c.unit_done, u + (u0 + 1))
                    dve_epilogue(dve, u, s, c.banks(2 * s), act_count, dve_count, q, j)
            pairs(dve, split, epilogue)

        if "pool" in background:
            @block.gpsimd
            def _(pool):
                def low(u):
                    s, n = u % 2, w if u < n_units else then[2] * P
                    pool.wait_ge(c.high_ready, u + u0 + 1)
                    nc.gpsimd.tensor_tensor(c.parts[:, s, 1, 0:n], c.raw[:, s, 0:n],
                                            c.parts[:, s, 0, 0:n].bitcast(F32),
                                            ALU.subtract).then_inc(c.low_ready, 1)
                background["pool"](*((pool, low) if pool_cuts else (pool,)))

        @block.tensor
        def _(pe):
            def product(bank, s, k0, kt, moving):
                n = 0
                for k in range(kt):
                    at = slice((k0 + k) * P, (k0 + k + 1) * P)
                    for wp, xp in ((0, 0), (0, 1), (1, 0)):
                        for h in range(halves):
                            mm = nc.tensor.matmul(c.psum[:, bank + h, 0:cols],
                                                  c.parts[:, s, wp, at], moving(k, xp, h),
                                                  start=(n < halves),
                                                  stop=(n >= halves * (3 * kt - 1)))
                            n += 1
                return mm

            def unit(u, s, turn, q, fresh, j):
                pe.wait_ge(c.low_ready, u + (u0 + 1))
                if not fresh:
                    if banks_read_by == "act":
                        pe.wait_ge(c.act_done, act_count(u - 2, act_per_unit - 1))
                    else:
                        pe.wait_ge(c.dve_done, dve_count(u - 2, dve_per_unit - 1))
                mm = product(2 * s, s, 0, kt, rhs)
                if extra_kt:
                    mm = product(4 + 2 * s, s, kt, extra_kt,
                                 lambda k, xp, h: extra_rhs(k, xp, h, q))
                mm.then_inc(c.unit_done, 1)
                if "pe" in background:
                    background["pe"](pe, q, j)
            units(pe, unit)


VECTORS = {}


def _columns():
    n = 0
    for name, k in (
        ("norm_mix_pre", 8), ("norm_mix_post", 8), ("norm_mlp_pre", 8), ("norm_mlp_post", 8),
        ("dn_conv", 24), ("b_gate", 32), ("mla_q_norm", 2), ("mla_kv_norm", 1),
        ("gla_gate_bias", 1), ("gla_norm", 1), ("dn_norm", 1), ("row_bias", 1), ("dn_a_log", 1),
        ("fox_f_bias", 1), ("norm_g_2", 8), ("final_g_2", 8), ("mod_b_2", 24), ("c_2", 16),
        ("a_conv_2", 32), ("a_br_2", 8), ("a_bi_2", 8), ("a_lam_2", 8), ("b_conv_2", 12),
        ("c_conv_2", 124), ("c_ln_g_2", 4), ("c_ln_b_2", 4), ("c_pw_b_2", 4), ("d_b_2", 4),
        ("d_scale_2", 4),
    ):
        VECTORS[name] = (n, k)
        n += k
    return n


N_VECTORS = _columns()


def vec(c, name, k=0, n=1):
    start, count = VECTORS[name]
    assert k + n <= count
    return c.vectors[:, start + k:start + k + n]


def bcast(ap, n):
    return ap.unsqueeze(2).broadcast_to([ap.shape[0], ap.shape[1], n])


def over_heads(ap, n=HEADS):
    return ap.unsqueeze(1).broadcast_to([ap.shape[0], n, ap.shape[1]])


def heads(ap, n=HEADS):
    return ap.rearrange("p (h m) -> p h m", h=n)


def store(c, eng, dram, tile):
    c.stored += 16
    eng.dma_start(dram, tile).then_inc(c.scratch_stored, 16)


def store_slot(c, eng, dram, tile, s):
    c.slots[s] += 16
    eng.dma_start(dram, tile).then_inc(c.slot_stored[s], 16)


def wait_slots(c, eng):
    for s in range(2):
        eng.wait_ge(c.slot_stored[s], c.slots[s])


def load_constants(nc, c, t):
    c.ident = c.sb("identity", [P, P])
    c.ones = c.sb("all_ones", [P, P])
    c.head_ones = c.sb("ones_by_head_pair", [P, P])
    c.vectors = c.sb("vectors", [P, N_VECTORS])
    c.eps = c.sb("epsilon", [P, 2])
    c.silu = c.sb("mod_silu", [P, 16])
    dma, vecs = Steps(c, "dma", [("load", 64)]), Steps(c, "vec", [("eps", 2)])
    silu = Steps(c, "act", ["silu"])
    with nc.Block() as block:
        @block.sync
        def _(sp):
            for n, (dst, src) in enumerate((
                (c.ident, t["squares"][0]), (c.ones, t["squares"][1]),
                (c.head_ones, t["squares"][2]), (c.vectors, t["vectors"]),
            )):
                sp.dma_start(dst[:], src).then_inc(dma.sem, 16)
            sp.wait_ge(dma.sem, 64)

        @block.vector
        def _(dve):
            for n, value in enumerate((EPS, LN_EPS)):
                nc.vector.memset(c.eps[:, n:n + 1], value).then_inc(vecs.step("eps"), 1)
        @block.scalar
        def _(act):
            act.wait_ge(dma.sem, 64)
            nc.scalar.activation(c.silu[:], vec(c, "c_2", 0, 16), ACT.Silu).then_inc(
                silu.step("silu"), 1)
    silu.end()
    c.base["dma"] = 64
    vecs.end()


def norm_input(nc, c, t, hidden):
    with ExitStack() as ctx:
        x = c.sb("x_tokens", [P, BLK, D], ctx=ctx)
        junk = c.sb("x_squares", [P, D], ctx=ctx)
        ss = c.sb("x_square_sums", [P, BLK], ctx=ctx)
        root = c.sb("x_rms", [P, BLK], ctx=ctx)
        rstd = c.sb("x_rstd", [P, BLK], ctx=ctx)
        half = BLK // NH
        act = Steps(c, "act", [("square", half), "root", ("square_1", half), "root_1",
                               ("high", KT * NH)])
        vecs = Steps(c, "vec", ["rstd", ("scaled", half), "rstd_1", ("scaled_1", half),
                                ("low", KT * NH)])
        pes = Steps(c, "pe", [("turned", KT * NH)])
        loaded = [c.sem(f"x_blocks_loaded_{n}") for n in range(4)]
        xb = t["x"].rearrange("(b p) d -> p b d", p=P)
        tag = ("", "_1")
        w = KT * P
        c.ahead = (t["w_in"].tensor.name, 0, KT)
        with nc.Block() as block:
            @block.sync
            def _(sp):
                for n in range(4):
                    sp.dma_start(x[:, 2 * n:2 * n + 2, :],
                                 xb[:, 2 * n:2 * n + 2, :]).then_inc(loaded[n], 16)
                for s in range(2):
                    sp.dma_start(c.raw[:, s, 0:w], t["w_in"][s]).then_inc(c.loaded[s], 16)

            @block.scalar
            def _(a):
                for h in range(NH):
                    for b in range(half):
                        if b % 2 == 0:
                            a.wait_ge(loaded[2 * h + b // 2], 16)
                        if b:
                            a.wait_ge(act.sem, act.value("square" + tag[h], b - 1))
                        elif h:
                            a.wait_ge(act.sem, act.value("square"))
                        at = half * h + b
                        nc.scalar.activation(junk[:], x[:, at, :], ACT.Square,
                                             accum_out=ss[:, at:at + 1]).then_inc(
                                                 act.step("square" + tag[h]), 1)
                    a.wait_ge(act.sem, act.value("square" + tag[h]))
                    blocks = slice(half * h, half * h + half)
                    nc.scalar.activation(root[:, blocks], ss[:, blocks], ACT.Sqrt, scale=1.0 / D,
                                         bias=c.eps[:, 0:1]).then_inc(act.step("root" + tag[h]), 1)
                for g in range(KT * NH):
                    h, k = g // KT, g % KT
                    a.wait_ge(pes.sem, pes.value("turned", g))
                    nc.scalar.activation(hidden[:, k, 0, h * HALF:(h + 1) * HALF],
                                         c.psum[:, g % 4, :], ACT.Copy,
                                         scale=vec(c, "norm_mix_pre", k)).then_inc(
                                             act.step("high"), 1)
                a.wait_ge(c.loaded[0], 16)
                nc.scalar.copy(c.parts[:, 0, 0, 0:w], c.raw[:, 0, 0:w]).then_inc(c.high_ready, 1)

            @block.vector
            def _(v):
                for h in range(NH):
                    blocks = slice(half * h, half * h + half)
                    v.wait_ge(act.sem, act.value("root" + tag[h]))
                    nc.vector.reciprocal(rstd[:, blocks], root[:, blocks]).then_inc(
                        vecs.step("rstd" + tag[h]), 1)
                    v.wait_ge(vecs.sem, vecs.value("rstd" + tag[h]))
                    for b in range(half * h, half * h + half):
                        nc.vector.tensor_scalar(x[:, b, :], x[:, b, :], rstd[:, b:b + 1], None,
                                                ALU.mult).then_inc(vecs.step("scaled" + tag[h]), 1)
                for g in range(KT * NH):
                    h, k = g // KT, g % KT
                    v.wait_ge(act.sem, act.value("high", g))
                    cols = slice(h * HALF, (h + 1) * HALF)
                    nc.vector.scalar_tensor_tensor(
                        hidden[:, k, 1, cols], c.psum[:, g % 4, :], vec(c, "norm_mix_pre", k),
                        hidden[:, k, 0, cols].bitcast(F32), ALU.mult, ALU.subtract).then_inc(
                            vecs.step("low"), 1)
                v.wait_ge(c.high_ready, 1)
                nc.vector.tensor_tensor(c.parts[:, 0, 1, 0:w], c.raw[:, 0, 0:w],
                                        c.parts[:, 0, 0, 0:w].bitcast(F32),
                                        ALU.subtract).then_inc(c.low_ready, 1)

            @block.tensor
            def _(p):
                for g in range(KT * NH):
                    h, k = g // KT, g % KT
                    if k == 0:
                        p.wait_ge(vecs.sem, vecs.value("scaled" + tag[h]))
                    if g >= 4:
                        p.wait_ge(vecs.sem, vecs.value("low", g - 4))
                    for q in range(half):
                        mm = nc.tensor.transpose(c.psum[:, g % 4, q * P:(q + 1) * P],
                                                 x[:, half * h + q, k * P:(k + 1) * P], c.ident[:])
                    mm.then_inc(pes.step("turned"), 1)
        for s in (act, vecs, pes):
            s.end()


def project(nc, c, weights, first, n_units, hidden, out, then=None, act_epilogue=None,
            **options):
    def evacuate(act, u, s, result, act_count, dve_count, q, j):
        nc.scalar.copy(out[:, bass.ds(u, 1), :].rearrange("p a n -> p (a n)"),
                       result).then_inc(c.act_done, 1)
    gemm(nc, c, weights, n_units, KT, lambda k, part, h: hidden[:, k, part, h * HALF:(h + 1) * HALF],
         act_per_unit=1, act_epilogue=act_epilogue or evacuate, first=first, then=then, **options)


MOD_LOADS = 8


class Modulation:

    def __init__(self, c, t, ctx):
        self.c, self.t = c, t
        self.w = c.sb("mod_weights", [P, 2, 3 * D], ctx=ctx)
        self.loaded = [c.sem(f"mod_weights_loaded_{s}") for s in range(2)]
        self.multiplied = c.sem("mod_load_multiplied")

    def load_first(self, pool):
        for q in range(2):
            pool.dma_start(self.w[:, q, :], self.t["mod_w"][q]).then_inc(self.loaded[q], 16)

    def load_others(self, pool):
        w, loaded = self.w, self.loaded
        with pool.Fori(1, MOD_LOADS // 2) as j:
            for q in range(2):
                pool.wait_ge(self.multiplied, 2 * j + (q - 1))
                pool.dma_start(w[:, q, :], self.t["mod_w"][2 * j + q]).then_inc(loaded[q], 16)

    def multiply(self, pe, q, j):
        c = self.c
        pe.wait_ge(self.loaded[q], 16 * j + 16)
        for x in range(3):
            at = 12 * j + (6 * q + 2 * x)
            for k in range(KT):
                mm = c.nc.tensor.matmul(c.psum[:, 7, bass.ds(at, 2)],
                                        self.w[:, q, x * D + k * P:x * D + (k + 1) * P],
                                        c.silu[:, 2 * k:2 * k + 2], start=(k == 0),
                                        stop=(k == KT - 1))
        mm.then_inc(self.multiplied, 1)


def modulate(nc, c, times, plus, gate):
    with ExitStack() as ctx:
        mod = c.sb("mod_out", [P, 24, 2], ctx=ctx)
        vecs = Steps(c, "vec", ["mod", "scale", "times", "plus", "gate"])
        with nc.Block() as block:
            @block.vector
            def _(v):
                nc.vector.tensor_tensor(
                    mod[:], c.psum[:, 7, 0:48].rearrange("p (u w) -> p u w", w=2),
                    bcast(vec(c, "mod_b_2", 0, 24), 2), ALU.add).then_inc(vecs.step("mod"), 1)
                v.wait_ge(vecs.sem, vecs.value("mod"))
                nc.vector.tensor_scalar(mod[:, 8:16, :], mod[:, 8:16, :], 1.0, None,
                                        ALU.add).then_inc(vecs.step("scale"), 1)
                v.wait_ge(vecs.sem, vecs.value("scale"))
                nc.vector.tensor_tensor(
                    times[:], mod[:, 8:16, :], bcast(vec(c, "norm_g_2", 0, 8), 2),
                    ALU.mult).then_inc(vecs.step("times"), 1)
                nc.vector.tensor_copy(plus[:], mod[:, 0:8, :]).then_inc(vecs.step("plus"), 1)
                nc.vector.tensor_copy(gate[:], mod[:, 16:24, 0]).then_inc(vecs.step("gate"), 1)
        vecs.end()


def tokens_to_channels(nc, c, o_tok, out_dram, gate=None, gain=None, norm=False):
    with ExitStack() as ctx:
        o = c.sb("branch_channels", [P, 2, S], ctx=ctx)
        sq = c.sb("branch_squares", [P, BLK * HEADS, DH], ctx=ctx) if norm else None
        ss = c.sb("branch_square_sums", [P, BLK * HEADS], ctx=ctx) if norm else None
        root = c.sb("branch_rms", [P, BLK * HEADS], ctx=ctx) if norm else None
        rstd = c.sb("branch_rstd", [P, BLK * HEADS], ctx=ctx) if norm else None
        silu = c.sb("branch_silu", [P, 2, S], ctx=ctx) if norm else None
        act = Steps(c, "act", (["square", "root", "silu"] if norm else []) + [("unused", 0)])
        vecs = Steps(c, "vec", (["sums", "rstd", "scaled"] if norm else []) + [("out", 4)])
        pes = Steps(c, "pe", [("turned", 4)])
        view = o_tok.rearrange("p b (h d) -> p (b h) d", d=DH)
        with nc.Block() as block:
            if norm:
                @block.scalar
                def _(a):
                    nc.scalar.activation(sq[:], view, ACT.Square).then_inc(act.step("square"), 1)
                    a.wait_ge(vecs.sem, vecs.value("sums"))
                    nc.scalar.activation(root[:], ss[:], ACT.Sqrt, scale=1.0 / DH,
                                         bias=c.eps[:, 0:1]).then_inc(act.step("root"), 1)
                    nc.scalar.activation(silu[:], gate, ACT.Silu).then_inc(act.step("silu"), 1)

            @block.vector
            def _(v):
                if norm:
                    v.wait_ge(act.sem, act.value("square"))
                    nc.vector.tensor_reduce(ss[:], sq[:], AX_X, ALU.add).then_inc(
                        vecs.step("sums"), 1)
                    v.wait_ge(act.sem, act.value("root"))
                    nc.vector.reciprocal(rstd[:], root[:]).then_inc(vecs.step("rstd"), 1)
                    v.wait_ge(vecs.sem, vecs.value("rstd"))
                    nc.vector.tensor_tensor(view, view, bcast(rstd[:], DH),
                                            ALU.mult).then_inc(vecs.step("scaled"), 1)
                    v.wait_ge(act.sem, act.value("silu"))
                for g in range(4):
                    t, h = g // 2, g % 2
                    cols = slice(h * HALF, (h + 1) * HALF)
                    v.wait_ge(pes.sem, pes.value("turned", g))
                    if norm:
                        nc.vector.scalar_tensor_tensor(
                            o[:, t, cols], c.psum[:, g, :], gain, silu[:, t, cols],
                            ALU.mult, ALU.mult).then_inc(vecs.step("out"), 1)
                    else:
                        nc.vector.tensor_copy(o[:, t, cols], c.psum[:, g, :]).then_inc(
                            vecs.step("out"), 1)

            @block.tensor
            def _(p):
                if norm:
                    p.wait_ge(vecs.sem, vecs.value("scaled"))
                for g in range(4):
                    t, h = g // 2, g % 2
                    for q in range(4):
                        mm = nc.tensor.transpose(c.psum[:, g, q * P:(q + 1) * P],
                                                 o_tok[:, 4 * h + q, t * P:(t + 1) * P], c.ident[:])
                    mm.then_inc(pes.step("turned"), 1)

            @block.sync
            def _(sp):
                sp.wait_ge(vecs.sem, vecs.value("out"))
                store(c, sp, out_dram, o[:])
                sp.wait_ge(c.scratch_stored, c.stored)
        for s in (act, vecs, pes):
            s.end()


def channels_to_tokens(nc, c, src, dst):
    pes = Steps(c, "pe", [("turned", 4)])
    vecs = Steps(c, "vec", [("kept", 4)])
    with nc.Block() as block:
        @block.tensor
        def _(p):
            for g in range(4):
                for q in range(2):
                    for t in range(2):
                        mm = nc.tensor.transpose(
                            c.psum[:, g, (2 * q + t) * P:(2 * q + t + 1) * P],
                            src[:, t, (2 * g + q) * P:(2 * g + q + 1) * P], c.ident[:])
                mm.then_inc(pes.step("turned"), 1)

        @block.vector
        def _(v):
            for g in range(4):
                v.wait_ge(pes.sem, pes.value("turned", g))
                nc.vector.tensor_copy(
                    dst[:, 2 * g:2 * g + 2, :].rearrange("p b n -> p (b n)"), c.psum[:, g, :]).then_inc(
                    vecs.step("kept"), 1)
    pes.end()
    vecs.end()


LEVELS = 6
DN_MASKS = 9


def delta_net(nc, c, t, hidden, small, modulated):
    with ExitStack() as ctx:
        proj = c.sb("dn_projected", [P, 8, S], ctx=ctx)
        o_tok = c.sb("dn_out_tokens", [P, BLK + 1, 256], ctx=ctx)
        with ExitStack() as inner:
            padded_rows = c.sb("dn_rows", [P, S + P], ctx=inner)
            rows = padded_rows[:, 0:S]
            g_tok = c.sb("dn_decay_tokens", [P, BLK, HEADS], ctx=inner)
            with ExitStack() as mod_ctx:
                modulation = Modulation(c, t, mod_ctx)
                project(nc, c, t["w_in"], 2, 8, hidden, proj, (t["w_in"], 10, KT),
                        background={"pool": modulation.load_first})
                delta_net_inputs(nc, c, t, proj, rows, g_tok, small, modulation, padded_rows)
            modulate(nc, c, *modulated)
            delta_net_chunks(nc, c, t, proj, padded_rows, g_tok, o_tok)
        tokens_to_channels(nc, c, o_tok[:, 1:, :], t["branch"][0], gate=proj[:, 6:8, :],
                           gain=vec(c, "dn_norm"), norm=True)


def delta_net_inputs(nc, c, t, proj, rows, g_tok, small, modulation, padded_rows):
    with ExitStack() as ctx:
        conv = c.sb("dn_conv_out", [P, 2, S], ctx=ctx)
        sq = c.sb("dn_squares", [P, 2, S], ctx=ctx)
        root = c.sb("dn_norms", [P, 2, S], ctx=ctx)
        restart = c.sb("dn_chunk_restart", [P, S], ctx=ctx)
        soft = c.sb("dn_softplus", [P, S], ctx=ctx)
        rate = c.sb("dn_rate", [P, 1], ctx=ctx)
        act = Steps(c, "act", [("silu", 6), ("square", 4), "beta", "abs", "exp", "ln", "rate",
                               ("root", 4), "kept", "decay", "tail"])
        vecs = Steps(c, "vec", ["zero", ("conv", 24), "relu", "soft", "g", "gc", "to_end",
                                (("rstd", "unit"), 4), ("g_tok", 2)])
        pes = Steps(c, "pe", [("sums", 4), ("turned", 2)])
        d0 = c.base["dma"]
        c.base["dma"] += 16
        gl = slice(32, 36)
        with nc.Block() as block:
            @block.sync
            def _(sp):
                sp.dma_start(restart[:], t["restart"].partition_broadcast(P)).then_inc(
                    c.steps["dma"], 16)

            @block.gpsimd
            def _(pool):
                modulation.load_others(pool)

            @block.scalar
            def _(a):
                for n in range(6):
                    a.wait_ge(vecs.sem, vecs.value("conv", 4 * n + 3))
                    nc.scalar.activation(proj[:, n, :], conv[:, n % 2, :], ACT.Silu).then_inc(
                        act.step("silu"), 1)
                for n in range(4):
                    a.wait_ge(act.sem, act.value("silu", n))
                    if n >= 2:
                        a.wait_ge(pes.sem, pes.value("sums", n - 2))
                    nc.scalar.activation(sq[:, n % 2, :], proj[:, n, :],
                                         ACT.Square).then_inc(act.step("square"), 1)
                a.wait_ge(vecs.sem, vecs.value("zero"))
                nc.scalar.activation(rows[0:4, :], small[0:4, 0, :], ACT.Sigmoid).then_inc(
                    act.step("beta"), 1)
                nc.scalar.activation(soft[gl, :], small[gl, 0, :], ACT.Abs,
                                     bias=vec(c, "row_bias")[gl, :]).then_inc(act.step("abs"), 1)
                a.wait_ge(act.sem, act.value("abs"))
                nc.scalar.activation(soft[gl, :], soft[gl, :], ACT.Exp, scale=-1.0).then_inc(
                    act.step("exp"), 1)
                a.wait_ge(act.sem, act.value("exp"))
                nc.scalar.activation(soft[gl, :], soft[gl, :], ACT.Ln, bias=1.0).then_inc(
                    act.step("ln"), 1)
                nc.scalar.activation(rate[gl, :], vec(c, "dn_a_log")[gl, :],
                                     ACT.Exp).then_inc(act.step("rate"), 1)
                for n in range(4):
                    a.wait_ge(pes.sem, pes.value("sums", n))
                    if n >= 2:
                        a.wait_ge(vecs.sem, vecs.value("unit", n - 2))
                    nc.scalar.activation(root[:, n % 2, :], c.banks(2 * (n % 3)),
                                         ACT.Sqrt, bias=c.eps[:, 0:1]).then_inc(act.step("root"), 1)
                a.wait_ge(vecs.sem, vecs.value("to_end"))
                nc.scalar.copy(rows[96:100, :], soft[gl, :]).then_inc(act.step("kept"), 1)
                nc.scalar.activation(rows[gl, :], soft[gl, :], ACT.Exp).then_inc(
                    act.step("decay"), 1)
                nc.scalar.activation(rows[64:68, :], small[gl, 0, :], ACT.Exp).then_inc(
                    act.step("tail"), 1)

            @block.vector
            def _(v):
                nc.vector.memset(padded_rows[:], 0.0).then_inc(vecs.step("zero"), 1)
                for n in range(6):
                    w = [vec(c, "dn_conv", 4 * n + k) for k in range(4)]
                    dst = conv[:, n % 2, :]
                    if n >= 2:
                        v.wait_ge(act.sem, act.value("silu", n - 2))
                    nc.vector.tensor_scalar(dst, proj[:, n, :], w[3], None,
                                            ALU.mult).then_inc(vecs.step("conv"), 1)
                    for s in (1, 2, 3):
                        v.wait_ge(vecs.sem, vecs.value("conv", 4 * n + s - 1))
                        nc.vector.scalar_tensor_tensor(
                            dst[:, s:], proj[:, n, 0:S - s], w[3 - s], dst[:, s:], ALU.mult,
                            ALU.add).then_inc(vecs.step("conv"), 1)
                v.wait_ge(act.sem, act.value("rate"))
                nc.vector.tensor_scalar(small[gl, 0, :], small[gl, 0, :],
                                        vec(c, "row_bias")[gl, :], 0.0, ALU.add,
                                        ALU.max).then_inc(vecs.step("relu"), 1)
                v.wait_ge(vecs.sem, vecs.value("relu"))
                nc.vector.tensor_tensor(small[gl, 0, :], small[gl, 0, :],
                                        soft[gl, :], ALU.add).then_inc(vecs.step("soft"), 1)
                v.wait_ge(vecs.sem, vecs.value("soft"))
                nc.vector.tensor_scalar(small[gl, 0, :], small[gl, 0, :],
                                        rate[gl, :], -1.0, ALU.mult, ALU.mult).then_inc(
                    vecs.step("g"), 1)
                v.wait_ge(vecs.sem, vecs.value("g"))
                v.wait_ge(c.steps["dma"], d0 + 16)
                nc.vector.tensor_tensor_scan(soft[gl, :], restart[gl, :],
                                             small[gl, 0, :], 0.0, ALU.mult, ALU.add).then_inc(
                    vecs.step("gc"), 1)
                v.wait_ge(vecs.sem, vecs.value("gc"))
                by_chunk = soft[gl, :].rearrange("p (n m) -> p n m", m=CH)
                nc.vector.tensor_tensor(
                    small[gl, 0, :].rearrange("p (n m) -> p n m", m=CH),
                    by_chunk[:, :, CH - 1:CH].broadcast_to([4, S // CH, CH]), by_chunk,
                    ALU.subtract).then_inc(vecs.step("to_end"), 1)
                for n in range(4):
                    v.wait_ge(act.sem, act.value("root", n))
                    nc.vector.reciprocal(root[:, n % 2, :], root[:, n % 2, :]).then_inc(
                        vecs.step("rstd"), 1)
                    v.wait_ge(vecs.sem, vecs.value("rstd", n))
                    nc.vector.scalar_tensor_tensor(
                        proj[:, n, :], proj[:, n, :], DH ** -0.5 if n < 2 else 1.0,
                        root[:, n % 2, :], ALU.mult, ALU.mult).then_inc(vecs.step("unit"), 1)
                for g in range(2):
                    v.wait_ge(pes.sem, pes.value("turned", g))
                    nc.vector.tensor_copy(
                        g_tok[:, 4 * g:4 * g + 4, :],
                        heads(c.psum[:, g, :])[:, :, 96:100]).then_inc(vecs.step("g_tok"), 1)

            @block.tensor
            def _(p):
                modulation.multiply(p, 0, 0)
                modulation.multiply(p, 1, 0)
                modulation.multiply(p, 0, 1)
                for n in range(4):
                    p.wait_ge(act.sem, act.value("square", n))
                    if n == 3:
                        modulation.multiply(p, 1, 1)
                        p.wait_ge(act.sem, act.value("root", 0))
                    for h in range(NH):
                        mm = nc.tensor.matmul(c.psum[:, 2 * (n % 3) + h, :], c.head_ones[:],
                                              sq[:, n % 2, h * HALF:(h + 1) * HALF],
                                              start=True, stop=True)
                    mm.then_inc(pes.step("sums"), 1)
                with p.Fori(2, MOD_LOADS // 2) as j:
                    for q in range(2):
                        modulation.multiply(p, q, j)
                p.wait_ge(act.sem, act.value("tail"))
                for g in range(2):
                    for q in range(4):
                        b = 4 * g + q
                        mm = nc.tensor.transpose(c.psum[:, g, q * P:(q + 1) * P],
                                                 rows[:, b * P:(b + 1) * P], c.ident[:])
                    mm.then_inc(pes.step("turned"), 1)
        for s in (act, vecs, pes):
            s.end()


def place(h):
    return 2 * (h % 2) + h // 2


def by_parity(tile):
    return tile[:].rearrange("p (a m) n -> p a (m n)", a=2)


def delta_net_chunks(nc, c, t, proj, rows, g_tok, o_tok):
    with ExitStack() as ctx:
        def sb(name, *shape):
            return c.sb("dn_" + name, [P, *shape], ctx=ctx)
        masks = sb("masks", DN_MASKS, P)
        select = sb("row_selectors", 10, P)
        ks, qs, kb, kbe, kt, vb = (sb(n, 2, P) for n in
                                   ("k", "q", "k_beta", "k_beta_decay", "k_tail", "v_beta"))
        twice = lambda *a: (sb(*a), sb(*a))
        qds, all_ends, qks = twice("q_decay", 2, P), twice("chunk_decay", 2, 2), \
            twice("qk_turned", HEADS, P)
        dec_t, dec = sb("decay_turned", HEADS, P), sb("decay", HEADS, P)
        a_t, a_0 = sb("a_turned", HEADS, P), sb("a", HEADS, P)
        a_lev = sb("a_levels_turned", LEVELS - 1, HEADS * P)
        inv, inv_t = sb("inverse", HEADS, P), sb("inverse_turned", HEADS, P)
        prod = a_0
        toks, vb_tok = twice("keys_by_token", HEADS * P), sb("values_by_token", 256)
        w_ts, us, v_new = twice("w_turned", 2, P), twice("u", 256), sb("v_new", 256)
        state, fading = sb("state", 2, P), sb("state_decayed", 2, P)
        levels = range(1, LEVELS)
        carried = {"pe": {1: "read0", 2: "add0", 3: "read1", 4: "add1"},
                   "vec": {n + 1: [f"{x}{n // 2}" for x in (("v_new", "fade"),
                                                            ("state_a", "state_b"))[n % 2]]
                           for n in range(4)}}
        pes = Steps(c, "pe", ["kk", "tok", "qk_odd"]
                    + sum([[f"a_inverse{n}"] + ([carried["pe"][n]] if n < 5 else ["next_rows"])
                           + ([f"grow{n}"] if n < 5 else []) + [f"grow_turned{n}"]
                           for n in levels], []) + ["uw"])
        act = Steps(c, "act", ["k", "q", "decay_turned", "decay", "keys_tok", "values_tok"]
                    + [f"a_inverse{n}" for n in levels[:-1]] + ["out", f"a_inverse{LEVELS - 1}"])
        vecs = Steps(c, "vec", ["k_beta", "v_beta", "q_decay", "k_tail", "k_beta_decay", "ends",
                                "diff", "upper", "lower", "a_turned", "a", "a_level0",
                                "inverse0", "a_level0t", "turned0", "qk_even", "qk_odd"]
                     + sum([[f"inverse{n}", f"turned{n}"] + carried["vec"][n]
                            for n in levels[:-1]], [])
                     + [f"turned{LEVELS - 1}", "w", "u"])
        pool = Steps(c, "pool", [f"level{n}" for n in levels])
        d0 = c.base["dma"]
        c.base["dma"] += 32
        for s in (pool, pes):
            s.base += s.n
        ps = c.psum
        ends_view = lambda: ps[:, 0, 256:512].rearrange("p (a j n) -> p a j n", a=2, j=2)

        def hp(h):
            return slice(64 * (h % 2), 64 * (h % 2) + 64)

        def blocks(eng, body):
            with eng.Fori(0, BLK // 2) as pair:
                for parity in range(2):
                    body(2 * pair + parity, parity)

        def read(j, par):
            r = slice(CH * j, CH * j + CH)
            for pair in range(2):
                to = slice(pair * P, (pair + 1) * P)
                nc.tensor.matmul(ps[r, 6, to], w_ts[par][:, pair, r], state[:, pair, :],
                                 start=True, stop=True)
                last = nc.tensor.matmul(ps[r, 7, to], qds[par][:, pair, r], state[:, pair, :],
                                        start=(pair == 0), stop=False, skip_group_check=True)
            return last

        def add(j, par):
            r = slice(CH * j, CH * j + CH)
            for pair in range(2):
                to = slice(pair * P, (pair + 1) * P)
                nc.tensor.matmul(ps[:, 6, 256 + pair * P:256 + (pair + 1) * P],
                                 toks[par][r, 256 + pair * P:256 + (pair + 1) * P],
                                 v_new[r, to], start=True, stop=True)
            for h in range(HEADS):
                to = slice(64 * h, 64 * h + 64)
                last = nc.tensor.matmul(ps[r, 7, to], qks[par][r, place(h), r], v_new[r, to],
                                        start=False, stop=(h == HEADS - 1), skip_group_check=True)
            return last

        def new_values(j, par):
            r = slice(CH * j, CH * j + CH)
            return nc.vector.tensor_tensor(v_new[r, :], us[par][r, :], ps[r, 6, 0:256],
                                           ALU.subtract)

        def fade(j, par):
            return nc.vector.tensor_tensor(fading[:], state[:], bcast(all_ends[par][:, :, j], P),
                                           ALU.mult)

        def new_state(half):
            q = slice(64 * half, 64 * half + 64)
            new = ps[:, 6, 256:512].rearrange("p (a n) -> p a n", a=2)
            return nc.vector.tensor_tensor(state[q, :, q], fading[q, :, q], new[q, :, q], ALU.add)

        def spread_rows(cols):
            for n in range(6):
                nc.tensor.matmul(ps[:, n // 4, (n % 4) * P:(n % 4 + 1) * P], select[:, n, :],
                                 rows[:, cols], start=True, stop=True)
            for h in range(HEADS):
                last = nc.tensor.matmul(ps[:, 2, h * P:(h + 1) * P], select[:, 6 + h, :],
                                        rows[:, cols], start=True, stop=True)
            return last

        first_rows = c.sem("dn_first_rows_spread")
        with nc.Block() as block:
            @block.sync
            def _(sp):
                sp.dma_start(masks[:], t["dn_masks"]).then_inc(c.steps["dma"], 16)
                sp.dma_start(select[:], t["selectors"]).then_inc(c.steps["dma"], 16)
                sp.wait_ge(c.steps["dma"], d0 + 32)

            @block.gpsimd
            def _(g):
                for tile in (w_ts[1], toks[1], qds[1], qks[1], all_ends[1]):
                    nc.gpsimd.memset(tile[:], 0.0)
                nc.gpsimd.memset(us[1][:], 0.0).then_inc(pes.sem, pes.n)
                nc.gpsimd.memset(state[:], 0.0).then_inc(pool.sem, pool.n)
                g.wait_ge(c.steps["dma"], d0 + 32)

                def body(i, par):
                    for n in levels:
                        g.wait_ge(vecs.sem, vecs.value("a_turned", i=i))
                        if n == 1:
                            g.wait_ge(pes.sem, pes.value_before(f"a_inverse{LEVELS - 1}", i))
                        nc.gpsimd.tensor_tensor(
                            heads(a_lev[:, n - 1, :]), a_t[:], over_heads(masks[:, 3 + n, :]),
                            ALU.mult).then_inc(pool.step(f"level{n}"), 1)
                blocks(g, body)

            @block.scalar
            def _(a):
                def body(i, par):
                    cols = bass.ds(i * P, P)
                    a.wait_ge(pes.sem, pes.value_before("qk_odd", i))
                    nc.scalar.copy(ks[:], proj[:, 2:4, cols]).then_inc(act.step("k"), 1)
                    nc.scalar.copy(qs[:], proj[:, 0:2, cols]).then_inc(act.step("q"), 1)
                    a.wait_ge(vecs.sem, vecs.value("upper", i=i))
                    nc.scalar.activation(dec_t[:], dec_t[:], ACT.Exp).then_inc(
                        act.step("decay_turned"), 1)
                    a.wait_ge(vecs.sem, vecs.value("lower", i=i))
                    nc.scalar.activation(dec[:], dec[:], ACT.Exp, scale=-1.0).then_inc(
                        act.step("decay"), 1)
                    a.wait_ge(pes.sem, pes.value("tok", i=i))
                    nc.scalar.copy(toks[par][:], ps[:, 0, :]).then_inc(act.step("keys_tok"), 1)
                    nc.scalar.copy(vb_tok[:], ps[:, 1, 0:256]).then_inc(act.step("values_tok"), 1)
                    for n in levels:
                        if n == LEVELS - 1:
                            a.wait_ge(pes.sem, pes.value("add1", i=i))
                            nc.scalar.copy(
                                o_tok[:, bass.ds(i, 1), :].rearrange("p b n -> p (b n)"),
                                ps[:, 7, 0:256]).then_inc(act.step("out"), 1)
                        a.wait_ge(pes.sem, pes.value(f"a_inverse{n}", i=i))
                        nc.scalar.copy(prod[:], heads(ps[:, 3, :])).then_inc(
                            act.step(f"a_inverse{n}"), 1)
                blocks(a, body)

            @block.vector
            def _(v):
                v.wait_ge(c.steps["dma"], d0 + 32)
                v.wait_ge(pool.sem, pool.base)
                v.wait_ge(pes.sem, pes.base)
                v.wait_ge(first_rows, 1)

                def body(i, par):
                    cols = bass.ds(i * P, P)
                    tt = nc.vector.tensor_tensor
                    before = 1 - par
                    qd, ends, qk = qds[par], all_ends[par], qks[par]
                    beta, decay = ps[:, 0, 0:256].rearrange("p (a n) -> p a n", a=2), \
                        ps[:, 0, 256:512].rearrange("p (a n) -> p a n", a=2)
                    tail = ps[:, 1, 0:256].rearrange("p (a n) -> p a n", a=2)
                    v.wait_ge(pes.sem, pes.value_before("next_rows", i))
                    v.wait_ge(act.sem, act.value("q", i=i))
                    tt(kb[:], ks[:], beta, ALU.mult).then_inc(vecs.step("k_beta"), 1)
                    tt(vb[:], proj[:, 4:6, cols], beta, ALU.mult).then_inc(vecs.step("v_beta"), 1)
                    tt(qd[:], qs[:], decay, ALU.mult).then_inc(vecs.step("q_decay"), 1)
                    tt(kt[:], ks[:], tail, ALU.mult).then_inc(vecs.step("k_tail"), 1)
                    v.wait_ge(vecs.sem, vecs.value("k_beta", i=i))
                    tt(kbe[:], kb[:], decay, ALU.mult).then_inc(vecs.step("k_beta_decay"), 1)
                    nc.vector.tensor_copy(ends[:], ends_view()[:, :, :, CH - 1]).then_inc(
                        vecs.step("ends"), 1)
                    gi = g_tok[:, bass.ds(i, 1), :].rearrange("p b h -> p (b h)")
                    tt(dec[:], heads(ps[:, 2, :]), bcast(gi, P), ALU.subtract).then_inc(
                        vecs.step("diff"), 1)
                    v.wait_ge(vecs.sem, vecs.value("diff", i=i))
                    tt(dec_t[:], dec[:], over_heads(masks[:, 0, :]), ALU.add).then_inc(
                        vecs.step("upper"), 1)
                    tt(dec[:], dec[:], over_heads(masks[:, 1, :]), ALU.add).then_inc(
                        vecs.step("lower"), 1)
                    v.wait_ge(pes.sem, pes.value("kk", i=i))
                    v.wait_ge(act.sem, act.value("decay", i=i))
                    tt(by_parity(a_t), ps[:, 3:6:2, 0:256], by_parity(dec_t),
                       ALU.mult).then_inc(vecs.step("a_turned"), 1)
                    tt(by_parity(a_0), ps[:, 3:6:2, 256:512], by_parity(dec),
                       ALU.mult).then_inc(vecs.step("a"), 1)
                    v.wait_ge(vecs.sem, vecs.value("a", i=i))
                    tt(a_0[:], a_0[:], over_heads(masks[:, 2, :]), ALU.mult).then_inc(
                        vecs.step("a_level0"), 1)
                    v.wait_ge(vecs.sem, vecs.value("a_level0", i=i))
                    tt(inv[:], over_heads(c.ident[:]), a_0[:], ALU.subtract).then_inc(
                        vecs.step("inverse0"), 1)
                    tt(inv_t[:], a_t[:], over_heads(masks[:, 3, :]),
                       ALU.mult).then_inc(vecs.step("a_level0t"), 1)
                    v.wait_ge(vecs.sem, vecs.value("a_level0t", i=i))
                    tt(inv_t[:], over_heads(c.ident[:]), inv_t[:],
                       ALU.subtract).then_inc(vecs.step("turned0"), 1)
                    tt(by_parity(qk)[:, 0, :], ps[:, 4, 0:256],
                       by_parity(dec_t)[:, 0, :], ALU.mult).then_inc(vecs.step("qk_even"), 1)
                    v.wait_ge(pes.sem, pes.value("qk_odd", i=i))
                    tt(by_parity(qk)[:, 1, :], ps[:, 2, 0:256],
                       by_parity(dec_t)[:, 1, :], ALU.mult).then_inc(vecs.step("qk_odd"), 1)
                    for n in levels:
                        if n < LEVELS - 1:
                            v.wait_ge(pes.sem, pes.value(f"grow{n}", i=i))
                            tt(inv[:], inv[:], heads(ps[:, 4, :]),
                               ALU.subtract).then_inc(vecs.step(f"inverse{n}"), 1)
                        v.wait_ge(pes.sem, pes.value(f"grow_turned{n}", i=i))
                        tt(inv_t[:], inv_t[:], heads(ps[:, 5, :]),
                           ALU.subtract).then_inc(vecs.step(f"turned{n}"), 1)
                        if n == LEVELS - 1:
                            break
                        j = (n - 1) // 2
                        if n % 2:
                            v.wait_ge(pes.sem, pes.value(f"read{j}", i=i))
                            new_values(j, before).then_inc(vecs.step(f"v_new{j}"), 1)
                            fade(j, before).then_inc(vecs.step(f"fade{j}"), 1)
                        else:
                            v.wait_ge(pes.sem, pes.value(f"add{j}", i=i))
                            v.wait_ge(vecs.sem, vecs.value(f"fade{j}", i=i))
                            new_state(0).then_inc(vecs.step(f"state_a{j}"), 1)
                            new_state(1).then_inc(vecs.step(f"state_b{j}"), 1)
                    v.wait_ge(pes.sem, pes.value("uw", i=i))
                    nc.vector.tensor_copy(
                        w_ts[par][:], ps[:, 3, 256:512].rearrange("p (a n) -> p a n", a=2)).then_inc(
                        vecs.step("w"), 1)
                    nc.vector.tensor_copy(us[par][:], ps[:, 3, 0:256]).then_inc(vecs.step("u"), 1)
                blocks(v, body)

            @block.tensor
            def _(p):
                p.wait_ge(c.steps["dma"], d0 + 32)
                mm = nc.tensor.matmul
                spread_rows(slice(0, P)).then_inc(first_rows, 1)

                def body(i, par):
                    before = 1 - par
                    tok = toks[par]
                    p.wait_ge(vecs.sem, vecs.value_before("u", i))
                    p.wait_ge(act.sem, act.value("q", i=i))
                    p.wait_ge(vecs.sem, vecs.value("k_beta", i=i))
                    for h in range(HEADS):
                        bank, m = 3 + 2 * (h % 2), h // 2
                        to, to_2 = slice(m * P, (m + 1) * P), slice(256 + m * P, 384 + m * P)
                        mm(ps[:, bank, to], ks[hp(h), m, :], kb[hp(h), m, :], start=True, stop=True)
                        last = mm(ps[:, bank, to_2], kb[hp(h), m, :], ks[hp(h), m, :],
                                  start=True, stop=True)
                        if h % 2 == 0:
                            mm(ps[:, 4, to], ks[hp(h), m, :], qs[hp(h), m, :], start=True,
                               stop=True)
                    last.then_inc(pes.step("kk"), 1)
                    p.wait_ge(vecs.sem, vecs.value("ends", i=i))
                    for n, src in enumerate((kbe, kt, vb)):
                        for pair in range(2):
                            q = 2 * n + pair
                            last = nc.tensor.transpose(ps[:, q // 4, (q % 4) * P:(q % 4 + 1) * P],
                                                       src[:, pair, :], c.ident[:])
                    last.then_inc(pes.step("tok"), 1)
                    p.wait_ge(vecs.sem, vecs.value("diff", i=i))
                    for m in range(2):
                        last = mm(ps[:, 2, m * P:(m + 1) * P], ks[hp(1), m, :], qs[hp(1), m, :],
                                  start=True, stop=True)
                    last.then_inc(pes.step("qk_odd"), 1)
                    for n in levels:
                        p.wait_ge(pool.sem, pool.value(f"level{n}", i=i))
                        p.wait_ge(vecs.sem,
                                  vecs.value(f"inverse{n - 1}", i=i))
                        for h in range(HEADS):
                            last = mm(ps[:, 3, h * P:(h + 1) * P],
                                      a_lev[:, n - 1, h * P:(h + 1) * P], inv[:, h, :], start=True,
                                      stop=True)
                        last.then_inc(pes.step(f"a_inverse{n}"), 1)
                        j = (n - 1) // 2
                        if n < LEVELS - 1 and n % 2:
                            if j:
                                p.wait_ge(vecs.sem, vecs.value("state_b0", i=i))
                            else:
                                p.wait_ge(act.sem, act.value_before("out", i))
                            read(j, before).then_inc(pes.step(f"read{j}"), 1)
                        elif n < LEVELS - 1:
                            p.wait_ge(vecs.sem, vecs.value(f"v_new{j}", i=i))
                            add(j, before).then_inc(pes.step(f"add{j}"), 1)
                        else:
                            p.wait_ge(act.sem, act.value("values_tok", i=i))
                            spread_rows(bass.ds((i + 1) * P, P)).then_inc(
                                pes.step("next_rows"), 1)
                        p.wait_ge(act.sem, act.value(f"a_inverse{n}", i=i))
                        p.wait_ge(vecs.sem, vecs.value("qk_even" if n == 1 else f"turned{n - 1}",
                                                       i=i))
                        if n < LEVELS - 1:
                            for h in range(HEADS):
                                last = mm(ps[:, 4, h * P:(h + 1) * P], inv_t[:, h, :],
                                          prod[:, h, :], start=True, stop=True)
                            last.then_inc(pes.step(f"grow{n}"), 1)
                        for h in range(HEADS):
                            last = mm(ps[:, 5, h * P:(h + 1) * P], prod[:, h, :], inv_t[:, h, :],
                                      start=True, stop=True)
                        last.then_inc(pes.step(f"grow_turned{n}"), 1)
                    p.wait_ge(vecs.sem, vecs.value(f"turned{LEVELS - 1}", i=i))
                    p.wait_ge(act.sem, act.value("values_tok", i=i))
                    for h in range(HEADS):
                        mm(ps[:, 3, 64 * h:64 * h + 64], inv_t[:, place(h), :],
                           vb_tok[:, 64 * h:64 * h + 64], start=True, stop=True)
                        last = mm(ps[hp(h), 3, 256 + P * (h // 2):256 + P * (h // 2) + P],
                                  tok[:, 64 * h:64 * h + 64], inv_t[:, place(h), :],
                                  start=True, stop=True)
                    last.then_inc(pes.step("uw"), 1)
                blocks(p, body)
        for s in (act, vecs, pes, pool):
            s.end(BLK)

        pes = Steps(c, "pe", ["read0", "add0", "read1", "add1"])
        vecs = Steps(c, "vec", ["v_new0", "fade0", "state_a0", "state_b0", "v_new1"])
        act = Steps(c, "act", ["out"])
        par = (BLK - 1) % 2
        with nc.Block() as block:
            @block.tensor
            def _(p):
                read(0, par).then_inc(pes.step("read0"), 1)
                p.wait_ge(vecs.sem, vecs.value("v_new0"))
                add(0, par).then_inc(pes.step("add0"), 1)
                p.wait_ge(vecs.sem, vecs.value("state_b0"))
                read(1, par).then_inc(pes.step("read1"), 1)
                p.wait_ge(vecs.sem, vecs.value("v_new1"))
                add(1, par).then_inc(pes.step("add1"), 1)

            @block.vector
            def _(v):
                v.wait_ge(pes.sem, pes.value("read0"))
                new_values(0, par).then_inc(vecs.step("v_new0"), 1)
                fade(0, par).then_inc(vecs.step("fade0"), 1)
                v.wait_ge(pes.sem, pes.value("add0"))
                v.wait_ge(vecs.sem, vecs.value("fade0"))
                new_state(0).then_inc(vecs.step("state_a0"), 1)
                new_state(1).then_inc(vecs.step("state_b0"), 1)
                v.wait_ge(pes.sem, pes.value("read1"))
                new_values(1, par).then_inc(vecs.step("v_new1"), 1)

            @block.scalar
            def _(a):
                a.wait_ge(pes.sem, pes.value("add1"))
                nc.scalar.copy(o_tok[:, BLK, :], ps[:, 7, 0:256]).then_inc(act.step("out"), 1)
        for s in (act, vecs, pes):
            s.end()


def gated_linear(nc, c, t, hidden, small):
    with ExitStack() as ctx:
        proj = c.sb("gla_projected", [P, 6, S], ctx=ctx)
        project(nc, c, t["w_in"], 13, 6, hidden, proj, (t["w_in"], 19, KT))
        o_tok = c.sb("gla_out_tokens", [P, BLK, 256], ctx=ctx)
        with ExitStack() as inner:
            v_tok = c.sb("gla_value_tokens", [P, BLK, 256], ctx=inner)
            channels_to_tokens(nc, c, proj[:, 2:4, :], v_tok)
            q_in, k_in, k_tail = (c.sb(n, [P, S], ctx=inner)
                                  for n in ("gla_q_in", "gla_k_in", "gla_k_tail"))
            ends = c.sb("gla_chunk_decay", [P, S // CH], ctx=inner)
            gated_linear_inputs(nc, c, t, proj, small, q_in, k_in, k_tail, ends)
            gated_linear_chunks(nc, c, t, q_in, k_in, k_tail, ends, v_tok, o_tok)
        tokens_to_channels(nc, c, o_tok, t["branch"][2], gate=proj[:, 4:6, :],
                           gain=vec(c, "gla_norm"), norm=True)


def gated_linear_inputs(nc, c, t, proj, small, q_in, k_in, k_tail, ends):
    with ExitStack() as ctx:
        restart = c.sb("gla_chunk_restart", [P, S], ctx=ctx)
        gate_up = c.sb("gla_gate_up", [32, P], ctx=ctx)
        soft = c.sb("gla_softplus", [P, S], ctx=ctx)
        b = c.sb("gla_log_decay", [P, S], ctx=ctx)
        act = Steps(c, "act", ["abs", "exp", "ln", "grow", "shrink", "tail"])
        vecs = Steps(c, "vec", ["neg", "log", "sum", "to_end", "ends", "q_in", "k_in", "k_tail"])
        pes = Steps(c, "pe", ["gate"])
        d0 = c.base["dma"]
        c.base["dma"] += 32
        tau = 1.0 / 16
        with nc.Block() as block:
            @block.sync
            def _(sp):
                sp.dma_start(restart[:], t["restart"].partition_broadcast(P)).then_inc(
                    c.steps["dma"], 16)
                sp.dma_start(gate_up[:], t["gla_gate_up"]).then_inc(c.steps["dma"], 16)

            @block.tensor
            def _(p):
                p.wait_ge(c.steps["dma"], d0 + 32)
                for h in range(NH):
                    mm = nc.tensor.matmul(c.psum[:, h, :], gate_up[:],
                                          small[0:32, 1, h * HALF:(h + 1) * HALF], start=True,
                                          stop=True)
                mm.then_inc(pes.step("gate"), 1)

            @block.scalar
            def _(a):
                bias = vec(c, "gla_gate_bias")
                a.wait_ge(pes.sem, pes.value("gate"))
                nc.scalar.activation(soft[:], c.banks(0), ACT.Abs, bias=bias).then_inc(
                    act.step("abs"), 1)
                a.wait_ge(act.sem, act.value("abs"))
                nc.scalar.activation(soft[:], soft[:], ACT.Exp, scale=-1.0).then_inc(
                    act.step("exp"), 1)
                a.wait_ge(act.sem, act.value("exp"))
                nc.scalar.activation(soft[:], soft[:], ACT.Ln, bias=1.0).then_inc(act.step("ln"), 1)
                a.wait_ge(vecs.sem, vecs.value("sum"))
                nc.scalar.activation(q_in[:], b[:], ACT.Exp, scale=tau).then_inc(
                    act.step("grow"), 1)
                nc.scalar.activation(k_in[:], b[:], ACT.Exp, scale=-tau).then_inc(
                    act.step("shrink"), 1)
                a.wait_ge(vecs.sem, vecs.value("to_end"))
                nc.scalar.activation(k_tail[:], k_tail[:], ACT.Exp, scale=tau).then_inc(
                    act.step("tail"), 1)

            @block.vector
            def _(v):
                v.wait_ge(act.sem, act.value("abs"))
                nc.vector.tensor_scalar(b[:], c.banks(0), vec(c, "gla_gate_bias"),
                                        0.0, ALU.add, ALU.min).then_inc(vecs.step("neg"), 1)
                v.wait_ge(vecs.sem, vecs.value("neg"))
                v.wait_ge(act.sem, act.value("ln"))
                nc.vector.tensor_tensor(soft[:], b[:], soft[:], ALU.subtract).then_inc(
                    vecs.step("log"), 1)
                v.wait_ge(vecs.sem, vecs.value("log"))
                v.wait_ge(c.steps["dma"], d0 + 32)
                nc.vector.tensor_tensor_scan(b[:], restart[:], soft[:], 0.0,
                                             ALU.mult, ALU.add).then_inc(vecs.step("sum"), 1)
                v.wait_ge(vecs.sem, vecs.value("sum"))
                chunks = b[:].rearrange("p (n m) -> p n m", m=CH)
                nc.vector.tensor_tensor(
                    k_tail[:].rearrange("p (n m) -> p n m", m=CH),
                    chunks[:, :, CH - 1:CH].broadcast_to([P, S // CH, CH]), chunks, ALU.subtract).then_inc(
                    vecs.step("to_end"), 1)
                v.wait_ge(act.sem, act.value("grow"))
                nc.vector.tensor_copy(
                    ends[:], q_in[:].rearrange("p (n m) -> p n m", m=CH)[:, :, CH - 1]).then_inc(
                    vecs.step("ends"), 1)
                v.wait_ge(vecs.sem, vecs.value("ends"))
                nc.vector.scalar_tensor_tensor(q_in[:], q_in[:], GDK ** -0.5,
                                               proj[:, 0, :], ALU.mult, ALU.mult).then_inc(
                    vecs.step("q_in"), 1)
                v.wait_ge(act.sem, act.value("shrink"))
                nc.vector.tensor_tensor(k_in[:], k_in[:], proj[:, 1, :], ALU.mult).then_inc(
                    vecs.step("k_in"), 1)
                v.wait_ge(act.sem, act.value("tail"))
                nc.vector.tensor_tensor(k_tail[:], k_tail[:], proj[:, 1, :],
                                        ALU.mult).then_inc(vecs.step("k_tail"), 1)
        for s in (act, vecs, pes):
            s.end()


def gated_linear_chunks(nc, c, t, q_in, k_in, k_tail, ends, v_tok, o_tok):
    with ExitStack() as ctx:
        def sb(name, *shape):
            return c.sb("gla_" + name, [P, *shape], ctx=ctx)
        masks = sb("masks", P + 256)
        qb, kb, tb, vb = sb("q_block", P), sb("k_block", P), sb("tail_block", P), sb("v_block", 256)
        attn, tail_tok, added = sb("attention", HEADS, P), sb("tail_tokens", P), sb("added", 256)
        state = sb("state", 2, 256)
        act = Steps(c, "act", ["q", "v", "out"])
        vecs = Steps(c, "vec", ["k", "tail", "attn", "tail_tok", "added0", "state0", "added1",
                                "state1"])
        pes = Steps(c, "pe", ["attn", "turned", "kv0", "kv1", "read0", "read1", "out"])
        d0 = c.base["dma"]
        c.base["dma"] += 16
        z0 = c.base["pool"]
        c.base["pool"] += 1
        ps = c.psum
        with nc.Block() as block:
            @block.sync
            def _(sp):
                sp.dma_start(masks[:], t["gla_masks"]).then_inc(c.steps["dma"], 16)

            @block.gpsimd
            def _(g):
                nc.gpsimd.memset(state[:], 0.0).then_inc(c.steps["pool"], 1)

            @block.scalar
            def _(a):
                with a.Fori(0, BLK) as i:
                    a.wait_ge(pes.sem, pes.value_before("out", i))
                    nc.scalar.copy(qb[:], q_in[:, bass.ds(i * P, P)]).then_inc(act.step("q"), 1)
                    nc.scalar.copy(vb[:], v_tok[:, bass.ds(i, 1), :].rearrange(
                        "p b n -> p (b n)")).then_inc(act.step("v"), 1)
                    a.wait_ge(pes.sem, pes.value("out", i=i))
                    nc.scalar.copy(o_tok[:, bass.ds(i, 1), :].rearrange(
                        "p b n -> p (b n)"), ps[:, 7, 0:256]).then_inc(act.step("out"), 1)

            @block.vector
            def _(v):
                v.wait_ge(c.steps["dma"], d0 + 16)
                v.wait_ge(c.steps["pool"], z0 + 1)
                with v.Fori(0, BLK) as i:
                    v.wait_ge(pes.sem, pes.value_before("turned", i))
                    nc.vector.tensor_copy(kb[:], k_in[:, bass.ds(i * P, P)]).then_inc(
                        vecs.step("k"), 1)
                    nc.vector.tensor_copy(tb[:], k_tail[:, bass.ds(i * P, P)]).then_inc(
                        vecs.step("tail"), 1)
                    v.wait_ge(pes.sem, pes.value("attn", i=i))
                    v.wait_ge(pes.sem, pes.value_before("out", i))
                    nc.vector.tensor_tensor(
                        attn[:], ps[:, 0:4, 0:P], over_heads(masks[:, 0:P]), ALU.mult).then_inc(vecs.step("attn"), 1)
                    v.wait_ge(pes.sem, pes.value("turned", i=i))
                    nc.vector.tensor_copy(tail_tok[:], ps[:, 4, 0:P]).then_inc(
                        vecs.step("tail_tok"), 1)
                    for j in range(2):
                        v.wait_ge(pes.sem, pes.value(f"kv{j}", i=i))
                        if j:
                            v.wait_ge(vecs.sem, vecs.value("state0", i=i))
                        nc.vector.tensor_tensor(
                            added[:], ps[:, 5 + j, 0:256], masks[:, P:], ALU.mult).then_inc(vecs.step(f"added{j}"), 1)
                        v.wait_ge(vecs.sem, vecs.value(f"added{j}", i=i))
                        if j:
                            v.wait_ge(pes.sem, pes.value("read0", i=i))
                        nc.vector.scalar_tensor_tensor(
                            state[:, 1 - j, :], state[:, j, :], ends[:, bass.ds(2 * i + j, 1)],
                            added[:], ALU.mult, ALU.add).then_inc(vecs.step(f"state{j}"), 1)

            @block.tensor
            def _(p):
                p.wait_ge(c.steps["pool"], z0 + 1)
                with p.Fori(0, BLK) as i:
                    mm = nc.tensor.matmul
                    p.wait_ge(act.sem, act.value("q", i=i))
                    p.wait_ge(vecs.sem, vecs.value("k", i=i))
                    for h in range(HEADS):
                        r = slice(32 * h, 32 * h + 32)
                        last = mm(ps[:, h, 0:P], kb[r, :], qb[r, :], start=True, stop=True)
                    last.then_inc(pes.step("attn"), 1)
                    p.wait_ge(vecs.sem, vecs.value("tail", i=i))
                    nc.tensor.transpose(ps[:, 4, 0:P], tb[:], c.ident[:]).then_inc(
                        pes.step("turned"), 1)
                    p.wait_ge(vecs.sem, vecs.value("tail_tok", i=i))
                    p.wait_ge(act.sem, act.value("v", i=i))
                    for j in range(2):
                        r = slice(CH * j, CH * j + CH)
                        mm(ps[:, 5 + j, 0:256], tail_tok[r, :], vb[r, :],
                           start=True, stop=True).then_inc(pes.step(f"kv{j}"), 1)
                    p.wait_ge(act.sem, act.value_before("out", i))
                    p.wait_ge(vecs.sem, vecs.value_before("state1", i))
                    for j in range(2):
                        r = slice(CH * j, CH * j + CH)
                        if j:
                            p.wait_ge(vecs.sem, vecs.value("state0", i=i))
                        mm(ps[r, 7, 0:256], qb[:, r], state[:, j, :],
                           start=True, stop=False, skip_group_check=True).then_inc(
                            pes.step(f"read{j}"), 1)
                    p.wait_ge(vecs.sem, vecs.value("attn", i=i))
                    for h in range(HEADS):
                        to = slice(64 * h, 64 * h + 64)
                        last = mm(ps[:, 7, to], attn[:, h, :], vb[:, to], start=False,
                                  stop=(h == HEADS - 1), skip_group_check=True)
                    last.then_inc(pes.step("out"), 1)
        for s in (act, vecs, pes):
            s.end(BLK)


def latent_attention(nc, c, t, hidden, small):
    with ExitStack() as ctx:
        o_tok = c.sb("mla_out_tokens", [P, BLK, 256], ctx=ctx)
        v_tok = c.sb("mla_value_tokens", [P, BLK, 256], ctx=ctx)
        q, k = (c.sb(n, [P, HEADS, S], ctx=ctx) for n in ("mla_q", "mla_k"))
        with ExitStack() as inner:
            latent = c.sb("mla_latent", [P, 3, S], ctx=inner)
            project(nc, c, t["w_in"], 10, 3, hidden, latent)
            latent_inputs(nc, c, t, latent, small, q, k, v_tok)
        attend(nc, c, t, 0, 96, q, k, v_tok, o_tok)
        tokens_to_channels(nc, c, o_tok, t["branch"][1])


def latent_inputs(nc, c, t, latent, small, q, k, v_tok):
    with ExitStack() as ctx:
        sq = c.sb("mla_squares", [P, 3, S], ctx=ctx)
        root = c.sb("mla_norms", [P, 2, S], ctx=ctx)
        rope = c.sb("mla_rope", [P, S], ctx=ctx)
        part = c.sb("mla_rotated", [P, 3, S], ctx=ctx)
        w_q = c.sb("mla_w_q", [P, 2, HEADS * P], ctx=ctx)
        w_kv = c.sb("mla_w_kv", [P, 512], ctx=ctx)
        act = Steps(c, "act", [("square", 3), ("root", 2), ("k", HEADS), ("plain", HEADS),
                               ("k_pe", HEADS)])
        vecs = Steps(c, "vec", ["pe_cos", "pe_sin", "pe", ("rstd", 2), ("unit", 3),
                                (("cos", "sin", "rot"), HEADS), ("v", 4)])
        pes = Steps(c, "pe", [("sums", 2), ("k", 2), ("q", HEADS), ("v", 4)])
        d0 = c.base["dma"]
        c.base["dma"] += 48
        cosr, sinr = slice(64, 96), slice(96, 128)
        scale = (DH + ROPE) ** -0.5
        with nc.Block() as block:
            @block.sync
            def _(sp):
                for dst, src in ((rope[:], t["rope"]), (w_q[:], t["mla_w_q"]),
                                 (w_kv[:], t["mla_w_kv"])):
                    sp.dma_start(dst, src).then_inc(c.steps["dma"], 16)

            @block.scalar
            def _(a):
                for n in range(3):
                    nc.scalar.activation(sq[:, n, :], latent[:, n, :], ACT.Square).then_inc(
                        act.step("square"), 1)
                for n in range(2):
                    a.wait_ge(pes.sem, pes.value("sums", n))
                    nc.scalar.activation(root[:, n, :], c.banks(2 * n), ACT.Sqrt,
                                         scale=1.0 / (256 if n == 0 else 128),
                                         bias=c.eps[:, 0:1]).then_inc(act.step("root"), 1)
                for h in range(HEADS):
                    a.wait_ge(pes.sem, pes.value("k", h // 2))
                    r = slice(64 * (h % 2), 64 * (h % 2) + 64)
                    nc.scalar.copy(k[0:64, h, :], c.banks(4 + 2 * (h // 2))[r, :]).then_inc(
                        act.step("k"), 1)
                for h in range(HEADS):
                    a.wait_ge(pes.sem, pes.value("q", h))
                    nc.scalar.mul(q[0:64, h, :], c.banks(2 * (h % 2))[0:64, :],
                                   scale).then_inc(act.step("plain"), 1)
                a.wait_ge(vecs.sem, vecs.value("pe"))
                for h in range(HEADS):
                    nc.scalar.copy(k[cosr, h, :], part[cosr, 0, :]).then_inc(act.step("k_pe"), 1)

            @block.vector
            def _(v):
                mult = lambda out, x, y: nc.vector.tensor_tensor(out, x, y, ALU.mult)
                v.wait_ge(c.steps["dma"], d0 + 48)
                mult(part[cosr, 0, :], small[cosr, 0, :], rope[cosr, :]).then_inc(
                    vecs.step("pe_cos"), 1)
                mult(part[cosr, 1, :], small[sinr, 0, :], rope[sinr, :]).then_inc(
                    vecs.step("pe_sin"), 1)
                v.wait_ge(vecs.sem, vecs.value("pe_sin"))
                nc.vector.tensor_tensor(part[cosr, 0, :], part[cosr, 0, :],
                                        part[cosr, 1, :], ALU.add).then_inc(vecs.step("pe"), 1)
                for n in range(2):
                    v.wait_ge(act.sem, act.value("root", n))
                    nc.vector.reciprocal(root[:, n, :], root[:, n, :]).then_inc(
                        vecs.step("rstd"), 1)
                v.wait_ge(vecs.sem, vecs.value("rstd"))
                for n in range(3):
                    gain = vec(c, "mla_q_norm", n) if n < 2 else vec(c, "mla_kv_norm")
                    nc.vector.scalar_tensor_tensor(
                        latent[:, n, :], latent[:, n, :], gain, root[:, n // 2, :], ALU.mult,
                        ALU.mult).then_inc(vecs.step("unit"), 1)
                for h in range(HEADS):
                    v.wait_ge(pes.sem, pes.value("q", h))
                    b = c.banks(2 * (h % 2))
                    nc.vector.scalar_tensor_tensor(
                        q[cosr, h, :], b[cosr, :], scale, rope[cosr, :], ALU.mult, ALU.mult).then_inc(
                        vecs.step("cos"), 1)
                    if h:
                        v.wait_ge(vecs.sem, vecs.value("rot", h - 1))
                    nc.vector.scalar_tensor_tensor(
                        part[cosr, 2, :], b[sinr, :], scale, rope[sinr, :], ALU.mult, ALU.mult).then_inc(
                        vecs.step("sin"), 1)
                    v.wait_ge(vecs.sem, vecs.value("sin", h))
                    nc.vector.tensor_tensor(q[cosr, h, :], q[cosr, h, :],
                                            part[cosr, 2, :], ALU.add).then_inc(vecs.step("rot"), 1)
                for g in range(4):
                    v.wait_ge(pes.sem, pes.value("v", g))
                    nc.vector.tensor_copy(
                        v_tok[:, 2 * g:2 * g + 2, :].rearrange("p b n -> p (b n)"), c.psum[:, g, :]).then_inc(
                        vecs.step("v"), 1)

            @block.tensor
            def _(p):
                mm = nc.tensor.matmul
                p.wait_ge(act.sem, act.value("square"))
                for h in range(NH):
                    cols = slice(h * HALF, (h + 1) * HALF)
                    for n in range(2):
                        last = mm(c.psum[:, h, :], c.ones[:], sq[:, n, cols], start=(n == 0),
                                  stop=(n == 1))
                last.then_inc(pes.step("sums"), 1)
                for h in range(NH):
                    last = mm(c.psum[:, 2 + h, :], c.ones[:], sq[:, 2, h * HALF:(h + 1) * HALF],
                              start=True, stop=True)
                last.then_inc(pes.step("sums"), 1)
                p.wait_ge(vecs.sem, vecs.value("unit"))
                p.wait_ge(c.steps["dma"], d0 + 48)
                for n in range(2):
                    for x in range(NH):
                        last = mm(c.psum[:, 4 + 2 * n + x, :], w_kv[:, n * P:(n + 1) * P],
                                  latent[:, 2, x * HALF:(x + 1) * HALF], start=True, stop=True)
                    last.then_inc(pes.step("k"), 1)
                for h in range(HEADS):
                    if h >= 2:
                        p.wait_ge(act.sem, act.value("plain", h - 2))
                        p.wait_ge(vecs.sem, vecs.value("sin", h - 2))
                    for x in range(NH):
                        for n in range(2):
                            last = mm(c.psum[:, 2 * (h % 2) + x, :], w_q[:, n, h * P:(h + 1) * P],
                                      latent[:, n, x * HALF:(x + 1) * HALF], start=(n == 0),
                                      stop=(n == 1))
                    last.then_inc(pes.step("q"), 1)
                p.wait_ge(act.sem, act.value("plain"))
                p.wait_ge(vecs.sem, vecs.value("sin"))
                for g in range(4):
                    for q2 in range(2):
                        b = 2 * g + q2
                        last = mm(c.psum[:, g, q2 * 256:(q2 + 1) * 256],
                                  latent[:, 2, b * P:(b + 1) * P], w_kv[:, 256:512], start=True,
                                  stop=True)
                    last.then_inc(pes.step("v"), 1)
        for s in (act, vecs, pes):
            s.end()


def forgetting_attention(nc, c, t, hidden, small):
    with ExitStack() as ctx:
        o_tok = c.sb("fox_out_tokens", [P, BLK, 256], ctx=ctx)
        v_tok = c.sb("fox_value_tokens", [P, BLK, 256], ctx=ctx)
        q, k = (c.sb(n, [P, HEADS, S], ctx=ctx) for n in ("fox_q", "fox_k"))
        with ExitStack() as inner:
            proj = c.sb("fox_projected", [P, 6, S], ctx=inner)
            project(nc, c, t["w_in"], 19, 6, hidden, proj, (t["w_gate"], 0, WK))
            channels_to_tokens(nc, c, proj[:, 4:6, :], v_tok)
            forgetting_inputs(nc, c, proj, small, q, k)
        attend(nc, c, t, 1, 97, q, k, v_tok, o_tok)
        tokens_to_channels(nc, c, o_tok, t["branch"][3])


def forgetting_inputs(nc, c, proj, small, q, k):
    with ExitStack() as ctx:
        soft = c.sb("fox_softplus", [P, S], ctx=ctx)
        ones = c.sb("fox_ones", [P, S], ctx=ctx)
        total = c.sb("fox_forget_sum", [P, S], ctx=ctx)
        act = Steps(c, "act", ["abs", "exp", "ln", ("q", HEADS), ("k", HEADS), ("f_q", HEADS),
                               ("f_k", HEADS)])
        vecs = Steps(c, "vec", ["neg", "log", "sum"])
        pool = Steps(c, "pool", ["ones", "q_zero", "k_zero", "q_one", "k_one"])
        f, bias = small[:, 1, :], vec(c, "fox_f_bias")
        with nc.Block() as block:
            @block.gpsimd
            def _(g):
                nc.gpsimd.memset(ones[:], 1.0).then_inc(pool.step("ones"), 1)
                g.wait_ge(pool.sem, pool.value("ones"))
                nc.gpsimd.memset(q[64:97, :, :], 0.0).then_inc(pool.step("q_zero"), 1)
                g.wait_ge(pool.sem, pool.value("q_zero"))
                nc.gpsimd.memset(k[64:97, :, :], 0.0).then_inc(pool.step("k_zero"), 1)
                g.wait_ge(pool.sem, pool.value("k_zero"))
                nc.gpsimd.memset(q[96:97, :, :], 1.0).then_inc(pool.step("q_one"), 1)
                g.wait_ge(pool.sem, pool.value("q_one"))
                nc.gpsimd.memset(k[64:65, :, :], 1.0).then_inc(pool.step("k_one"), 1)

            @block.scalar
            def _(a):
                nc.scalar.activation(soft[:], f, ACT.Abs, bias=bias).then_inc(act.step("abs"), 1)
                a.wait_ge(act.sem, act.value("abs"))
                nc.scalar.activation(soft[:], soft[:], ACT.Exp, scale=-1.0).then_inc(
                    act.step("exp"), 1)
                a.wait_ge(act.sem, act.value("exp"))
                nc.scalar.activation(soft[:], soft[:], ACT.Ln, bias=1.0).then_inc(act.step("ln"), 1)
                for h in range(HEADS):
                    r = slice(64 * (h % 2), 64 * (h % 2) + 64)
                    nc.scalar.mul(q[0:64, h, :], proj[r, h // 2, :], DH ** -0.5).then_inc(
                        act.step("q"), 1)
                for h in range(HEADS):
                    r = slice(64 * (h % 2), 64 * (h % 2) + 64)
                    nc.scalar.copy(k[0:64, h, :], proj[r, 2 + h // 2, :]).then_inc(act.step("k"), 1)
                a.wait_ge(vecs.sem, vecs.value("sum"))
                a.wait_ge(pool.sem, pool.value("k_one"))
                for h in range(HEADS):
                    nc.scalar.copy(q[64:65, h, :], total[32 * h:32 * h + 1, :]).then_inc(
                        act.step("f_q"), 1)
                for h in range(HEADS):
                    nc.scalar.mul(k[96:97, h, :], total[32 * h:32 * h + 1, :], -1.0).then_inc(
                        act.step("f_k"), 1)

            @block.vector
            def _(v):
                nc.vector.tensor_scalar(total[:], f, bias, 0.0, ALU.add, ALU.min).then_inc(
                    vecs.step("neg"), 1)
                v.wait_ge(vecs.sem, vecs.value("neg"))
                v.wait_ge(act.sem, act.value("ln"))
                nc.vector.tensor_tensor(soft[:], total[:], soft[:], ALU.subtract).then_inc(
                    vecs.step("log"), 1)
                v.wait_ge(vecs.sem, vecs.value("log"))
                v.wait_ge(pool.sem, pool.value("ones"))
                nc.vector.tensor_tensor_scan(total[:], ones[:], soft[:], 0.0,
                                             ALU.mult, ALU.add).then_inc(vecs.step("sum"), 1)
        for s in (act, vecs, pool):
            s.end()


def attend(nc, c, t, which_mask, rows, q, k, v_tok, o_tok):
    with ExitStack() as ctx:
        mask = c.sb("attention_mask", [P, P], ctx=ctx)
        prob = c.sb("attention_probs", [P, 2, S], ctx=ctx)
        turned = c.sb("attention_probs_turned", [P, 2, S], ctx=ctx)
        neg_max = c.sb("attention_neg_max", [P, 2], ctx=ctx)
        sums = c.sb("attention_sums", [P, BLK * HEADS], ctx=ctx)
        turns = range(BLK * HEADS)
        last_turn = turns[-1]
        pe_spec, act_spec, vec_spec = ["scores0"], [], []
        for n in range(len(turns) + 1):
            if n < last_turn:
                pe_spec.append(f"scores{n + 1}")
            if n <= last_turn:
                pe_spec.append(f"turned{n}")
                act_spec += [f"exp{n}", f"low{n}"]
                vec_spec += [f"mask{n}", f"max{n}"]
                if n // 4 >= 4:
                    vec_spec.append(f"high{n}")
            if n:
                pe_spec.append(f"values{n - 1}")
                if n % 4 == 0:
                    vec_spec += [f"inverse{n // 4 - 1}", f"out{n // 4 - 1}"]
        pes, act = Steps(c, "pe", pe_spec), Steps(c, "act", act_spec)
        vecs = Steps(c, "vec", vec_spec)
        d0 = c.base["dma"]
        c.base["dma"] += 16

        def scores(n, keys):
            return c.banks(2 * (n % 2))[:, keys]

        with nc.Block() as block:
            @block.sync
            def _(sp):
                sp.dma_start(mask[:], t["attention_masks"][:, which_mask, :]).then_inc(
                    c.steps["dma"], 16)

            @block.scalar
            def _(a):
                for n in turns:
                    nk = (n // 4 + 1) * P
                    a.wait_ge(vecs.sem, vecs.value(f"max{n}"))
                    if n >= 2:
                        a.wait_ge(pes.sem, pes.value(f"turned{n - 2}"))
                    nc.scalar.activation(
                        prob[:, n % 2, 0:nk], scores(n, slice(0, nk)), ACT.Exp,
                        bias=neg_max[:, n % 2:n % 2 + 1], accum_out=sums[:, n:n + 1]).then_inc(act.step(f"exp{n}"), 1)
                    a.wait_ge(pes.sem, pes.value(f"turned{n}"))
                    if n >= 2:
                        a.wait_ge(pes.sem, pes.value(f"values{n - 2}"))
                    m = min(nk, HALF)
                    nc.scalar.copy(turned[:, n % 2, 0:m], c.psum[:, 4, 0:m]).then_inc(
                        act.step(f"low{n}"), 1)

            @block.vector
            def _(v):
                v.wait_ge(c.steps["dma"], d0 + 16)

                def finish(b):
                    s = slice(4 * b, 4 * b + 4)
                    v.wait_ge(act.sem, act.value(f"exp{4 * b + 3}"))
                    nc.vector.reciprocal(sums[:, s], sums[:, s]).then_inc(
                        vecs.step(f"inverse{b}"), 1)
                    v.wait_ge(pes.sem, pes.value(f"values{4 * b + 3}"))
                    v.wait_ge(vecs.sem, vecs.value(f"inverse{b}"))
                    nc.vector.tensor_tensor(
                        heads(o_tok[:, b, :]), heads(c.psum[:, 6 + b % 2, 0:256]),
                        bcast(sums[:, s], DH), ALU.mult).then_inc(vecs.step(f"out{b}"), 1)

                for n in turns:
                    nk = (n // 4 + 1) * P
                    v.wait_ge(pes.sem, pes.value(f"scores{n}"))
                    own = scores(n, slice(nk - P, nk))
                    nc.vector.tensor_tensor(own, own, mask[:], ALU.add).then_inc(
                        vecs.step(f"mask{n}"), 1)
                    v.wait_ge(vecs.sem, vecs.value(f"mask{n}"))
                    if n >= 2:
                        v.wait_ge(act.sem, act.value(f"exp{n - 2}"))
                    nc.vector.tensor_reduce(
                        neg_max[:, n % 2:n % 2 + 1], scores(n, slice(0, nk)), AX_X, ALU.max,
                        negate=True).then_inc(vecs.step(f"max{n}"), 1)
                    if n // 4 >= 4:
                        v.wait_ge(pes.sem, pes.value(f"turned{n}"))
                        if n >= 2:
                            v.wait_ge(pes.sem, pes.value(f"values{n - 2}"))
                        nc.vector.tensor_copy(
                            turned[:, n % 2, HALF:nk], c.psum[:, 5, 0:nk - HALF]).then_inc(vecs.step(f"high{n}"), 1)
                    if n and n % 4 == 0:
                        finish(n // 4 - 1)
                finish(BLK - 1)

            @block.tensor
            def _(p):
                mm = nc.tensor.matmul

                def score(n):
                    b, h = n // 4, n % 4
                    if n >= 2:
                        p.wait_ge(act.sem, act.value(f"exp{n - 2}"))
                    for x in range(0, (b + 1) * P, HALF):
                        m = min(HALF, (b + 1) * P - x)
                        last = mm(c.psum[:, 2 * (n % 2) + x // HALF, 0:m],
                                  q[0:rows, h, b * P:(b + 1) * P], k[0:rows, h, x:x + m],
                                  start=True, stop=True)
                    last.then_inc(pes.step(f"scores{n}"), 1)

                score(0)
                for n in range(len(turns) + 1):
                    if n < last_turn:
                        score(n + 1)
                    if n <= last_turn:
                        p.wait_ge(act.sem, act.value(f"exp{n}"))
                        if n:
                            p.wait_ge(act.sem, act.value(f"low{n - 1}"))
                            if (n - 1) // 4 >= 4:
                                p.wait_ge(vecs.sem, vecs.value(f"high{n - 1}"))
                        for x in range(n // 4 + 1):
                            last = nc.tensor.transpose(
                                c.psum[:, 4 + x // 4, x % 4 * P:(x % 4 + 1) * P],
                                prob[:, n % 2, x * P:(x + 1) * P], c.ident[:])
                        last.then_inc(pes.step(f"turned{n}"), 1)
                    if n:
                        m = n - 1
                        b, h = m // 4, m % 4
                        p.wait_ge(act.sem, act.value(f"low{m}"))
                        if b >= 4:
                            p.wait_ge(vecs.sem, vecs.value(f"high{m}"))
                        if b >= 2 and h == 0:
                            p.wait_ge(vecs.sem, vecs.value(f"out{b - 2}"))
                        for x in range(b + 1):
                            last = mm(c.psum[:, 6 + b % 2, 64 * h:64 * h + 64],
                                      turned[:, m % 2, x * P:(x + 1) * P],
                                      v_tok[:, x, 64 * h:64 * h + 64], start=(x == 0),
                                      stop=(x == b))
                        last.then_inc(pes.step(f"values{m}"), 1)
        for s in (act, vecs, pes):
            s.end()


def gate_and_merge(nc, c, t, hidden, merged_ctx):
    with ExitStack() as ctx:
        o = c.sb("branches", [P, 8, 2, S], F32R, ctx=ctx)
        with ExitStack() as inner:
            plain = c.sb("branch_plain", [P, 4, 2, S], ctx=inner)
            act, vecs = Steps(c, "act", [("high", 4)]), Steps(c, "vec", [("low", 4)])
            loaded = [c.sem(f"branch_loaded_{i}") for i in range(4)]
            with nc.Block() as block:
                @block.sync
                def _(sp):
                    for i in range(4):
                        sp.dma_start(plain[:, i], t["branch"][i]).then_inc(loaded[i], 16)

                @block.scalar
                def _(a):
                    for i in range(4):
                        a.wait_ge(loaded[i], 16)
                        nc.scalar.copy(o[:, 2 * i:2 * i + 2, 0, :],
                                       plain[:, i]).then_inc(act.step("high"), 1)

                @block.vector
                def _(v):
                    for i in range(4):
                        v.wait_ge(act.sem, act.value("high", i))
                        nc.vector.tensor_tensor(o[:, 2 * i:2 * i + 2, 1, :], plain[:, i],
                                                o[:, 2 * i:2 * i + 2, 0, :].bitcast(F32),
                                                ALU.subtract).then_inc(vecs.step("low"), 1)
            act.end()
            vecs.end()
        merged = c.sb("merged", [P, KT, S], ctx=merged_ctx, side="right")
        gate = c.sb("gate", [P, 2, S], ctx=ctx)
        start = VECTORS["b_gate"][0]

        def sigmoid(act, u, s, result, act_count, dve_count, q, j):
            if not isinstance(u, int) or u >= 2:
                act.wait_ge(c.dve_done, dve_count(u - 2, 1))
            nc.scalar.activation(gate[:, s, :], result, ACT.Sigmoid,
                                 bias=c.vectors[:, bass.ds(u + start, 1)]).then_inc(c.act_done, 1)

        def add(dve, u, s, result, act_count, dve_count, q, j):
            dve.wait_ge(c.act_done, act_count(u))
            out = merged[:, bass.ds(j, 1), :].rearrange("p a n -> p (a n)")
            to = gate[:, s, :] if q else out
            nc.vector.tensor_tensor(to, gate[:, s, :], c.banks(4 + 2 * s),
                                    ALU.mult).then_inc(c.dve_done, 1 if q else 2)
            if q:
                dve.wait_ge(c.dve_done, dve_count(u))
                nc.vector.tensor_tensor(out, out, gate[:, s, :], ALU.add).then_inc(c.dve_done, 1)

        gemm(nc, c, t["w_gate"], 32, KT, lambda k, x, h: hidden[:, k, x, h * HALF:(h + 1) * HALF],
             act_per_unit=1, act_epilogue=sigmoid, dve_per_unit=2, dve_epilogue=add,
             banks_read_by="dve", unroll=4, extra_kt=2, then=(t["w_out"], 0, KT),
             extra_rhs=lambda k, x, h, i: o[:, 2 * i + k, x, h * HALF:(h + 1) * HALF])
        return merged


def split(nc, c, src, dst, wait=None, meanwhile=None):
    n = src.shape[1]
    act, vecs = Steps(c, "act", [("high", n)]), Steps(c, "vec", [("low", n)])
    with nc.Block() as block:
        if meanwhile:
            @block.sync
            def _(sp):
                meanwhile(sp)

        @block.scalar
        def _(a):
            for k in range(n):
                if wait:
                    wait(c, a, k)
                nc.scalar.copy(dst[:, k, 0, :], src[:, k, :]).then_inc(act.step("high"), 1)

        @block.vector
        def _(v):
            for k in range(n):
                if wait:
                    wait(c, v, k)
                v.wait_ge(act.sem, act.value("high", k))
                nc.vector.tensor_tensor(dst[:, k, 1, :], src[:, k, :],
                                        dst[:, k, 0, :].bitcast(F32), ALU.subtract).then_inc(
                                            vecs.step("low"), 1)
    act.end()
    vecs.end()


def one(tile, u):
    return tile[:, bass.ds(u, 1), :].rearrange("p a n -> p (a n)")


def sum_squares(nc, c, y, sq, total, add):
    def square(act, u, s, result, act_count, dve_count, q, j):
        if not isinstance(u, int) or u >= 2:
            act.wait_ge(c.dve_done, dve_count(u - 2, 1))
        act.wait_ge(c.dve_done, dve_count(u, 0))
        nc.scalar.activation(sq[:, s, :], one(y, u), ACT.Square).then_inc(c.act_done, 1)

    def keep(dve, u, s, result, act_count, dve_count, q, j):
        if add:
            nc.vector.tensor_tensor(one(y, u), one(y, u), result, ALU.add).then_inc(c.dve_done, 1)
        else:
            nc.vector.tensor_copy(one(y, u), result).then_inc(c.dve_done, 1)
        dve.wait_ge(c.act_done, act_count(u))
        if not isinstance(u, int) or u:
            dve.wait_ge(c.dve_done, dve_count(u - 1, 1))
        nc.vector.tensor_tensor(total[:], total[:], sq[:, s, :], ALU.add).then_inc(c.dve_done, 1)
    return dict(act_per_unit=1, act_epilogue=square, dve_per_unit=2, dve_epilogue=keep,
                banks_read_by="dve", background=clearing(nc, c, total[:]))


def clearing(nc, c, tile):
    vecs = Steps(c, "vec", ["zero"])
    vecs.end()

    def clear(dve, q, j):
        if isinstance(j, int) and j == 0 and q == 0:
            nc.vector.memset(tile, 0.0).then_inc(vecs.step("zero"), 1)
            dve.wait_ge(vecs.sem, vecs.value("zero"))
    return {"dve": clear}


def add_residual(nc, c, t, y, total, factor, x_tokens, x_dram, keep_dram, out=None, times=None,
                 plus=None, defer=False, loaded=None):
    with ExitStack() as ctx:
        x = loaded if loaded is not None else c.sb("residual_in", [P, KT, S], ctx=ctx)
        sq = c.sb("residual_squares", [P, 2, S], ctx=ctx)
        rstd = c.sb("residual_rstd", [P, 2, S], ctx=ctx)
        normed = c.sb("residual_normed", [P, 2, S], ctx=ctx)
        if defer:
            tail = []
        else:
            tail = ["normed0"] + [f"{n}" for k in range(1, KT)
                                  for n in (f"normed{k}", f"low{k - 1}")] + [f"low{KT - 1}"]
        where = total[:] if defer else rstd[:, 1, :]
        act = Steps(c, "act", ["root1"]
                    + [(("square", "high") if defer else "square", KT), "root2"]
                    + ([] if defer else [("high", KT)]))
        adds = sum([[f"scaled{k}"] + ([f"added{k - 1}"] if k else [])
                    + ([f"low{k - 2}"] if defer and k > 1 else []) for k in range(KT)], [])
        adds += [f"added{KT - 1}"] + ([f"low{KT - 2}", f"low{KT - 1}"] if defer else [])
        vecs = Steps(c, "vec", ["rstd1"] + adds + ([] if defer else ["rstd2"]) + tail)
        turns = KT if x_tokens is not None else 0
        order = sum([([f"turned{k}"] if k < turns else []) + ([f"sum2{k - 3}"] if k > 2 else [])
                     for k in range(KT + 3)], [])
        pes = Steps(c, "pe", ["sum1"] + order)
        ps = c.psum
        with nc.Block() as block:
            @block.sync
            def _(sp):
                if loaded is None:
                    load_residual(c, sp, x, x_dram if x_tokens is None else x_tokens,
                                  x_tokens is not None)
                if keep_dram is not None:
                    sp.wait_ge(vecs.sem, vecs.value(f"added{KT - 1}"))
                    store(c, sp, keep_dram, y[:])
                    sp.wait_ge(c.scratch_stored, c.stored)

            @block.scalar
            def _(a):
                def root(name, bank, to):
                    nc.scalar.activation(to, c.banks(bank), ACT.Sqrt,
                                         scale=1.0 / D, bias=c.eps[:, 0:1]).then_inc(
                        act.step(name), 1)
                a.wait_ge(pes.sem, pes.value("sum1"))
                root("root1", 0, rstd[:, 0, :])
                for k in range(KT):
                    a.wait_ge(vecs.sem, vecs.value(f"added{k}"))
                    if k >= 2:
                        a.wait_ge(pes.sem, pes.value(f"sum2{k - 2}"))
                    nc.scalar.activation(sq[:, k % 2, :], y[:, k, :], ACT.Square).then_inc(
                        act.step("square"), 1)
                    if defer:
                        nc.scalar.activation(out[:, k, 0, :], y[:, k, :], ACT.Copy,
                                             scale=times(k)).then_inc(act.step("high"), 1)
                a.wait_ge(pes.sem, pes.value(f"sum2{KT - 1}"))
                root("root2", 6, where)
                if not defer:
                    for k in range(KT):
                        a.wait_ge(vecs.sem, vecs.value(f"normed{k}"))
                        if plus is None:
                            nc.scalar.copy(out[:, k, 0, :], normed[:, k % 2, :]).then_inc(
                                act.step("high"), 1)
                        else:
                            nc.scalar.activation(
                                out[:, k, 0, :], normed[:, k % 2, :], ACT.Identity, bias=plus(k)).then_inc(
                                act.step("high"), 1)

            @block.vector
            def _(v):
                v.wait_ge(act.sem, act.value("root1"))
                nc.vector.reciprocal(rstd[:, 0, :], rstd[:, 0, :]).then_inc(
                    vecs.step("rstd1"), 1)
                v.wait_ge(vecs.sem, vecs.value("rstd1"))
                stt = nc.vector.scalar_tensor_tensor

                def added(k):
                    v.wait_ge(vecs.sem, vecs.value(f"scaled{k}"))
                    if x_tokens is not None:
                        v.wait_ge(pes.sem, pes.value(f"turned{k}"))
                        other = c.banks(2 + 2 * (k % 2))
                    else:
                        wait_residual(c, v, k)
                        other = x[:, k, :]
                    nc.vector.tensor_tensor(y[:, k, :], y[:, k, :], other,
                                            ALU.add).then_inc(vecs.step(f"added{k}"), 1)

                def low_deferred(k):
                    v.wait_ge(act.sem, act.value("high", k))
                    stt(out[:, k, 1, :], y[:, k, :], times(k),
                        out[:, k, 0, :].bitcast(F32), ALU.mult, ALU.subtract).then_inc(
                        vecs.step(f"low{k}"), 1)
                for k in range(KT + 2):
                    if k < KT:
                        stt(y[:, k, :], y[:, k, :], factor(k),
                            rstd[:, 0, :], ALU.mult, ALU.mult).then_inc(
                            vecs.step(f"scaled{k}"), 1)
                    if 0 < k <= KT:
                        added(k - 1)
                    if defer and k > 1:
                        low_deferred(k - 2)
                if not defer:
                    v.wait_ge(act.sem, act.value("root2"))
                    nc.vector.reciprocal(where, where).then_inc(vecs.step("rstd2"), 1)
                    v.wait_ge(vecs.sem, vecs.value("rstd2"))

                def low(k):
                    v.wait_ge(act.sem, act.value("high", k))
                    high = out[:, k, 0, :].bitcast(F32)
                    if plus is None:
                        nc.vector.tensor_tensor(
                            out[:, k, 1, :], normed[:, k % 2, :], high, ALU.subtract).then_inc(vecs.step(f"low{k}"), 1)
                    else:
                        stt(out[:, k, 1, :], normed[:, k % 2, :], plus(k),
                            high, ALU.add, ALU.subtract).then_inc(vecs.step(f"low{k}"), 1)
                for k in range(0 if defer else KT):
                    if k >= 2:
                        v.wait_ge(vecs.sem, vecs.value(f"low{k - 2}"))
                    stt(normed[:, k % 2, :], y[:, k, :], times(k),
                        rstd[:, 1, :], ALU.mult, ALU.mult).then_inc(vecs.step(f"normed{k}"), 1)
                    if k:
                        low(k - 1)
                if not defer:
                    low(KT - 1)

            @block.tensor
            def _(p):
                mm = nc.tensor.matmul
                for h in range(NH):
                    last = mm(ps[:, h, :], c.ones[:], total[:, h * HALF:(h + 1) * HALF],
                              start=True, stop=True)
                last.then_inc(pes.step("sum1"), 1)

                def turn(k):
                    if k >= 2:
                        p.wait_ge(vecs.sem, vecs.value(f"added{k - 2}"))
                    if k % 4 == 0:
                        wait_residual(c, p, k)
                    for b in range(BLK):
                        last = nc.tensor.transpose(
                            ps[:, 2 + 2 * (k % 2) + b // 4, b % 4 * P:(b % 4 + 1) * P],
                            x[:, b, k * P:(k + 1) * P], c.ident[:])
                    last.then_inc(pes.step(f"turned{k}"), 1)

                def add(k):
                    p.wait_ge(act.sem, act.value("square", k))
                    for h in range(NH):
                        last = mm(ps[:, 6 + h, :], c.ones[:], sq[:, k % 2, h * HALF:(h + 1) * HALF],
                                  start=(k == 0), stop=(k == KT - 1))
                    last.then_inc(pes.step(f"sum2{k}"), 1)
                for k in range(KT + 3):
                    if k < turns:
                        turn(k)
                    if k > 2:
                        add(k - 3)
        for s in (act, vecs, pes):
            s.end()


def load_residual(c, sp, x, source, tokens):
    for n in range(2):
        c.residuals[n] += 16
        at = slice(n * HALF, (n + 1) * HALF) if tokens else slice(n * KT // 2, (n + 1) * KT // 2)
        to, src = (x[:, :, at], source[:, :, at]) if tokens else (x[:, at, :], source[:, at, :])
        sp.dma_start(to, src).then_inc(c.residual_loaded[n], 16)


def wait_residual(c, eng, k):
    n = k * 2 // KT
    eng.wait_ge(c.residual_loaded[n], c.residuals[n])


FF_CHUNKS = 4


def mlp(nc, c, t, h, y, total, sq):
    rstd = total[:]
    with ExitStack() as ctx:
        u_parts = c.sb("mlp_hidden", [P, KT, 2, S], F32R, ctx=ctx)

        def relu(dve, u, s, result, act_count, dve_count, q, j):
            nc.vector.scalar_tensor_tensor(sq[:, s, :], result, 0.0, rstd, ALU.max,
                                           ALU.mult).then_inc(c.dve_done, 1)
            dve.wait_ge(c.act_done, act_count(u, 1))
            low, high = (u_parts[:, bass.ds(u, 1), x, :].rearrange("p a n -> p (a n)")
                         for x in (1, 0))
            nc.vector.tensor_tensor(low, sq[:, s, :], high.bitcast(F32),
                                    ALU.subtract).then_inc(c.dve_done, 1)

        def square(act, u, s, result, act_count, dve_count, q, j):
            act.wait_ge(c.dve_done, dve_count(u))
            nc.scalar.activation(sq[:, s, :], sq[:, s, :], ACT.Square).then_inc(c.act_done, 1)
            act.wait_ge(c.act_done, act_count(u))
            nc.scalar.copy(u_parts[:, bass.ds(u, 1), 0, :].rearrange("p a n -> p (a n)"),
                           sq[:, s, :]).then_inc(c.act_done, 1)

        def add(dve, u, s, result, act_count, dve_count, q, j):
            nc.vector.tensor_tensor(one(y, u), one(y, u), result, ALU.add).then_inc(c.dve_done, 1)

        def copy(dve, u, s, result, act_count, dve_count, q, j):
            nc.vector.tensor_copy(one(y, u), result).then_inc(c.dve_done, 1)

        vecs = Steps(c, "vec", ["rstd"])

        def invert(dve, q, j):
            if isinstance(j, int) and j == 0 and q == 0:
                nc.vector.reciprocal(rstd, rstd).then_inc(vecs.step("rstd"), 1)
                dve.wait_ge(vecs.sem, vecs.value("rstd"))
        for chunk in range(FF_CHUNKS):
            gemm(nc, c, t["w_mlp_in"], KT, KT, lambda k, x, n: h[:, k, x, n * HALF:(n + 1) * HALF],
                 act_per_unit=2, act_epilogue=square, dve_per_unit=2, dve_epilogue=relu,
                 banks_read_by="dve", first=KT * chunk, then=(t["w_mlp_out"], KT * chunk, KT),
                 background=None if chunk else {"dve": invert})
            if chunk == 0:
                vecs.end()
            if chunk < FF_CHUNKS - 1:
                how = dict(dve_per_unit=1, dve_epilogue=add if chunk else copy, banks_read_by="dve")
            else:
                how = sum_squares(nc, c, y, sq, total, True)
            gemm(nc, c, t["w_mlp_out"], KT, KT,
                 lambda k, x, n: u_parts[:, k, x, n * HALF:(n + 1) * HALF], first=KT * chunk,
                 then=(t["w_mlp_in"], KT * (chunk + 1), KT) if chunk < FF_CHUNKS - 1
                 else (t["w_in_2"], 0, KT), **how)


def branches(nc, c, t, merged_ctx, modulated):
    with ExitStack() as ctx:
        hidden = c.sb("hidden", [P, KT, 2, S], F32R, ctx=ctx)
        norm_input(nc, c, t, hidden)
        with ExitStack() as inner:
            small = c.sb("small_projections", [P, 2, S], ctx=inner)
            project(nc, c, t["w_in"], 0, 2, hidden, small, (t["w_in"], 2, KT))
            delta_net(nc, c, t, hidden, small, modulated)
            latent_attention(nc, c, t, hidden, small)
            gated_linear(nc, c, t, hidden, small)
            forgetting_attention(nc, c, t, hidden, small)
        return gate_and_merge(nc, c, t, hidden, merged_ctx)


def mix_out(nc, c, t, merged, merged_ctx, y, total, sq, x_ctx):
    with ExitStack() as ctx:
        parts = c.sb("merged_parts", [P, KT, 2, S], F32R, ctx=ctx)
        split(nc, c, merged, parts)
        merged_ctx.close()
        x = c.sb("mlp_residual", [P, KT, S], ctx=x_ctx, side="right")
        with nc.Block() as block:
            @block.sync
            def _(sp):
                load_residual(c, sp, x, t["x"].rearrange("(b p) d -> p b d", p=P), True)
        gemm(nc, c, t["w_out"], KT, KT, lambda k, x, n: parts[:, k, x, n * HALF:(n + 1) * HALF],
             then=(t["w_mlp_in"], 0, KT), **sum_squares(nc, c, y, sq, total, False))
    return x


PAD = 3
EXT = S + PAD + CTX
MIX = 4


def context_values(nc, c, t, times, plus, v_ctx):
    with ExitStack() as ctx:
        x = c.sb("ctx_tokens", [P, 2, D], ctx=ctx)
        junk = c.sb("ctx_squares", [P, D], ctx=ctx)
        ss = c.sb("ctx_square_sums", [P, 2], ctx=ctx)
        root = c.sb("ctx_rms", [P, 2], ctx=ctx)
        rstd = c.sb("ctx_rstd", [P, 2], ctx=ctx)
        plain = c.sb("ctx_plain", [P, 2, CTX], ctx=ctx)
        parts = c.sb("ctx_parts", [P, KT, 2, CTX], F32R, ctx=ctx)
        act = Steps(c, "act", [("square", 2), "root", (("plain", "high"), KT)])
        vecs = Steps(c, "vec", ["rstd", ("scaled", 2), ("low", KT)])
        pes = Steps(c, "pe", [("turned", KT)])
        d0 = c.base["dma"]
        c.base["dma"] += 16
        with nc.Block() as block:
            @block.sync
            def _(sp):
                sp.dma_start(x[:], t["ctx"].rearrange("(b p) d -> p b d", p=P)).then_inc(
                    c.steps["dma"], 16)

            @block.scalar
            def _(a):
                a.wait_ge(c.steps["dma"], d0 + 16)
                for b in range(2):
                    if b:
                        a.wait_ge(act.sem, act.value("square", 0))
                    nc.scalar.activation(junk[:], x[:, b, :], ACT.Square,
                                         accum_out=ss[:, b:b + 1]).then_inc(act.step("square"), 1)
                a.wait_ge(act.sem, act.value("square"))
                nc.scalar.activation(root[:], ss[:], ACT.Sqrt, scale=1.0 / D,
                                     bias=c.eps[:, 0:1]).then_inc(act.step("root"), 1)
                for k in range(KT):
                    a.wait_ge(pes.sem, pes.value("turned", k))
                    if k >= 2:
                        a.wait_ge(vecs.sem, vecs.value("low", k - 2))
                    nc.scalar.activation(
                        plain[:, k % 2, :], c.psum[:, k % 4, 0:CTX], ACT.Identity,
                        scale=times[:, k, 1:2], bias=plus[:, k, 1:2]).then_inc(act.step("plain"), 1)
                    a.wait_ge(act.sem, act.value("plain", k))
                    nc.scalar.copy(parts[:, k, 0, :], plain[:, k % 2, :]).then_inc(
                        act.step("high"), 1)

            @block.vector
            def _(v):
                v.wait_ge(act.sem, act.value("root"))
                nc.vector.reciprocal(rstd[:], root[:]).then_inc(vecs.step("rstd"), 1)
                v.wait_ge(vecs.sem, vecs.value("rstd"))
                for b in range(2):
                    nc.vector.tensor_scalar(x[:, b, :], x[:, b, :],
                                            rstd[:, b:b + 1], None, ALU.mult).then_inc(
                        vecs.step("scaled"), 1)
                for k in range(KT):
                    v.wait_ge(act.sem, act.value("high", k))
                    nc.vector.tensor_tensor(parts[:, k, 1, :], plain[:, k % 2, :],
                                            parts[:, k, 0, :].bitcast(F32),
                                            ALU.subtract).then_inc(vecs.step("low"), 1)

            @block.tensor
            def _(p):
                p.wait_ge(vecs.sem, vecs.value("scaled"))
                for k in range(KT):
                    if k >= 4:
                        p.wait_ge(act.sem, act.value("plain", k - 4))
                    for b in range(2):
                        mm = nc.tensor.transpose(c.psum[:, k % 4, b * P:(b + 1) * P],
                                                 x[:, b, k * P:(k + 1) * P], c.ident[:])
                    mm.then_inc(pes.step("turned"), 1)
        for s in (act, vecs, pes):
            s.end()

        def evacuate(act, u, s, result, act_count, dve_count, q, j):
            nc.scalar.copy(one(v_ctx, u), c.psum[:, 2 * s, 0:CTX]).then_inc(c.act_done, 1)
        gemm(nc, c, t["w_in_2"], MIX, KT, lambda k, x, h: parts[:, k, x, :], act_per_unit=1,
             act_epilogue=evacuate, halves=1, cols=CTX, then=(t["w_in_2"], 0, KT))


def project_and_decay_rates(nc, c, t, h, y, rate):
    with ExitStack() as ctx:
        e, s, q, poly, relu = (c.sb("lru_" + n, [P, 8], ctx=ctx)
                               for n in ("exp", "ratio", "ratio_square", "series", "relu"))
        lam = vec(c, "a_lam_2", 0, 8)
        act = Steps(c, "act", ["abs", "exp"])
        terms = [1.0 / n for n in range(15, 0, -2)]
        vecs = Steps(c, "vec", ["plus2", "inverse", "ratio", "square", "first",
                                (("times", "plus"), len(terms) - 1), "odd", "relu", "sum", "rate",
                                "minus"])

        def exponential(a, q, j):
            if isinstance(j, int) and j == 0 and q == 0:
                nc.scalar.activation(e[:], lam, ACT.Abs).then_inc(act.step("abs"), 1)
                a.wait_ge(act.sem, act.value("abs"))
                nc.scalar.activation(e[:], e[:], ACT.Exp, scale=-1.0).then_inc(act.step("exp"), 1)

        def series(v, quarter, j):
            if not (isinstance(j, int) and j == 0 and quarter == 0):
                return
            ts, tt = nc.vector.tensor_scalar, nc.vector.tensor_tensor

            def do(name, ins):
                ins.then_inc(vecs.step(name), 1)
                v.wait_ge(vecs.sem, vecs.base + (vecs.next or vecs.n))
            v.wait_ge(act.sem, act.value("exp"))
            do("plus2", ts(s[:], e[:], 2.0, None, ALU.add))
            do("inverse", nc.vector.reciprocal(s[:], s[:]))
            do("ratio", tt(s[:], s[:], e[:], ALU.mult))
            do("square", tt(q[:], s[:], s[:], ALU.mult))
            do("first", nc.vector.memset(poly[:], terms[0]))
            for x in terms[1:]:
                do("times", tt(poly[:], poly[:], q[:], ALU.mult))
                do("plus", ts(poly[:], poly[:], x, None, ALU.add))
            do("odd", tt(poly[:], poly[:], s[:], ALU.mult))
            do("relu", ts(relu[:], lam, -1.0, 0.0, ALU.mult, ALU.max))
            do("sum", nc.vector.scalar_tensor_tensor(poly[:], poly[:], 2.0, relu[:], ALU.mult,
                                                     ALU.add))
            do("rate", ts(rate[:, 0, :], poly[:], -8.0, None, ALU.mult))
            do("minus", ts(rate[:, 1, :], poly[:], 8.0, None, ALU.mult))
        project(nc, c, t["w_in_2"], 0, 2 * MIX, h, y, (t["w_in_2"], 24, KT),
                background={"act": exponential, "dve": series})
        act.end()
        vecs.end()


def recurrence_branch(nc, c, t, h, y, v_ctx):
    with ExitStack() as ctx:
        def sb(name, *shape):
            return c.sb("lru_" + name, [P, *shape], ctx=ctx)
        rate = sb("rate", 2, 8)
        project_and_decay_rates(nc, c, t, h, y, rate)
        padded = sb("padded", 2, EXT + 2 * PAD)
        xc, r, ig = sb("convolved", 2, EXT), sb("r", 2, EXT), sb("gated_input", 2, EXT)
        a = sb("a", 2, EXT)
        run_ctx = sb("context_run", CTX)
        ys = sb("sum", 2, S)
        w = sb("gate_weights", 2, 2, MIX, P)
        items = [(p, d, x) for p in range(2) for d in range(2) for x in range(2)]
        tag = ["".join(map(str, i)) for i in items]
        groups = ["00", "01", "10", "11"]
        a_spec, v_spec = [], ["zero"]
        pads = lambda p: [f"pad{p}{x}{y}" for x in range(2) for y in ("x", "ctx")]
        convolved = lambda g, x: [f"{n}{g}{x}" for n in ("c0", "c1", "c2", "c3")]
        v_spec += convolved("00", 0) + convolved("00", 1)
        for g in groups:
            if g == "00":
                a_spec += pads(0)
            a_spec += [f"{n}{g}{x}" for x in range(2) for n in ("r", "ig")]
            a_spec += [f"{n}{g}{x}" for x in range(2) for n in ("a", "tanh", "square")]
            if g == "01":
                a_spec += pads(1)
            a_spec += [f"root{g}{x}" for x in range(2)]
            v_spec += [f"{n}{g}{x}" for n in ("in", "one") for x in range(2)]
            for x in range(2):
                if g != "11":
                    v_spec += convolved(groups[groups.index(g) + 1], x)
                v_spec += [f"{n}{g}{x}"
                           for n in ("b", "sctx", "scan") + (("add",) if g[1] == "1" else ())]
            if g[1] == "1":
                a_spec += [f"silu{g[0]}{x}" for x in range(2)]
                v_spec += [f"out{g[0]}{x}" for x in range(2)]
        act, vecs = Steps(c, "act", a_spec), Steps(c, "vec", v_spec)
        pes = Steps(c, "pe", [f"gates{n}" for n in tag])
        d0 = c.base["dma"]
        c.base["dma"] += 16
        s0 = list(c.slots)
        lat, con = slice(0, S), slice(S + PAD, EXT)
        bank3 = lambda n: c.psum[:, 3 * n:3 * n + 3, :].rearrange("p b n -> p (b n)")[:, 0:EXT]
        with nc.Block() as block:
            @block.sync
            def _(sp):
                sp.dma_start(w[:], t["lru_w"]).then_inc(c.steps["dma"], 16)
                for p in range(2):
                    for x in range(2):
                        sp.wait_ge(vecs.sem, vecs.value(f"out{p}{x}"))
                        store_slot(c, sp, t["cat"][2 * p + x], ys[:, x, :], x)
                wait_slots(c, sp)

            @block.scalar
            def _(e):
                def pad(p):
                    if p == 0:
                        e.wait_ge(vecs.sem, vecs.value("zero"))
                    else:
                        e.wait_ge(vecs.sem, vecs.value("c3011"))
                    for x in range(2):
                        nc.scalar.copy(padded[:, x, PAD:PAD + S],
                                       y[:, 2 * p + x, :]).then_inc(act.step(f"pad{p}{x}x"), 1)
                        nc.scalar.copy(
                            padded[:, x, 2 * PAD + S:2 * PAD + S + CTX], v_ctx[:, 2 * p + x, :]).then_inc(
                            act.step(f"pad{p}{x}ctx"), 1)
                pad(0)
                for g in groups:
                    p, d = int(g[0]), int(g[1])
                    for x in range(2):
                        m = 4 * d + 2 * p + x
                        e.wait_ge(pes.sem, pes.value(f"gates{g}{x}"))
                        if g != "00":
                            e.wait_ge(vecs.sem, vecs.value(f"b{groups[groups.index(g) - 1]}{x}"))
                        nc.scalar.activation(
                            r[:, x, :], bank3(0), ACT.Sigmoid, bias=vec(c, "a_br_2", m)).then_inc(
                            act.step(f"r{g}{x}"), 1)
                        if g != "00":
                            e.wait_ge(vecs.sem,
                                      vecs.value(f"{'scan' if d else 'add'}{groups[groups.index(g) - 1]}{x}"))
                        nc.scalar.activation(
                            ig[:, x, :], bank3(1), ACT.Sigmoid, bias=vec(c, "a_bi_2", m)).then_inc(
                            act.step(f"ig{g}{x}"), 1)
                    for x in range(2):
                        m = 4 * d + 2 * p + x
                        e.wait_ge(act.sem, act.value(f"r{g}{x}"))
                        nc.scalar.activation(a[:, x, :], r[:, x, :], ACT.Exp,
                                             scale=rate[:, 0, m:m + 1]).then_inc(
                            act.step(f"a{g}{x}"), 1)
                        e.wait_ge(act.sem, act.value(f"a{g}{x}"))
                        nc.scalar.activation(
                            r[:, x, :], r[:, x, :], ACT.Tanh, scale=rate[:, 1, m:m + 1]).then_inc(
                            act.step(f"tanh{g}{x}"), 1)
                        e.wait_ge(vecs.sem, vecs.value(f"in{g}{x}"))
                        nc.scalar.activation(xc[:, x, :], a[:, x, :],
                                             ACT.Square).then_inc(act.step(f"square{g}{x}"), 1)
                    if g == "01":
                        pad(1)
                    for x in range(2):
                        e.wait_ge(vecs.sem, vecs.value(f"one{g}{x}"))
                        nc.scalar.activation(r[:, x, :], r[:, x, :],
                                             ACT.Sqrt).then_inc(act.step(f"root{g}{x}"), 1)
                    if d == 1:
                        for x in range(2):
                            nc.scalar.activation(
                                y[:, MIX + 2 * p + x, :], y[:, MIX + 2 * p + x, :], ACT.Silu).then_inc(
                                act.step(f"silu{p}{x}"), 1)

            @block.vector
            def _(v):
                tt, stt = nc.vector.tensor_tensor, nc.vector.scalar_tensor_tensor
                nc.vector.memset(padded[:], 0.0).then_inc(vecs.step("zero"), 1)

                def convolve(g, x):
                    p, d = int(g[0]), int(g[1])
                    m = 2 * p + x
                    taps = [vec(c, "a_conv_2", 16 * d + 4 * m + k) for k in range(4)]
                    at = PAD if d else 0
                    v.wait_ge(act.sem, act.value(f"pad{p}{x}ctx"))
                    if g != "00":
                        v.wait_ge(vecs.sem, vecs.value(f"one{groups[groups.index(g) - 1]}{x}"))
                    nc.vector.tensor_scalar(xc[:, x, :], padded[:, x, at:at + EXT], taps[0], None,
                                            ALU.mult).then_inc(vecs.step(f"c0{g}{x}"), 1)
                    for k in range(1, 4):
                        v.wait_ge(vecs.sem, vecs.value(f"c{k - 1}{g}{x}"))
                        stt(xc[:, x, :], padded[:, x, at + k:at + k + EXT], taps[k], xc[:, x, :],
                            ALU.mult, ALU.add).then_inc(vecs.step(f"c{k}{g}{x}"), 1)

                convolve("00", 0)
                convolve("00", 1)
                for g in groups:
                    p, d = int(g[0]), int(g[1])
                    for x in range(2):
                        v.wait_ge(act.sem, act.value(f"ig{g}{x}"))
                        v.wait_ge(vecs.sem, vecs.value(f"c3{g}{x}"))
                        tt(ig[:, x, :], ig[:, x, :], xc[:, x, :], ALU.mult).then_inc(
                            vecs.step(f"in{g}{x}"), 1)
                    for x in range(2):
                        v.wait_ge(act.sem, act.value(f"square{g}{x}"))
                        stt(r[:, x, :], xc[:, x, :], 1.0, r[:, x, :],
                            ALU.add, ALU.mult).then_inc(vecs.step(f"one{g}{x}"), 1)
                    for x in range(2):
                        if g != "11":
                            convolve(groups[groups.index(g) + 1], x)
                        v.wait_ge(act.sem, act.value(f"root{g}{x}"))
                        v.wait_ge(vecs.sem, vecs.value(f"in{g}{x}"))
                        tt(ig[:, x, :], ig[:, x, :], r[:, x, :], ALU.mult).then_inc(
                            vecs.step(f"b{g}{x}"), 1)
                        v.wait_ge(vecs.sem, vecs.value(f"b{g}{x}"))

                        def run(tile, cols):
                            view = tile[:, x, cols] if cols is not None else tile
                            return view[:, ::-1] if d else view
                        if g != "00" or x:
                            last = f"{g}0" if x else f"{groups[groups.index(g) - 1]}1"
                            v.wait_ge(vecs.sem, vecs.value("scan" + last))
                        out_ctx = run_ctx[:, ::-1] if d else run_ctx[:]
                        nc.vector.tensor_tensor_scan(
                            out_ctx, run(a, con), run(ig, con), 0.0, ALU.mult, ALU.add).then_inc(
                            vecs.step(f"sctx{g}{x}"), 1)
                        v.wait_ge(vecs.sem, vecs.value(f"sctx{g}{x}"))
                        first = run_ctx[:, 0:1] if d else run_ctx[:, CTX - 1:CTX]
                        if d == 0 and p:
                            v.wait_ge(c.slot_stored[x], s0[x] + 16)
                        to = run(ys, lat) if d == 0 else run(ig, lat)
                        nc.vector.tensor_tensor_scan(
                            to, run(a, lat), run(ig, lat), first, ALU.mult, ALU.add).then_inc(vecs.step(f"scan{g}{x}"), 1)
                        v.wait_ge(vecs.sem, vecs.value(f"scan{g}{x}"))
                        if d:
                            tt(ys[:, x, :], ys[:, x, :], ig[:, x, lat],
                               ALU.add).then_inc(vecs.step(f"add{g}{x}"), 1)
                    if d:
                        for x in range(2):
                            v.wait_ge(act.sem, act.value(f"silu{p}{x}"))
                            v.wait_ge(vecs.sem, vecs.value(f"add{g}{x}"))
                            tt(ys[:, x, :], ys[:, x, :],
                               y[:, MIX + 2 * p + x, :], ALU.mult).then_inc(
                                vecs.step(f"out{p}{x}"), 1)

            @block.tensor
            def _(e):
                e.wait_ge(c.steps["dma"], d0 + 16)
                for n, (p, d, x) in enumerate(items):
                    e.wait_ge(vecs.sem, vecs.value(f"c3{tag[n]}"))
                    if n:
                        e.wait_ge(act.sem, act.value(f"ig{tag[n - 1]}"))
                    for kind in range(2):
                        for q, (lo, hi) in enumerate(((0, HALF), (HALF, S), (S, EXT))):
                            last = nc.tensor.matmul(c.psum[:, 3 * kind + q, 0:hi - lo],
                                                    w[:, kind, d, 2 * p + x, :], xc[:, x, lo:hi],
                                                    start=True, stop=True)
                    last.then_inc(pes.step(f"gates{tag[n]}"), 1)
        for s in (act, vecs, pes):
            s.end()


def glu_input(nc, c, t, h, y):
    def evacuate(act, u, s, result, act_count, dve_count, q, j):
        if q == 0:
            nc.scalar.copy(one(y, j), result).then_inc(c.act_done, 1)
        else:
            nc.scalar.activation(one(y[:, MIX:2 * MIX, :], j), result,
                                 ACT.Sigmoid).then_inc(c.act_done, 1)

    def times(dve, u, s, result, act_count, dve_count, q, j):
        if q:
            dve.wait_ge(c.act_done, act_count(u))
            nc.vector.tensor_tensor(one(y, j), one(y, j), one(y[:, MIX:2 * MIX, :], j),
                                    ALU.mult).then_inc(vecs.step("gated"), 1)
    vecs = Steps(c, "vec", ["gated"])
    project(nc, c, t["w_in_2"], 24, 2 * MIX, h, None, (t["w_in_2"], 8, KT), act_epilogue=evacuate,
            dve_epilogue=times)
    vecs.end(MIX)


TAPS = 31


def two_convolutions(nc, c, t, h, y):
    half = TAPS // 2
    order = [half] + [k for k in range(TAPS) if k != half]
    start3, start31 = VECTORS["b_conv_2"][0], VECTORS["c_conv_2"][0]
    with ExitStack() as ctx:
        z = c.sb("gated_conv_projected", [P, 4, S], ctx=ctx)
        conv = c.sb("gated_conv_out", [P, S], ctx=ctx)
        result_b = c.sb("gated_conv_branch", [P, MIX, S], ctx=ctx)
        vecs = Steps(c, "vec", [("tap", 24), ("last", TAPS - 25), "left", "right"])
        acts = Steps(c, "act", ["centre", "mid"])
        pool_steps = Steps(c, "pool", ["cv", "b", "out"])
        evacuated = c.base["gemm_act"]
        b, x, val, gate = (z[:, n, :] for n in range(4))

        def weight(first, j, step, k):
            return c.vectors[:, bass.ds(j * step + (first + k), 1)]

        def tap(dve, j, name, n, k):
            x, to = one(y, j), one(y[:, MIX:2 * MIX, :], j)
            w, s = weight(start31, j, TAPS, order[k]), order[k] - half
            if k == 1:
                dve.wait_ge(acts.sem, acts.value("centre", i=j))
            elif n:
                dve.wait_ge(vecs.sem, vecs.value(name, n - 1, i=j))
            else:
                dve.wait_ge(vecs.sem, vecs.value("tap", 23, i=j))
            at = to[:, max(0, -s):S - max(0, s)]
            nc.vector.scalar_tensor_tensor(at, x[:, max(0, s):S - max(0, -s)], w, at, ALU.mult,
                                           ALU.add).then_inc(vecs.step(name), 1)

        def taps(dve, q, j):
            for n in range(8 if q < 3 else TAPS - 25):
                if q < 3:
                    tap(dve, j, "tap", 8 * q + n, 8 * q + n + 1)
                else:
                    tap(dve, j, "last", n, 8 * q + n + 1)

        def evacuate(act, u, s, result, act_count, dve_count, q, j):
            if q == 0 and (not isinstance(j, int) or j):
                act.wait_ge(pool_steps.sem, pool_steps.value_before("out", j))
            nc.scalar.activation(z[:, q, :], result,
                                 ACT.Silu if q == 3 else ACT.Copy).then_inc(c.act_done, 1)

        def middle_taps(act, q, j):
            if q == 0:
                nc.scalar.activation(one(y[:, MIX:2 * MIX, :], j), one(y, j), ACT.Copy,
                                     scale=weight(start31, j, TAPS, half)).then_inc(
                                         acts.step("centre"), 1)
            if q == 3:
                act.wait_ge(pool_steps.sem, pool_steps.value("cv", i=j))
                nc.scalar.activation(conv[:], x, ACT.Copy,
                                     scale=weight(start3, j, 3, 1)).then_inc(acts.step("mid"), 1)

        def outer_taps(dve, u, s, result, act_count, dve_count, q, j):
            if q == 3:
                stt = nc.vector.scalar_tensor_tensor
                dve.wait_ge(acts.sem, acts.value("mid", i=j))
                stt(conv[:, 1:], x[:, 0:S - 1], weight(start3, j, 3, 0), conv[:, 1:], ALU.mult,
                    ALU.add).then_inc(vecs.step("left"), 1)
                dve.wait_ge(vecs.sem, vecs.value("left", i=j))
                stt(conv[:, 0:S - 1], x[:, 1:], weight(start3, j, 3, 2), conv[:, 0:S - 1],
                    ALU.mult, ALU.add).then_inc(vecs.step("right"), 1)

        stored = c.sem("gated_conv_stored")

        def cut_and_combine(pool, low):
            tt = nc.gpsimd.tensor_tensor
            for u in range(1, 4):
                low(u)
            for j in range(MIX):
                low(4 * j + 4)
                pool.wait_ge(c.act_done, 4 * j + (evacuated + 3))
                tt(x, x, val, ALU.mult).then_inc(pool_steps.step("cv"), 1)
                if j < MIX - 1:
                    low(4 * j + 5)
                pool.wait_ge(vecs.sem, vecs.value("right", i=j))
                pool.wait_ge(c.act_done, 4 * j + (evacuated + 4))
                tt(one(result_b, j), b, conv[:], ALU.mult).then_inc(pool_steps.step("b"), 1)
                pool.wait_ge(pool_steps.sem, pool_steps.value("b", i=j))
                tt(one(result_b, j), one(result_b, j), gate,
                   ALU.mult).then_inc(pool_steps.step("out"), 1)
                pool.wait_ge(pool_steps.sem, pool_steps.value("out", i=j))
                pool.dma_start(t["cat"][j + MIX], one(result_b, j)).then_inc(stored, 16)
                if j < MIX - 1:
                    low(4 * j + 6)
                    low(4 * j + 7)
            pool.wait_ge(stored, 16 * MIX)
        project(nc, c, t["w_in_2"], 8, 4 * MIX, h, None, (t["w_in_2"], 32, KT),
                act_epilogue=evacuate, dve_epilogue=outer_taps, unroll=4,
                background={"dve": taps, "act": middle_taps, "pool": cut_and_combine}, pool_cuts=True)
        for s in (vecs, acts, pool_steps):
            s.end(MIX)


def glu_conv_branch(nc, c, t, h, h_ctx, y, tiles, x_ctx):
    u, gate = y[:, MIX:2 * MIX, :], y[:, 0:MIX, :]
    with ExitStack() as ctx:
        parts = c.sb("glu_parts", [P, MIX, 2, S], F32R, ctx=ctx)
        sq, stat = tiles[:, 0:MIX, :], tiles[:, MIX, :]
        act = Steps(c, "act", [("square", MIX), "root"])
        vecs = Steps(c, "vec", [("centred", MIX), "rstd", ("normed", MIX)])
        pes = Steps(c, "pe", ["mean", "variance"])

        def sums(pe, name, bank, src):
            for x in range(NH):
                for m in range(MIX):
                    mm = nc.tensor.matmul(c.psum[:, bank + x, :], c.ones[:],
                                          src[:, m, x * HALF:(x + 1) * HALF],
                                          start=(m == 0), stop=(m == MIX - 1))
            mm.then_inc(pes.step(name), 1)

        def on_pe(pe, q, j):
            if q == 0:
                sums(pe, "mean", 4, u)
            if q == 2:
                pe.wait_ge(act.sem, act.value("square"))
                sums(pe, "variance", 6, sq)

        def on_act(a, q, j):
            if q == 2:
                for m in range(MIX):
                    a.wait_ge(vecs.sem, vecs.value("centred", m))
                    nc.scalar.activation(sq[:, m, :], u[:, m, :], ACT.Square).then_inc(
                        act.step("square"), 1)
            if q == 3:
                a.wait_ge(pes.sem, pes.value("variance"))
                nc.scalar.activation(stat, c.banks(6), ACT.Sqrt,
                                     scale=1.0 / (MIX * P), bias=c.eps[:, 1:2]).then_inc(
                    act.step("root"), 1)

        def on_dve(v, q, j):
            stt = nc.vector.scalar_tensor_tensor
            if q == 1:
                v.wait_ge(pes.sem, pes.value("mean"))
                for m in range(MIX):
                    stt(u[:, m, :], c.banks(4), -1.0 / (MIX * P),
                        u[:, m, :], ALU.mult, ALU.add).then_inc(vecs.step("centred"), 1)
            if q == 3:
                v.wait_ge(act.sem, act.value("root"))
                nc.vector.reciprocal(stat, stat).then_inc(vecs.step("rstd"), 1)
                v.wait_ge(vecs.sem, vecs.value("rstd"))
                for m in range(MIX):
                    stt(u[:, m, :], u[:, m, :], vec(c, "c_ln_g_2", m),
                        stat, ALU.mult, ALU.mult).then_inc(vecs.step("normed"), 1)

        def evacuate(a, n, s, result, act_count, dve_count, q, j):
            nc.scalar.activation(gate[:, n, :], result, ACT.Silu).then_inc(c.act_done, 1)
        project(nc, c, t["w_in_2"], 32, MIX, h, None, (t["w_in_2"], 36, KT),
                act_epilogue=evacuate, unroll=4,
                background={"pe": on_pe, "act": on_act, "dve": on_dve})
        for x in (act, vecs, pes):
            x.end()
        act, vecs = Steps(c, "act", [("silu", MIX), ("high", MIX)]), Steps(c, "vec", [("low", MIX)])

        def silu_and_high(a, q, j):
            if q == 0:
                for m in range(MIX):
                    nc.scalar.activation(u[:, m, :], u[:, m, :], ACT.Silu,
                                         bias=vec(c, "c_ln_b_2", m)).then_inc(act.step("silu"), 1)
            if q == 1:
                for m in range(MIX):
                    a.wait_ge(act.sem, act.value("silu", m))
                    nc.scalar.copy(parts[:, m, 0, :], u[:, m, :]).then_inc(act.step("high"), 1)

        def low(v, q, j):
            if q == 2:
                for m in range(MIX):
                    v.wait_ge(act.sem, act.value("high", m))
                    nc.vector.tensor_tensor(parts[:, m, 1, :], u[:, m, :],
                                            parts[:, m, 0, :].bitcast(F32),
                                            ALU.subtract).then_inc(vecs.step("low"), 1)
        project(nc, c, t["w_in_2"], 36, MIX, h, tiles, (t["w_in_2"], 40, KT), unroll=4,
                background={"act": silu_and_high, "dve": low})
        act.end()
        vecs.end()

        def silu(a, n, s, result, act_count, dve_count, q, j):
            nc.scalar.activation(tiles[:, MIX + n, :], result, ACT.Silu).then_inc(c.act_done, 1)
        project(nc, c, t["w_in_2"], 40, MIX, h, None, (t["c_pw"], 0, MIX), unroll=4,
                act_epilogue=silu)
        h_ctx.close()
        x = c.sb("mixed", [P, KT, S], ctx=x_ctx, side="right")
        with nc.Block() as block:
            @block.sync
            def _(sp):
                load_residual(c, sp, x, t["cat"][0:KT].rearrange("n p s -> p n s"), False)
        glu_product(nc, c, t, parts, u, gate)
        return x


def glu_product(nc, c, t, parts, u, gate):
    bias = VECTORS["c_pw_b_2"][0]

    def plus_bias(act, n, s, result, act_count, dve_count, q, j):
        nc.scalar.activation(one(u, n), result, ACT.Identity,
                             bias=c.vectors[:, bass.ds(n + bias, 1)]).then_inc(c.act_done, 1)

    def gated(dve, n, s, result, act_count, dve_count, q, j):
        dve.wait_ge(c.act_done, act_count(n))
        nc.vector.tensor_tensor(one(u, n), one(u, n), one(gate, n),
                                ALU.mult).then_inc(c.dve_done, 1)
    gemm(nc, c, t["c_pw"], MIX, MIX, lambda k, x, h2: parts[:, k, x, h2 * HALF:(h2 + 1) * HALF],
         act_per_unit=1, act_epilogue=plus_bias, dve_per_unit=1, dve_epilogue=gated,
         then=(t["w_out_2"], 0, KT))


class Pooling:

    def __init__(self, nc, c, t, tiles, ctx):
        self.nc, self.c, self.t, self.tiles = nc, c, t, tiles
        self.rows, self.edge = S // GRID_W, max(WINDOWS) // 2
        self.tall = c.sb("pool_rows", [P, 3, self.rows + 2 * self.edge, GRID_W], ctx=ctx)
        self.wide = c.sb("pool_columns", [P, 3, self.rows, GRID_W + 2 * self.edge], ctx=ctx)
        self.share = c.sb("pool_share", [P, S], ctx=ctx)
        self.w = c.sb("pool_weights", [P, MIX, P], ctx=ctx)
        spec = ["zero_tall", "zero_wide"]
        for g in range(MIX):
            spec += [f"in{g}"] + [f"row{g}_{k}" for k in range(g + 1)]
            spec += [f"bias{g - 1}", f"out{g - 1}"] if g else []
            spec += [f"column{g}_{k}" for k in range(g + 1)] + [f"mean{g}", f"less{g}"]
        self.vecs = Steps(c, "vec", spec + ["bias3", "out3"])
        self.pes = Steps(c, "pe", [("product", MIX)])
        self.share_loaded, self.w_loaded = c.sem("pool_share_loaded"), c.sem("pool_weights_loaded")

    def on_sp(self, sp, q, j):
        if q == 0:
            sp.dma_start(self.w[:], self.t["d_w"]).then_inc(self.w_loaded, 16)
        if q % 2 == 0:
            g = q // 2
            if g:
                sp.wait_ge(self.vecs.sem, self.vecs.value(f"mean{g - 1}"))
            sp.dma_start(self.share[:],
                         self.t["pool_shares"][g].partition_broadcast(P)).then_inc(
                             self.share_loaded, 16)

    def do(self, v, name, ins):
        ins.then_inc(self.vecs.step(name), 1)
        v.wait_ge(self.vecs.sem, self.vecs.value(name))

    def finish(self, v, g):
        tile = self.tiles[:, g, :]
        v.wait_ge(self.pes.sem, self.pes.value("product", g))
        self.do(v, f"bias{g}", self.nc.vector.tensor_scalar(
            tile, self.c.banks(4 + 2 * (g % 2)), vec(self.c, "d_b_2", g),
            vec(self.c, "d_scale_2", g), ALU.add, ALU.mult))
        self.do(v, f"out{g}", self.nc.vector.tensor_tensor(tile, tile, self.tiles[:, MIX + g, :],
                                                           ALU.mult))

    def on_dve(self, v, q, j):
        g, tt, tall, wide = q // 2, self.nc.vector.tensor_tensor, self.tall, self.wide
        win = WINDOWS[g]
        grid = self.tiles[:, g, :].rearrange("p (r w) -> p r w", w=GRID_W)
        first, src = self.edge - win // 2, 0
        if q == 0:
            self.do(v, "zero_tall", self.nc.vector.memset(tall[:], 0.0))
            self.do(v, "zero_wide", self.nc.vector.memset(wide[:], 0.0))
        if q % 2 == 0:
            self.do(v, f"in{g}", self.nc.vector.tensor_copy(
                tall[:, 0, self.edge:self.edge + self.rows, :], grid))
            for k in range(g + 1):
                step, n = 2 ** k, self.rows + win - 2 ** (k + 1)
                a, b = (tall[:, src, first + x:first + x + n, :] for x in (0, step))
                if k == g:
                    to = wide[:, 0, :, self.edge:self.edge + GRID_W]
                else:
                    to = tall[:, 1 + k % 2, first:first + n, :]
                self.do(v, f"row{g}_{k}", tt(to, a, b, ALU.add))
                src = 1 + k % 2
            return
        if g:
            self.finish(v, g - 1)
        for k in range(g + 1):
            step, n = 2 ** k, GRID_W + win - 2 ** (k + 1)
            a, b = (wide[:, src, :, first + x:first + x + n] for x in (0, step))
            self.do(v, f"column{g}_{k}", tt(wide[:, 1 + k % 2, :, first:first + n], a, b,
                                            ALU.add))
            src = 1 + k % 2
        v.wait_ge(self.share_loaded, 16 * (g + 1))
        total = wide[:, src, :, first:first + GRID_W]
        share = self.share[:].rearrange("p (r w) -> p r w", w=GRID_W)
        mean = tall[:, 1, 0:self.rows, :]
        self.do(v, f"mean{g}", tt(mean, total, share, ALU.mult))
        self.do(v, f"less{g}", tt(grid, mean, grid, ALU.subtract))

    def on_pe(self, pe, q, j):
        if q % 2 == 0 and q:
            self.product(pe, q // 2 - 1)

    def product(self, pe, g):
        if g == 0:
            pe.wait_ge(self.w_loaded, 16)
        pe.wait_ge(self.vecs.sem, self.vecs.value(f"less{g}"))
        if g >= 2:
            pe.wait_ge(self.vecs.sem, self.vecs.value(f"bias{g - 2}"))
        for n in range(NH):
            mm = self.nc.tensor.matmul(self.c.psum[:, 4 + 2 * (g % 2) + n, :], self.w[:, g, :],
                                       self.tiles[:, g, n * HALF:(n + 1) * HALF], start=True,
                                       stop=True)
        mm.then_inc(self.pes.step("product"), 1)


def mixer_out(nc, c, t, y, tiles, x, x_ctx, final_ctx, gate):
    def copy(dve, u, s, result, act_count, dve_count, q, j):
        nc.vector.tensor_copy(one(y, u), result).then_inc(c.dve_done, 1)

    glu_dram = t["cat"][2 * MIX:3 * MIX].rearrange("n p s -> p n s")
    with ExitStack() as ctx:
        parts = c.sb("mixed_parts", [P, KT, 2, S], F32R, ctx=ctx)

        def product(half, how, then, dve_per_unit=1, **options):
            gemm(nc, c, t["w_out_2"], KT, KT,
                 lambda k, p, n: parts[:, k, p, n * HALF:(n + 1) * HALF], first=KT * half,
                 then=then, dve_per_unit=dve_per_unit, dve_epilogue=how, banks_read_by="dve",
                 **options)
        split(nc, c, x, parts, wait=wait_residual,
              meanwhile=lambda sp: (store(c, sp, glu_dram, y[:, MIX:2 * MIX, :]),
                                    sp.wait_ge(c.scratch_stored, c.stored)))
        x_ctx.close()
        with ExitStack() as inner:
            pooling = Pooling(nc, c, t, tiles, inner)
            product(0, copy, (t["w_out_2"], KT, KT), unroll=8,
                    background={"sp": pooling.on_sp, "dve": pooling.on_dve, "pe": pooling.on_pe})
            with nc.Block() as block:
                @block.tensor
                def _(pe):
                    pooling.product(pe, MIX - 1)

                @block.vector
                def _(v):
                    pooling.finish(v, MIX - 1)
            pooling.vecs.end()
            pooling.pes.end()
        final = c.sb("final_residual", [P, KT, S], ctx=final_ctx, side="right")
        total = c.sb("final_totals", [P, S], ctx=final_ctx, side="right")
        sq = c.sb("final_squares", [P, 2, S], ctx=ctx)
        glu = tiles[:, MIX:, :]
        loaded = c.sem("glu_result_loaded")
        with nc.Block() as block:
            @block.sync
            def _(sp):
                sp.dma_start(glu, glu_dram).then_inc(loaded, 16)
        split(nc, c, tiles[:, 0:MIX, :], parts[:, MIX:, :, :])
        split(nc, c, glu, parts, wait=lambda c, eng, k: eng.wait_ge(loaded, 16),
              meanwhile=lambda sp: load_residual(c, sp, final, t["x_second"], False))
        g0 = VECTORS["final_g_2"][0]

        def square_and_scale(act, u, s, result, act_count, dve_count, q, j):
            act.wait_ge(c.dve_done, dve_count(u, 1))
            if not isinstance(u, int) or u >= 2:
                act.wait_ge(c.dve_done, dve_count(u - 2, 2))
            nc.scalar.activation(sq[:, s, :], one(y, u), ACT.Square).then_inc(c.act_done, 1)
            nc.scalar.activation(one(final, u), one(y, u), ACT.Copy,
                                 scale=c.vectors[:, bass.ds(u + g0, 1)]).then_inc(c.act_done, 1)

        def add_all(dve, u, s, result, act_count, dve_count, q, j):
            nc.vector.tensor_tensor(one(y, u), one(y, u), result, ALU.add).then_inc(c.dve_done, 1)
            dve.wait_ge(c.dve_done, dve_count(u))
            for k in (0, KT - 1):
                wait_residual(c, dve, k)
            nc.vector.scalar_tensor_tensor(one(y, u), one(y, u), gate[:, bass.ds(u, 1)],
                                           one(final, u), ALU.mult, ALU.add).then_inc(c.dve_done, 1)
            dve.wait_ge(c.act_done, act_count(u))
            if not isinstance(u, int) or u:
                dve.wait_ge(c.dve_done, dve_count(u - 1, 2))
            nc.vector.tensor_tensor(total[:], total[:], sq[:, s, :], ALU.add).then_inc(c.dve_done, 1)
        product(1, add_all, None, dve_per_unit=3, act_per_unit=2, act_epilogue=square_and_scale,
                background=clearing(nc, c, total[:]))
    return final, total


def final_norm(nc, c, t, y, x, total):
    with ExitStack() as ctx:
        sums, rstd = c.sb("final_sums", [1, S], ctx=ctx), c.sb("final_rstd", [P, BLK], ctx=ctx)
        pes = Steps(c, "pe", ["sums", ("turned", 3), "columns", ("turned_late", BLK - 3)])
        vecs = Steps(c, "vec", ["row", "rstd", ("rows", BLK // 2)])
        act = Steps(c, "act", ["root", ("rows", BLK // 2)])
        ps = c.psum

        def turned(b):
            return pes.value("turned", b) if b < 3 else pes.value("turned_late", b - 3)

        def rows_done(b):
            return (vecs if b % 2 else act).value("rows", b // 2)
        with nc.Block() as block:
            @block.tensor
            def _(p):
                for h in range(NH):
                    mm = nc.tensor.matmul(ps[0:1, 6 + h, :], c.ones[:, 0:1],
                                          total[:, h * HALF:(h + 1) * HALF], start=True, stop=True)
                mm.then_inc(pes.step("sums"), 1)
                for b in range(BLK):
                    if b == 3:
                        p.wait_ge(vecs.sem, vecs.value("row"))
                        for n in range(BLK):
                            mm = nc.tensor.matmul(ps[:, 6, n:n + 1], sums[:, n * P:(n + 1) * P],
                                                  c.ones[0:1, 0:1], start=True, stop=True)
                        mm.then_inc(pes.step("columns"), 1)
                    if b >= 3:
                        p.wait_ge((vecs if (b - 3) % 2 else act).sem, rows_done(b - 3))
                    for k in range(KT):
                        mm = nc.tensor.transpose(
                            ps[:, 2 * (b % 3) + k // 4, k % 4 * P:(k % 4 + 1) * P],
                            x[:, k, b * P:(b + 1) * P], c.ident[:])
                    mm.then_inc(pes.step("turned" if b < 3 else "turned_late"), 1)

            @block.scalar
            def _(a):
                a.wait_ge(pes.sem, pes.value("columns"))
                nc.scalar.activation(rstd[:], ps[:, 6, 0:BLK], ACT.Sqrt, scale=1.0 / D,
                                     bias=c.eps[:, 0:1]).then_inc(act.step("root"), 1)
                a.wait_ge(vecs.sem, vecs.value("rstd"))
                for b in range(0, BLK, 2):
                    a.wait_ge(pes.sem, turned(b))
                    nc.scalar.activation(y[:, b, :], c.banks(2 * (b % 3)), ACT.Copy,
                                         scale=rstd[:, b:b + 1]).then_inc(act.step("rows"), 1)

            @block.vector
            def _(v):
                v.wait_ge(pes.sem, pes.value("sums"))
                nc.vector.tensor_copy(sums[:], ps[0:1, 6:8, :].rearrange("p b n -> p (b n)")
                                      ).then_inc(vecs.step("row"), 1)
                v.wait_ge(act.sem, act.value("root"))
                nc.vector.reciprocal(rstd[:], rstd[:]).then_inc(vecs.step("rstd"), 1)
                v.wait_ge(vecs.sem, vecs.value("rstd"))
                for b in range(1, BLK, 2):
                    v.wait_ge(pes.sem, turned(b))
                    nc.vector.tensor_scalar(y[:, b, :], c.banks(2 * (b % 3)), rstd[:, b:b + 1],
                                            None, ALU.mult).then_inc(vecs.step("rows"), 1)

            @block.sync
            def _(sp):
                for b in range(BLK):
                    sp.wait_ge((vecs if b % 2 else act).sem, rows_done(b))
                    store(c, sp, t["out"][b * P:(b + 1) * P, :], y[:, b, :])
                sp.wait_ge(c.scratch_stored, c.stored)
        for s in (pes, vecs, act):
            s.end()


def build(nc, t):
    with ExitStack() as ctx:
        c = Core(nc, ctx)
        scratch = {"branch": [4, P, 2, S], "x_mid": [P, KT, S], "x_second": [P, KT, S],
                   "cat": [4 * MIX, P, S]}
        for name, shape in scratch.items():
            t[name] = nc.dram_tensor(f"{name}_scratch", shape, F32, kind="Internal").ap()
        load_constants(nc, c, t)
        merged_ctx = ctx.enter_context(ExitStack())
        times, plus = c.sb("mod_times", [P, KT, 2]), c.sb("mod_plus", [P, KT, 2])
        gate = c.sb("mod_gate", [P, KT])
        merged = branches(nc, c, t, merged_ctx, (times, plus, gate))
        y = c.sb("y", [P, KT, S])
        with ExitStack() as mix_ctx:
            with ExitStack() as sums_ctx:
                total = c.sb("square_totals", [P, S], ctx=sums_ctx)
                sq = c.sb("squares", [P, 2, S], ctx=sums_ctx)
                with ExitStack() as mlp_ctx:
                    x_ctx = ctx.enter_context(ExitStack())
                    x = mix_out(nc, c, t, merged, merged_ctx, y, total, sq, x_ctx)
                    h = c.sb("mlp_in", [P, KT, 2, S], F32R, ctx=mlp_ctx)
                    add_residual(nc, c, t, y, total, lambda k: vec(c, "norm_mix_post", k),
                                 True, None, t["x_mid"], out=h,
                                 times=lambda k: vec(c, "norm_mlp_pre", k), defer=True, loaded=x)
                    x_ctx.close()
                    mlp(nc, c, t, h, y, total, sq)
                h = c.sb("mixer_in", [P, KT, 2, S], F32R, ctx=mix_ctx, side="right")
                add_residual(nc, c, t, y, total, lambda k: vec(c, "norm_mlp_post", k), None,
                             t["x_mid"], t["x_second"], out=h, times=lambda k: times[:, k, 0:1],
                             plus=lambda k: plus[:, k, 0:1])
            with ExitStack() as inner:
                v_ctx = c.sb("ctx_values", [P, MIX, CTX], ctx=inner)
                context_values(nc, c, t, times, plus, v_ctx)
                recurrence_branch(nc, c, t, h, y, v_ctx)
            glu_input(nc, c, t, h, y)
            two_convolutions(nc, c, t, h, y)
            with ExitStack() as tiles_ctx:
                tiles = c.sb("pool_projected", [P, 2 * MIX, S], ctx=tiles_ctx)
                x_ctx, final_ctx = ctx.enter_context(ExitStack()), ctx.enter_context(ExitStack())
                x = glu_conv_branch(nc, c, t, h, mix_ctx, y, tiles, x_ctx)
                final, total = mixer_out(nc, c, t, y, tiles, x, x_ctx, final_ctx, gate)
        final_norm(nc, c, t, y, final, total)


def unit_columns():
    names = ("dn_q", "dn_k", "dn_v", "dn_z", "dn_b", "dn_a", "mla_cq", "mla_ckv", "mla_kpe",
             "gla_q", "gla_k", "gla_v", "gla_g", "gla_lr", "fox_q", "fox_k", "fox_v", "fox_f")
    sizes = (256, 256, 256, 256, 4, 4, 256, 128, 32, 128, 128, 256, 256, 16, 256, 256, 256, 4)
    at = dict(zip(names, np.cumsum((0, *sizes))[:-1]))
    kpe = at["mla_kpe"] + np.arange(ROPE)
    swap = np.roll(np.arange(ROPE), ROPE // 2)
    small_1, small_2 = np.full(P, -1), np.full(P, -1)
    order = np.array([0, 2, 1, 3])
    small_1[0:4] = at["dn_b"] + order
    small_1[32:36] = at["dn_a"] + order
    small_1[64:96], small_1[96:128] = kpe, kpe[swap]
    small_2[0:128:32] = at["fox_f"] + np.arange(4)
    small_2[1:17] = at["gla_lr"] + np.arange(16)
    units = [small_1, small_2]
    for name, size in zip(names, sizes):
        if size >= P:
            units += [at[name] + P * n + np.arange(P) for n in range(size // P)]
    return units


def in_units(w, columns=None):
    k, n = w.shape
    if columns is not None:
        w = np.concatenate([w, np.zeros((k, 1), w.dtype)], axis=1)[:, np.concatenate(columns)]
        n = w.shape[1]
    w = w.reshape(k // P, P, n // P, P)
    return np.ascontiguousarray(w.transpose(2, 1, 0, 3)).reshape(n // P, P, -1)


def by_partition(v):
    v = np.asarray(v)
    return v.reshape(-1, P).T


def constants():
    i = np.arange(P)
    row, col = i[:, None], i[None, :]
    chunk = row // CH == col // CH
    f = np.float32
    squares = np.stack([row == col, np.ones((P, P)), chunk]).astype(f)
    masks = [np.where(chunk & (col >= row), 0, -1e30), np.where(chunk & (col <= row), 0, 1e30)]
    for level in range(LEVELS):
        b = 2 ** level
        m = (row // (2 * b) == col // (2 * b)) & (row // b % 2 == 1) & (col // b % 2 == 0)
        masks += [m, m.T] if level == 0 else [m.T]
    select = np.zeros((P, 10, P), f)
    for kind in range(3):
        for pair in range(2):
            for half in range(2):
                select[32 * kind + place(2 * pair + half), 2 * kind + pair, 64 * half:64 * half + 64] = 1
    for h in range(HEADS):
        select[96 + h, 6 + h, :] = 1
    out = {
        "squares": squares,
        "dn_masks": np.ascontiguousarray(np.stack(masks).astype(f).transpose(1, 0, 2)),
        "selectors": select,
        "restart": (np.arange(S) % CH != 0).astype(f),
    }
    pos = np.arange(S, dtype=f)
    inv = (1.0 / (f(10000.0) ** (np.arange(0, ROPE, 2, dtype=f) / f(ROPE)))).astype(f)
    ang = np.concatenate([inv, inv])[:, None] * pos[None, :]
    sign = np.where(np.arange(ROPE) < ROPE // 2, -1, 1)[:, None]
    rope = np.zeros((P, S), f)
    rope[64:96], rope[96:128] = np.cos(ang), sign * np.sin(ang)
    out["rope"] = rope
    block = row // CH >= col // CH
    out["attention_masks"] = np.ascontiguousarray(
        np.stack([np.where(block, 0, -1e30), np.where(row >= col, 0, -1e30)]).astype(f).transpose(1, 0, 2))
    upper = (chunk & (row <= col)).astype(f)
    kv = np.zeros((P, 256), f)
    for h in range(HEADS):
        kv[32 * h:32 * h + 32, 64 * h:64 * h + 64] = 1
    out["gla_masks"] = np.concatenate([upper, kv], axis=1)
    counts = []
    for w in WINDOWS:
        def n(size):
            p = np.arange(size)
            return np.clip(p + w // 2, 0, size) - np.clip(p - w // 2, 0, size)
        counts.append((n(S // GRID_W)[:, None] * n(GRID_W)[None, :]).reshape(S))
    out["pool_shares"] = (1 / np.stack(counts)).astype(f)
    return out


def lay_out(inputs):
    a = {k: np.asarray(v) for k, v in inputs.items()}
    f = np.float32
    out = constants()
    out["x"] = a["x"][0]
    out["w_in"] = in_units(a["w_in"][0], unit_columns())
    gate = np.stack([in_units(w) for w in a["w_gate"][0]], axis=1)
    up = np.stack([in_units(w) for w in a["w_branch_up"][0]], axis=1)
    out["w_gate"] = np.concatenate([gate, up], axis=3).reshape(32, P, -1)
    out["w_out"] = in_units(a["w_out"][0])
    out["w_mlp_in"] = in_units(a["w_mlp_in"][0])
    out["w_mlp_out"] = np.concatenate([in_units(w) for w in a["w_mlp_out"][0].reshape(4, D, D)])
    slots = a["w_in_2"][0].reshape(D, 11, MIX * P)
    tile = lambda s, m: slots[:, s, m * P:(m + 1) * P]
    order = [(s, m) for s in (0, 1) for m in range(MIX)]
    order += [(s, m) for m in range(MIX) for s in (2, 3, 4, 5)]
    order += [(s, m) for m in range(MIX) for s in (6, 7)]
    order += [(s, m) for s in (8, 9, 10) for m in range(MIX)]
    out["w_in_2"] = in_units(np.concatenate([tile(s, m) for s, m in order], axis=1))
    out["w_out_2"] = np.concatenate([in_units(w) for w in a["w_out_2"][0].reshape(2, D, D)])
    out["c_pw"] = in_units(a["c_pw_2"][0])
    mod = in_units(a["mod_w_2"][0]).reshape(MOD_LOADS, 3, P, D)
    out["mod_w"] = mod.transpose(0, 2, 1, 3).reshape(MOD_LOADS, P, 3 * D)
    out["d_w"] = a["d_w_2"][0].transpose(1, 0, 2)
    out["ctx"] = a["ctx_2"][0]
    lru = np.zeros((2, 2, MIX, P, P), f)
    for kind, name in enumerate(("a_wr_2", "a_wi_2")):
        w = a[name][0].reshape(2, MIX, 2, CH, CH)
        for x in range(2):
            lru[kind, :, :, CH * x:CH * x + CH, CH * x:CH * x + CH] = w[:, :, x]
    out["lru_w"] = lru.transpose(3, 0, 1, 2, 4)
    vectors = np.zeros((P, N_VECTORS), f)

    def put(name, value):
        start, count = VECTORS[name]
        assert value.shape == (P, count), (name, value.shape)
        vectors[:, start:start + count] = value

    for name in ("norm_mix_pre", "norm_mix_post", "norm_mlp_pre", "norm_mlp_post", "mla_q_norm",
                 "mla_kv_norm", "gla_gate_bias", "norm_g_2", "final_g_2", "mod_b_2", "a_br_2",
                 "a_bi_2", "a_lam_2", "c_ln_g_2", "c_ln_b_2", "c_pw_b_2", "d_b_2", "d_scale_2"):
        put(name, by_partition(a[name]))

    def taps(w, tiles):
        return w.reshape(w.shape[0], tiles, P).transpose(2, 1, 0).reshape(P, -1)

    put("dn_conv", taps(a["dn_conv"][0], 6))
    put("b_conv_2", taps(a["b_conv_2"][0], 4))
    put("c_conv_2", taps(a["c_conv_2"][0], 4))
    put("a_conv_2", np.concatenate([taps(a["a_conv_2"][0, d], 4) for d in range(2)], axis=1))
    put("b_gate", a["b_gate"][0].reshape(4, KT, P).transpose(2, 1, 0).reshape(P, 32))
    put("gla_norm", np.concatenate([a["gla_norm"][0]] * 2)[:, None])
    put("dn_norm", np.concatenate([a["dn_norm"][0]] * 2)[:, None])
    c2 = np.stack([a["c_2"][0], a["c_ctx_2"]])
    put("c_2", c2.reshape(2, KT, P).transpose(2, 1, 0).reshape(P, 16))
    for name, src in (("row_bias", "dn_dt_bias"), ("dn_a_log", "dn_a_log")):
        column = np.zeros((P, 1), f)
        column[32:36, 0] = a[src][0][[0, 2, 1, 3]]
        put(name, column)
    column = np.zeros((P, 1), f)
    column[0:128:32, 0] = a["fox_f_bias"][0]
    put("fox_f_bias", column)
    out["vectors"] = vectors
    up = np.zeros((32, P), f)
    up[1:17] = a["gla_w_gate_up"][0]
    out["gla_gate_up"] = up
    head = np.concatenate([np.arange(DH + ROPE), DH + np.roll(np.arange(ROPE), ROPE // 2)])
    cols = np.concatenate([h * (DH + ROPE) + head for h in range(HEADS)])
    out["mla_w_q"] = a["mla_w_q_up"][0][:, cols].reshape(2, P, HEADS * P).transpose(1, 0, 2)
    kv = a["mla_w_kv_up"][0].reshape(P, HEADS, 2, DH).transpose(0, 2, 1, 3)
    out["mla_w_kv"] = kv.reshape(P, 512)
    return {k: np.ascontiguousarray(v) for k, v in out.items()}


def kernel(**inputs):
    import concourse.bacc as bacc
    from concourse.bass_utils import run_bass_kernel_spmd

    arrays = lay_out(inputs)
    nc = bacc.Bacc("TRN2", target_bir_lowering=False, num_devices=1)
    t = {k: nc.dram_tensor(f"in_{k}", v.shape, F32, kind="ExternalInput").ap()
         for k, v in arrays.items()}
    t["out"] = nc.dram_tensor("out_tokens", [S, D], F32, kind="ExternalOutput").ap()
    build(nc, t)
    r = run_bass_kernel_spmd(nc, [{f"in_{k}": v for k, v in arrays.items()}], core_ids=[0])
    return r.results[0]["out_tokens"].reshape(1, S, D)
```
